# Optimizing a Trainium2 kernel written in Bass

```python
import math
import jax, jax.numpy as jnp
from jax import lax
import numpy as np

D_MODEL = 1024
BATCH = 1
SEQ = 512
DEPTH = 1

GRID_W = 64
F32 = jnp.float32
EPS = 1e-6
HY_WIDTH = D_MODEL // 4
NA_HEAD_DIM = 64
NA_WIDTH = D_MODEL // 2
NA_HEADS = NA_WIDTH // NA_HEAD_DIM
POOL_WIDTH = D_MODEL // 4
POOL_WINDOWS = (2, 4, 8, 16)
POOL_GROUPS = len(POOL_WINDOWS)
POOL_GROUP_DIM = POOL_WIDTH // POOL_GROUPS
IN_WIDTH = 3 * HY_WIDTH + 3 * NA_WIDTH + POOL_WIDTH
SHORT_CONV = 3
FILTER_EMB = 33
FILTER_BANDS = (FILTER_EMB - 1) // 2
FILTER_HIDDEN = 64
DECAY_FAST = 0.3
DECAY_SLOW = 1.5
DECAY_TARGET = 1e-2
NA_KH_MAX = 8
NA_KW = 16
N_EXPERTS = 16
EC_CAPACITY = 2
EXPERT_FF = 2 * D_MODEL


def rms_norm(x, g):
    xf = x.astype(F32)
    y = xf * lax.rsqrt(jnp.mean(xf * xf, axis=-1, keepdims=True) + EPS)
    return (y * g.astype(F32)).astype(x.dtype)

def short_conv(u, w, b):
    up = jnp.pad(u, ((0, 0), (1, 1), (0, 0)))
    return up[:, :-2] * w[0] + up[:, 1:-1] * w[1] + up[:, 2:] * w[2] + b

def hyena_filter(L, w1, b1, w2, b2, w_out, freq):
    t = jnp.linspace(0.0, 1.0, L, dtype=F32)[:, None]
    ang = 2.0 * math.pi * jnp.arange(L, dtype=F32)[:, None] / L
    f = jnp.linspace(1e-4, FILTER_BANDS - 1, FILTER_BANDS, dtype=F32)[None, :]
    z = jnp.concatenate([t, jnp.cos(f * ang), -jnp.sin(f * ang)], axis=-1)
    fr = freq.astype(F32)
    h = jnp.sin(fr * (z @ w1.astype(F32) + b1.astype(F32)))
    h = jnp.sin(fr * (h @ w2.astype(F32) + b2.astype(F32)))
    h = h @ w_out.astype(F32)
    deltas = jnp.abs(jnp.linspace(math.log(DECAY_TARGET) / DECAY_FAST,
                                  math.log(DECAY_TARGET) / DECAY_SLOW, HY_WIDTH, dtype=F32))
    decay = jnp.exp(-t * deltas)
    h = h * jnp.concatenate([decay, decay], axis=-1)
    h_fwd, h_bwd = h[:, :HY_WIDTH], h[:, HY_WIDTH:]
    return jnp.concatenate([h_fwd, jnp.zeros((1, HY_WIDTH), F32), h_bwd[1:][::-1]], axis=0)

def hyena_mixer(u, sw, sb, filt, skip):
    u = short_conv(u, sw, sb)
    x0, x1, v = jnp.split(u, 3, axis=-1)
    z = (v * x1).astype(F32)
    L = z.shape[1]
    Z = jnp.fft.rfft(z, n=2 * L, axis=1)
    Hf = jnp.fft.rfft(filt, n=2 * L, axis=0)
    y = jnp.fft.irfft(Z * Hf[None], n=2 * L, axis=1)[:, :L]
    y = y + z * skip.astype(F32)
    return y.astype(u.dtype) * x0

def neighbourhood_attention(q, k, v, rpb):
    B, L, _ = q.shape
    rows = L // GRID_W
    kh = min(NA_KH_MAX, rows)
    shp = (B, rows, GRID_W, NA_HEADS, NA_HEAD_DIM)
    qg = (q * (NA_HEAD_DIM ** -0.5)).reshape(shp).transpose(1, 0, 2, 3, 4)
    kg = k.reshape(shp)
    vg = v.reshape(shp)
    cols = jnp.arange(GRID_W)
    col_start = jnp.clip(cols - NA_KW // 2, 0, GRID_W - NA_KW)
    col_idx = col_start[:, None] + jnp.arange(NA_KW)[None, :]
    dc_idx = col_idx - cols[:, None] + NA_KW - 1

    def one_row(args):
        q_row, r = args
        rs = jnp.clip(r - kh // 2, 0, rows - kh)
        k_nb = lax.dynamic_slice_in_dim(kg, rs, kh, axis=1)[:, :, col_idx]
        v_nb = lax.dynamic_slice_in_dim(vg, rs, kh, axis=1)[:, :, col_idx]
        s = jnp.einsum('bchd,bicjhd->bhcij', q_row, k_nb).astype(F32)
        dr_idx = rs + jnp.arange(kh) - r + NA_KH_MAX - 1
        bias = rpb[:, dr_idx][:, :, dc_idx].transpose(0, 2, 1, 3)
        s = s + bias.astype(F32)[None]
        p = jax.nn.softmax(s.reshape(B, NA_HEADS, GRID_W, kh * NA_KW), axis=-1)
        p = p.reshape(s.shape).astype(v_nb.dtype)
        return jnp.einsum('bhcij,bicjhd->bchd', p, v_nb)

    out = lax.map(one_row, (qg, jnp.arange(rows)))
    return out.transpose(1, 0, 2, 3, 4).reshape(B, L, NA_WIDTH)

def pool_mixer(u, pool_w, pool_scale):
    B, L, _ = u.shape
    ug = u.reshape(B, L, POOL_GROUPS, POOL_GROUP_DIM).astype(F32)
    S = jnp.concatenate([jnp.zeros((B, 1, POOL_GROUPS, POOL_GROUP_DIM), F32),
                         jnp.cumsum(ug, axis=1)], axis=1)
    t = jnp.arange(L)
    means = []
    for g, w in enumerate(POOL_WINDOWS):
        lo = jnp.clip(t - w // 2, 0, L)
        hi = jnp.clip(t + w // 2, 0, L)
        cnt = (hi - lo).astype(F32)[None, :, None]
        means.append((S[:, hi, g] - S[:, lo, g]) / cnt)
    pooled = jnp.stack(means, axis=2) - ug
    y = jnp.einsum('blgc,gcd->blgd', pooled, pool_w.astype(F32)).reshape(B, L, POOL_WIDTH)
    return (y * pool_scale.astype(F32)).astype(u.dtype)

def expert_choice_moe(h, w_router, w_gate, w_up, w_down):
    B, L, D = h.shape
    cap = EC_CAPACITY * L // N_EXPERTS
    aff = jax.nn.softmax(h.astype(F32) @ w_router.astype(F32), axis=-1)
    gate, idx = lax.top_k(aff.transpose(0, 2, 1), cap)
    xs = jax.vmap(lambda hb, ib: hb[ib])(h, idx)
    a = jnp.einsum('becd,edf->becf', xs, w_gate)
    b = jnp.einsum('becd,edf->becf', xs, w_up)
    y = jnp.einsum('becf,efd->becd', jax.nn.silu(a) * b, w_down)
    y = y * gate.astype(y.dtype)[..., None]
    return jax.vmap(lambda yb, ib: jnp.zeros((L, D), yb.dtype).at[ib.reshape(-1)].add(
        yb.reshape(-1, D)))(y, idx)

def first_inputs(seed: int = 0) -> dict:
    key = jax.random.key(seed)
    ks = jax.random.split(key, 24)
    n = lambda k, s, sc: jax.random.normal(k, s, F32) * sc
    gain = lambda k, s: 1.0 + 0.02 * jax.random.normal(k, s, F32)
    L_ = DEPTH
    return {
        'x': jax.random.normal(ks[0], (BATCH, SEQ, D_MODEL), F32),
        'norm1_g': gain(ks[1], (L_, D_MODEL)),
        'w_in': n(ks[2], (L_, D_MODEL, IN_WIDTH), D_MODEL ** -0.5),
        'hy_short_w': n(ks[3], (L_, SHORT_CONV, 3 * HY_WIDTH), SHORT_CONV ** -0.5),
        'hy_short_b': n(ks[4], (L_, 3 * HY_WIDTH), 0.02),
        'hy_f_w1': n(ks[5], (L_, FILTER_EMB, FILTER_HIDDEN), FILTER_EMB ** -0.5),
        'hy_f_b1': n(ks[6], (L_, FILTER_HIDDEN), 0.02),
        'hy_f_w2': n(ks[7], (L_, FILTER_HIDDEN, FILTER_HIDDEN), FILTER_HIDDEN ** -0.5),
        'hy_f_b2': n(ks[8], (L_, FILTER_HIDDEN), 0.02),
        'hy_f_wout': n(ks[9], (L_, FILTER_HIDDEN, 2 * HY_WIDTH), FILTER_HIDDEN ** -0.5),
        'hy_f_freq': gain(ks[10], (L_, FILTER_HIDDEN)),
        'hy_skip': n(ks[11], (L_, HY_WIDTH), 1.0),
        'na_rpb': n(ks[12], (L_, NA_HEADS, 2 * NA_KH_MAX - 1, 2 * NA_KW - 1), 0.02),
        'pool_w': n(ks[13], (L_, POOL_GROUPS, POOL_GROUP_DIM, POOL_GROUP_DIM), POOL_GROUP_DIM ** -0.5),
        'pool_scale': 1.0 + 0.1 * jax.random.normal(ks[14], (L_, POOL_WIDTH), F32),
        'mix_norm_g': gain(ks[15], (L_, D_MODEL)),
        'w_out': n(ks[16], (L_, D_MODEL, D_MODEL), D_MODEL ** -0.5),
        'norm2_g': gain(ks[17], (L_, D_MODEL)),
        'w_router': n(ks[18], (L_, D_MODEL, N_EXPERTS), D_MODEL ** -0.5),
        'w_gate': n(ks[19], (L_, N_EXPERTS, D_MODEL, EXPERT_FF), D_MODEL ** -0.5),
        'w_up': n(ks[20], (L_, N_EXPERTS, D_MODEL, EXPERT_FF), D_MODEL ** -0.5),
        'w_down': n(ks[21], (L_, N_EXPERTS, EXPERT_FF, D_MODEL), EXPERT_FF ** -0.5),
        'final_g': gain(ks[22], (D_MODEL,)),
    }

def first_block(x, norm1_g, w_in, hy_short_w, hy_short_b, hy_f_w1, hy_f_b1, hy_f_w2, hy_f_b2,
              hy_f_wout, hy_f_freq, hy_skip, na_rpb, pool_w, pool_scale, mix_norm_g, w_out,
              norm2_g, w_router, w_gate, w_up, w_down, final_g):
    L = x.shape[1]
    cuts = [3 * HY_WIDTH, 3 * HY_WIDTH + NA_WIDTH, 3 * HY_WIDTH + 2 * NA_WIDTH,
            3 * HY_WIDTH + 3 * NA_WIDTH]
    for i in range(DEPTH):
        h = rms_norm(x, norm1_g[i])
        proj = h @ w_in[i]
        hy_in, q, k, v, pool_in = jnp.split(proj, cuts, axis=-1)
        filt = hyena_filter(L, hy_f_w1[i], hy_f_b1[i], hy_f_w2[i], hy_f_b2[i],
                            hy_f_wout[i], hy_f_freq[i])
        y_hy = hyena_mixer(hy_in, hy_short_w[i], hy_short_b[i], filt, hy_skip[i])
        y_na = neighbourhood_attention(q, k, v, na_rpb[i])
        y_pool = pool_mixer(pool_in, pool_w[i], pool_scale[i])
        g = mix_norm_g[i]
        mixed = jnp.concatenate([
            rms_norm(y_hy, g[:HY_WIDTH]),
            rms_norm(y_na, g[HY_WIDTH:HY_WIDTH + NA_WIDTH]),
            rms_norm(y_pool, g[HY_WIDTH + NA_WIDTH:])], axis=-1)
        x = x + mixed @ w_out[i]
        x = x + expert_choice_moe(rms_norm(x, norm2_g[i]), w_router[i], w_gate[i],
                                  w_up[i], w_down[i])
    return rms_norm(x, final_g)


PLE_DIM = 256
GDN_HEADS = 4
GDN_DK = 128
GDN_DV = 128
CONV_WIDTH = 4
MLSTM_HEADS = 4
MLSTM_DQK = 64
MLSTM_DV = 128
CHUNK = 64
D_FF = -(-(8 * D_MODEL) // (3 * 256)) * 256
GDN_QK = GDN_HEADS * GDN_DK
GDN_V = GDN_HEADS * GDN_DV
ML_QK = MLSTM_HEADS * MLSTM_DQK
ML_V = MLSTM_HEADS * MLSTM_DV
IN_SIZES = (GDN_QK, GDN_QK, GDN_V, GDN_V, GDN_HEADS, GDN_HEADS,
            ML_QK, ML_QK, ML_V, ML_V, MLSTM_HEADS, MLSTM_HEADS,
            D_MODEL, D_MODEL)
IN_WIDTH_2 = 2 * GDN_QK + 2 * GDN_V + 2 * GDN_HEADS + 2 * ML_QK + 2 * ML_V + 2 * MLSTM_HEADS + 2 * D_MODEL
CONV_CH = 2 * GDN_QK + GDN_V
NORM_EPS = 1e-6


def _rmsnorm(x, gain):
    xf = x.astype(jnp.float32)
    y = xf * lax.rsqrt(jnp.mean(xf * xf, axis=-1, keepdims=True) + NORM_EPS)
    return (y * gain.astype(jnp.float32)).astype(x.dtype)

def _l2norm(x):
    return x * lax.rsqrt(jnp.sum(x * x, axis=-1, keepdims=True) + NORM_EPS)

def _causal_conv(x, w):
    c = x.shape[-1]
    return lax.conv_general_dilated(x, w[:, None, :].astype(x.dtype), window_strides=(1,),
                                    padding=[(CONV_WIDTH - 1, 0)],
                                    dimension_numbers=('NWC', 'WIO', 'NWC'),
                                    feature_group_count=c)

def _chunk_seq(t):
    b, s, h, d = t.shape
    return t.reshape(b, s // CHUNK, CHUNK, h, d).transpose(1, 0, 3, 2, 4)

def _chunk_gate(t):
    b, s, h = t.shape
    return t.reshape(b, s // CHUNK, CHUNK, h).transpose(1, 0, 3, 2)

def _unchunk(t):
    n, b, h, c, d = t.shape
    return t.transpose(1, 0, 3, 2, 4).reshape(b, n * c, h, d)

def gated_delta_rule(q, k, v, g, beta):
    dk = q.shape[-1]
    dv = v.shape[-1]
    q = _l2norm(q) * (dk ** -0.5)
    k = _l2norm(k)
    qc, kc, vc = _chunk_seq(q), _chunk_seq(k), _chunk_seq(v)
    gc = jnp.cumsum(_chunk_gate(g), axis=-1)
    bc = _chunk_gate(beta)
    incl = jnp.tril(jnp.ones((CHUNK, CHUNK), dtype=bool))
    strict = jnp.tril(jnp.ones((CHUNK, CHUNK), dtype=bool), -1)
    decay = jnp.exp(jnp.where(incl, gc[..., :, None] - gc[..., None, :], -jnp.inf))
    k_beta = kc * bc[..., None]
    m = jnp.where(strict, jnp.einsum('nbhcd,nbhsd->nbhcs', k_beta, kc) * decay, 0.0)
    a = m + jnp.eye(CHUNK, dtype=m.dtype)
    rhs = jnp.concatenate([vc * bc[..., None], k_beta * jnp.exp(gc)[..., None]], axis=-1)
    sol = lax.linalg.triangular_solve(a, rhs, left_side=True, lower=True, unit_diagonal=True)
    u, w = sol[..., :dv], sol[..., dv:]
    attn = jnp.einsum('nbhcd,nbhsd->nbhcs', qc, kc) * decay
    g_last = gc[..., -1]

    def step(state, inp):
        q_i, k_i, u_i, w_i, g_i, gl_i, attn_i = inp
        v_new = u_i - jnp.einsum('bhcd,bhde->bhce', w_i, state)
        o = (jnp.einsum('bhcd,bhde->bhce', q_i * jnp.exp(g_i)[..., None], state)
             + jnp.einsum('bhcs,bhse->bhce', attn_i, v_new))
        k_dec = k_i * jnp.exp(gl_i[..., None] - g_i)[..., None]
        state = state * jnp.exp(gl_i)[..., None, None] + jnp.einsum('bhcd,bhce->bhde', k_dec, v_new)
        return state, o

    init = jnp.zeros(qc.shape[1:3] + (dk, dv), jnp.float32)
    _, out = lax.scan(step, init, (qc, kc, u, w, gc, g_last, attn))
    return _unchunk(out)

def mlstm_chunkwise(q, k, v, i_pre, f_pre):
    dqk = q.shape[-1]
    qc = _chunk_seq(q * (dqk ** -0.5))
    kc, vc = _chunk_seq(k), _chunk_seq(v)
    ic = _chunk_gate(i_pre)
    bc = jnp.cumsum(_chunk_gate(jax.nn.log_sigmoid(f_pre)), axis=-1)
    incl = jnp.tril(jnp.ones((CHUNK, CHUNK), dtype=bool))

    def step(carry, inp):
        c_bar, n_bar, m = carry
        q_i, k_i, v_i, i_i, b_i = inp
        d_log = jnp.where(incl, b_i[..., :, None] - b_i[..., None, :] + i_i[..., None, :], -jnp.inf)
        m_inter = b_i + m[..., None]
        m_t = jnp.maximum(m_inter, jnp.max(d_log, axis=-1))
        w_inter = jnp.exp(m_inter - m_t)
        s = jnp.einsum('bhcd,bhsd->bhcs', q_i, k_i) * jnp.exp(d_log - m_t[..., None])
        num = (w_inter[..., None] * jnp.einsum('bhcd,bhde->bhce', q_i, c_bar)
               + jnp.einsum('bhcs,bhse->bhce', s, v_i))
        den = w_inter * jnp.einsum('bhcd,bhd->bhc', q_i, n_bar) + jnp.sum(s, axis=-1)
        h = num / jnp.maximum(jnp.abs(den), jnp.exp(-m_t))[..., None]
        b_last = b_i[..., -1]
        a_i = b_last[..., None] - b_i + i_i
        m_new = jnp.maximum(b_last + m, jnp.max(a_i, axis=-1))
        scale_prev = jnp.exp(b_last + m - m_new)
        k_w = k_i * jnp.exp(a_i - m_new[..., None])[..., None]
        c_bar = scale_prev[..., None, None] * c_bar + jnp.einsum('bhcd,bhce->bhde', k_w, v_i)
        n_bar = scale_prev[..., None] * n_bar + jnp.sum(k_w, axis=-2)
        return (c_bar, n_bar, m_new), h

    nb, bb, hh = qc.shape[0], qc.shape[1], qc.shape[2]
    init = (jnp.zeros((bb, hh, dqk, vc.shape[-1]), jnp.float32),
            jnp.zeros((bb, hh, dqk), jnp.float32),
            jnp.zeros((bb, hh), jnp.float32))
    _, out = lax.scan(step, init, (qc, kc, vc, ic, bc))
    return _unchunk(out)

def _head_rmsnorm(x, gain):
    return x * lax.rsqrt(jnp.mean(x * x, axis=-1, keepdims=True) + NORM_EPS) * gain.astype(jnp.float32)

def _layer(x, p_i, g_mix, w_in, conv_w, a_log, dt_bias, gdn_norm, ml_i_bias, ml_f_bias, ml_norm,
           w_branch_a, w_branch_b, w_out, g_ffn, w1, w3, w2, g_ple, w_ple_gate, w_ple):
    bsz, seq, _ = x.shape
    dt = x.dtype
    h = _rmsnorm(x, g_mix)
    proj = h @ w_in
    idx = [int(v) for v in np.cumsum(IN_SIZES)[:-1]]
    (gq, gk, gv, gz, gbeta, galpha, mq, mk, mv, mo, mi, mf, gate_a, gate_b) = jnp.split(proj, idx, axis=-1)

    qkv = jax.nn.silu(_causal_conv(jnp.concatenate([gq, gk, gv], axis=-1), conv_w))
    gq, gk, gv = jnp.split(qkv.astype(jnp.float32), [GDN_QK, 2 * GDN_QK], axis=-1)
    beta = jax.nn.sigmoid(gbeta.astype(jnp.float32))
    g = -jnp.exp(a_log.astype(jnp.float32)) * jax.nn.softplus(galpha.astype(jnp.float32) + dt_bias.astype(jnp.float32))
    o_a = gated_delta_rule(gq.reshape(bsz, seq, GDN_HEADS, GDN_DK),
                           gk.reshape(bsz, seq, GDN_HEADS, GDN_DK),
                           gv.reshape(bsz, seq, GDN_HEADS, GDN_DV), g, beta)
    o_a = _head_rmsnorm(o_a, gdn_norm) * jax.nn.silu(gz.astype(jnp.float32)).reshape(bsz, seq, GDN_HEADS, GDN_DV)
    y_a = o_a.reshape(bsz, seq, GDN_V).astype(dt) @ w_branch_a

    o_b = mlstm_chunkwise(mq.astype(jnp.float32).reshape(bsz, seq, MLSTM_HEADS, MLSTM_DQK),
                          mk.astype(jnp.float32).reshape(bsz, seq, MLSTM_HEADS, MLSTM_DQK),
                          mv.astype(jnp.float32).reshape(bsz, seq, MLSTM_HEADS, MLSTM_DV),
                          mi.astype(jnp.float32) + ml_i_bias.astype(jnp.float32),
                          mf.astype(jnp.float32) + ml_f_bias.astype(jnp.float32))
    o_b = _head_rmsnorm(o_b, ml_norm) * jax.nn.sigmoid(mo.astype(jnp.float32)).reshape(bsz, seq, MLSTM_HEADS, MLSTM_DV)
    y_b = o_b.reshape(bsz, seq, ML_V).astype(dt) @ w_branch_b

    mixed = jax.nn.sigmoid(gate_a) * y_a + jax.nn.sigmoid(gate_b) * y_b
    x = x + mixed @ w_out

    h = _rmsnorm(x, g_ffn)
    x = x + (jax.nn.silu(h @ w1) * (h @ w3)) @ w2

    gate = jax.nn.sigmoid(_rmsnorm(x, g_ple) @ w_ple_gate)
    x = x + gate * (p_i @ w_ple)
    return x

def second_inputs(seed: int = 0) -> dict:
    key = jax.random.key(seed)
    ks = jax.random.split(key, 24)
    f32 = jnp.float32
    L, D = DEPTH, D_MODEL

    def nrm(k, shape, scale):
        return jax.random.normal(k, shape, f32) * scale

    def gain(k, shape):
        return 1.0 + 0.05 * jax.random.normal(k, shape, f32)

    dt0 = jnp.exp(jax.random.uniform(ks[5], (L, GDN_HEADS), f32, np.log(1e-3), np.log(1e-1)))
    return {
        'x': jax.random.normal(ks[0], (BATCH, SEQ, D), f32),
        'p': jax.random.normal(ks[1], (DEPTH, BATCH, SEQ, PLE_DIM), f32),
        'g_mix': gain(ks[2], (L, D)),
        'w_in': nrm(ks[3], (L, D, IN_WIDTH_2), D ** -0.5),
        'conv_w': nrm(ks[4], (L, CONV_WIDTH, CONV_CH), CONV_WIDTH ** -0.5),
        'a_log': jnp.log(jax.random.uniform(ks[6], (L, GDN_HEADS), f32, 1.0, 16.0)),
        'dt_bias': dt0 + jnp.log(-jnp.expm1(-dt0)),
        'gdn_norm': gain(ks[7], (L, GDN_DV)),
        'ml_i_bias': nrm(ks[8], (L, MLSTM_HEADS), 0.1),
        'ml_f_bias': jnp.linspace(3.0, 6.0, MLSTM_HEADS, dtype=f32)[None, :] + nrm(ks[9], (L, MLSTM_HEADS), 0.1),
        'ml_norm': gain(ks[10], (L, MLSTM_HEADS, MLSTM_DV)),
        'w_branch_a': nrm(ks[11], (L, GDN_V, D), GDN_V ** -0.5),
        'w_branch_b': nrm(ks[12], (L, ML_V, D), ML_V ** -0.5),
        'w_out': nrm(ks[13], (L, D, D), D ** -0.5),
        'g_ffn': gain(ks[14], (L, D)),
        'w1': nrm(ks[15], (L, D, D_FF), D ** -0.5),
        'w3': nrm(ks[16], (L, D, D_FF), D ** -0.5),
        'w2': nrm(ks[17], (L, D_FF, D), D_FF ** -0.5),
        'g_ple': gain(ks[18], (L, D)),
        'w_ple_gate': nrm(ks[19], (L, D, D), D ** -0.5),
        'w_ple': nrm(ks[20], (L, PLE_DIM, D), PLE_DIM ** -0.5),
        'g_final': gain(ks[21], (D,)),
    }

def second_block(x, p, g_mix, w_in, conv_w, a_log, dt_bias, gdn_norm, ml_i_bias, ml_f_bias, ml_norm,
              w_branch_a, w_branch_b, w_out, g_ffn, w1, w3, w2, g_ple, w_ple_gate, w_ple, g_final):
    for i in range(DEPTH):
        x = _layer(x, p[i], g_mix[i], w_in[i], conv_w[i], a_log[i], dt_bias[i], gdn_norm[i],
                   ml_i_bias[i], ml_f_bias[i], ml_norm[i], w_branch_a[i], w_branch_b[i], w_out[i],
                   g_ffn[i], w1[i], w3[i], w2[i], g_ple[i], w_ple_gate[i], w_ple[i])
    return _rmsnorm(x, g_final)


def setup_inputs(seed=0):
    out = dict(first_inputs(seed))
    for name, value in second_inputs(seed + 1).items():
        if name != "x":
            out[name + "_2"] = value
    return out


def reference(
    x, norm1_g, w_in, hy_short_w, hy_short_b, hy_f_w1, hy_f_b1, hy_f_w2, hy_f_b2, hy_f_wout,
    hy_f_freq, hy_skip, na_rpb, pool_w, pool_scale, mix_norm_g, w_out, norm2_g, w_router,
    w_gate, w_up, w_down, final_g, p_2, g_mix_2, w_in_2, conv_w_2, a_log_2, dt_bias_2,
    gdn_norm_2, ml_i_bias_2, ml_f_bias_2, ml_norm_2, w_branch_a_2, w_branch_b_2, w_out_2,
    g_ffn_2, w1_2, w3_2, w2_2, g_ple_2, w_ple_gate_2, w_ple_2, g_final_2,
):
    x = first_block(
        x, norm1_g, w_in, hy_short_w, hy_short_b, hy_f_w1, hy_f_b1, hy_f_w2, hy_f_b2, hy_f_wout,
        hy_f_freq, hy_skip, na_rpb, pool_w, pool_scale, mix_norm_g, w_out, norm2_g, w_router,
        w_gate, w_up, w_down, final_g,
    )
    return second_block(
        x, p_2, g_mix_2, w_in_2, conv_w_2, a_log_2, dt_bias_2, gdn_norm_2, ml_i_bias_2,
        ml_f_bias_2, ml_norm_2, w_branch_a_2, w_branch_b_2, w_out_2, g_ffn_2, w1_2, w3_2, w2_2,
        g_ple_2, w_ple_gate_2, w_ple_2, g_final_2,
    )


_drawn_inputs = setup_inputs


def setup_inputs(seed=0):
    import zlib

    import numpy as np

    out = dict(_drawn_inputs(seed))
    spreads = {}
    factors = {'hy_short_b': 2.855,
     'hy_f_b1': 2.999,
     'hy_f_b2': 3.029,
     'hy_f_freq': 4.141,
     'na_rpb': 3.772,
     'mix_norm_g': 2.669,
     'norm2_g': 4.101,
     'gdn_norm_2': 4.219,
     'ml_i_bias_2': 200.0,
     'ml_norm_2': 3.859,
     'g_ple_2': 136.068,
     'g_ffn_2': 2.78}
    for name, (base, spread) in spreads.items():
        noise = np.random.default_rng([zlib.crc32(name.encode()), seed]).standard_normal(out[name].shape)
        drawn = base * np.exp(spread * noise) if base else spread * noise
        out[name] = __import__('jax').numpy.asarray(drawn.astype(out[name].dtype))
    for name, factor in factors.items():
        out[name] = (out[name] * factor).astype(out[name].dtype)
    return out
```

```python
from contextlib import ExitStack

import numpy as np

import concourse.bass as bass
from concourse import mybir

F32 = mybir.dt.float32
ACT = mybir.ActivationFunctionType
ALU = mybir.AluOpType
AX = mybir.AxisListType

P = 128
D = 1024
L = 512
NT = L // P
KD = D // P
EPS = 1e-6
HY, NAW, PW = D // 4, D // 2, D // 4
NH, HD = 8, 64
GW = 64
ROWS = L // GW
KWIN = 16
QC = P // ROWS
KC = 32
NKEY = KC * ROWS
KSTART = [0, 8, 24, 32]
KIND = [0, 1, 1, 2]
KOFF = [0, -8, -16]
TABW = 48
NE, CAP, FF = 16, 64, 2048
FC = 512
NFC = FF // FC
GH, DK = 4, 128
MH, MQ, MV = 4, 64, 128
DFF = 2816
NFT = DFF // P
PLE = 256
MAGIC = 12582912.0
TWO_PI_HI = 6.28125
TWO_PI_LO = 0.0019353071795864769
PI = 3.1415925
R = 4
WCH = 2048
MSLOT = 4096

N_IN1, N_OUT1 = 10, 4
N_QKV, N_MQK, N_TOK = 6, 2, 6
N_BR = 12
N_OUT2, N_UP, N_DOWN, N_PLE, N_PG = 4, NFT, 12, 1, 4
C_OUT1 = N_IN1
C_QKV = C_OUT1 + N_OUT1
C_TOK = C_QKV + N_QKV + N_MQK
C_BR = C_TOK + N_TOK
C_OUT2 = C_BR + N_BR
C_UP = C_OUT2 + N_OUT2
C_DOWN = C_UP + N_UP
C_PLE = C_DOWN + N_DOWN
C_PG = C_PLE + N_PLE
N_CHUNKS = C_PG + N_PG

COLS = {}


def lay_columns():
    at = 0
    for name, n in (("norm1", 8), ("hw0", 6), ("hw1", 6), ("hw2", 6), ("hb", 6), ("skip", 2),
        ("pscale", 2), ("mixg", 8), ("gmix2", 8), ("cw0", 12), ("cw1", 12),
                    ("cw2", 12), ("cw3", 12), ("gffn", 8), ("gple", 8), ("fb1", 1), ("fb2", 1),
                    ("freq", 1), ("wk", 4), ("negt", 4), ("alt2", 1)):
        COLS[name] = at
        at += n
    return at


N_COLS = lay_columns()
ROW = {"gdn": (0, 128), "mln": (128, 512), "alog": (640, 4), "dtb": (644, 4), "ib": (648, 4), "fb": (652, 4)}
N_ROW = 656


SHARED = {
    "dve_variances": (("var1_made", 1), ("hvar_made", 2), ("nvar_made", 1), ("n2var_made", 1),
        ("ovar_made", 2)),
    "act_roots": (("sd1_made", 1), ("hsd_made", 2), ("nsd_made", 1), ("n2sd_made", 1), ("osd_made", 2)),
    "act_squares": (("psq_made", 2), ("nsq_made", 4), ("n2sq_made", 4), ("osq_made", 2)),
    "dve_squares": (("sq1_made", 8), ("hsq_made", 2)),
    "act_steps": (("decay_made", 4), ("fh_made", 2), ("z_copied", 4), ("rs_made", 8), ("pmix_copied", 2),
        ("ot_copied", 4), ("lg_exp", 1), ("beta_made", 1), ("glog_made", 1), ("eg_made", 1),
        ("em_made", 1)),
    "pe_steps": (("net1_filled", 1), ("net2_filled", 1), ("filt_filled", 4), ("z_turned", 4),
        ("four_filled", 4), ("pmix_filled", 2), ("yhy_filled", 2), ("hsum_filled", 2), ("ot_filled", 4),
        ("h2_turned", 8), ("lg_filled", 1), ("aff_turned", 1), ("rank_turned", 1), ("gates_filled", 1),
        ("gc_filled", 1), ("rows_filled", 1), ("mcol_filled", 1)),
    "dve_steps": (("z_made", 2), ("filt_made", 4), ("pq_made", 2), ("lg_made", 1), ("aff_made", 1),
        ("rank_made", 1), ("gabs_made", 1), ("mrow_made", 1)),
}
SHARED_AT = {}
for _sem, _signals in SHARED.items():
    _base = 0
    for _name, _count in _signals:
        SHARED_AT[_name] = (_sem, _base)
        _base += _count


def program(nc, A, out):
    ctx = ExitStack()
    with ctx:
        arena = ctx.enter_context(nc.sbuf_tensor("arena", [P, 53200], F32))
        bank = [ctx.enter_context(nc.psum_tensor(f"bank{i}", [P, 512], F32)) for i in range(8)]
        named = {}

        def S(name):
            sem = SHARED_AT[name][0] if name in SHARED_AT else name
            if sem not in named:
                named[sem] = ctx.enter_context(nc.semaphore(sem))
            return named[sem]

        def nth(name, n):
            return SHARED_AT[name][1] + n

        def view(start, *dims):
            n = int(np.prod(dims))
            v = arena[:, start:start + n]
            if len(dims) == 2:
                v = v.rearrange("p (a b) -> p a b", b=dims[1])
            elif len(dims) == 3:
                v = v.rearrange("p (a b c) -> p a b c", b=dims[1], c=dims[2])
            return v

        x_res = view(0, NT, D)
        hT = view(4096, KD, L)
        ident = view(8192, P)
        ones = view(8320, P)
        utri = view(8448, P)
        strict = view(8576, P)
        cols = view(8704, 192)
        rows = view(8896, N_ROW)
        grow = view(9600, D)
        stat = view(10624, 400)
        wring = [view(11024 + WCH * s, WCH) for s in range(R)]
        B = 11024 + WCH * R

        def col(name, i=0, p0=0, p1=P):
            c = COLS[name] + i
            return cols[p0:p1, c:c + 1]

        def row(name):
            a, n = ROW[name]
            return rows[:, a:a + n]

        def slot(c):
            return wring[c % R]

        hyu = view(B, 6, L)
        hz = view(B + 2 * L, 2, L)
        zqp = view(B + 3072, NT, 768)
        rs = view(B + 6144, 512)
        filt = view(B + 6656, NT, 512)
        ywf = view(B + 6656, NT, 512)
        hyt = view(B + 8704, 2, 512)
        pr = [view(B + 8704 + 256 * i, 256) for i in range(4)]
        cosm = view(B + 9728, NT, 512)
        sinm = view(B + 11776, NT, 512)
        table = view(B + 9728, NH * ROWS, TABW)
        pos = view(B + 13824, 512)
        fw1 = view(B + 14336, P)
        fw2 = view(B + 14464, P)
        fwo = view(B + 14592, 512)
        fa = view(B + 15104, 512)
        fk = view(B + 15616, 512)
        fh = view(B + 16128, 512)
        decay = view(B + 16640, NT, 256)
        PADW = 544
        pu = view(B + 13824, 2, PADW)
        p2 = view(B + 13824 + 1088, PADW)
        p4 = view(B + 13824 + 1632, PADW)
        p8 = view(B + 13824 + 2176, PADW)
        pooled = view(B + 13824 + 2720, 2, L)
        pwbd = view(B + 17664, 2, P)
        qz = view(B + 17920, NH, L)
        kT = view(B + 22016, 4, L)
        va = view(B + 24064, NT, NAW)
        vb_ = view(B + 26112, 3, NAW)
        bias = view(B + 27648, 3, NH * NKEY)
        sc = [view(B + 3072 + 512 * i, 512) for i in range(2)]
        pt = [view(B + 4096 + 512 * i, 512) for i in range(2)]
        ona = view(B + 9728, NT, NAW)
        mixT = hT
        hperm = view(0, NT, KD * P)
        invc = view(9600, 2, L)

        mslot = [view(11024 + MSLOT * s, MSLOT) for s in range(6)]
        M0 = 11024 + 6 * MSLOT
        h2 = view(M0, NT, D)
        onehot = view(M0 + 4096, NT, NE * CAP)
        xsT = view(M0 + 8192, KD, CAP)
        pg = view(M0 + 8704, NT, P)
        gt = view(M0 + 9216, L)
        silu = [view(M0 + 9728 + 256 * i, 256) for i in range(2)]
        hid = [view(M0 + 10240 + 256 * i, 256) for i in range(2)]
        hidT = [view(M0 + 10752 + 256 * i, 256) for i in range(2)]
        ysb = view(M0 + 11264, 1024)
        wr = view(M0 + 12288, KD, NE)
        aff = view(M0 + 12416, NT, NE)
        work = view(M0 + 12480, L)
        rank = view(M0 + 12992, L)
        sel = view(M0 + 13504, L)
        rankc = view(M0 + 14016, NT, NE)
        iota = view(M0 + 14080, CAP)
        lg = view(M0 + 14144, NT, NE)
        sqd = view(M0 + 14208, D)

        hn = view(B, NT, D)
        oa = view(B, NT, 512)
        ob = view(B + 2048, NT, 512)
        qkv = view(B + 4096, 12, L)
        gz = view(B + 10240, NT, 512)
        mo = view(B + 12288, NT, 512)
        mqz = view(B + 14336, MH, L)
        mk = view(B + 16384, 2, L)
        mv = view(B + 17408, NT, MH * 129)
        GS = B + 19472
        wg = view(GS, KD, 16)
        gate = view(GS + 128, NT, 16)
        gx = view(GS + 192, NT, 8)
        gl_ = view(GS + 224, NT, 8)
        beta = view(GS + 256, NT, 4)
        gg = view(GS + 272, NT, 4)
        lf = view(GS + 288, NT, 4)
        ip = view(GS + 304, NT, 4)
        gc = view(GS + 320, NT, 4)
        eg = view(GS + 336, NT, 4)
        ebg = view(GS + 352, NT, 4)
        edec = view(GS + 368, NT, 4)
        ea = view(GS + 384, 4)
        acol = view(GS + 388, NT, 4)
        emcol = view(GS + 404, NT, 4)
        gsm = view(GS + 420, 64)
        T0 = B + 20480

        def tmp(i, n=1):
            return view(T0 + 512 * i, 512 * n)

        class Own:

            def __init__(self, eng, name):
                self.eng, self.name, self.n = eng, name, 0

            def __call__(self, ins):
                ins.then_inc(S(self.name), 1)
                self.n += 1
                return self.n

            def wait(self, n=None):
                self.eng.wait_ge(S(self.name), self.n if n is None else n)

        block = ctx.enter_context(nc.Block())

        used = {}
        for c in range(8):
            used[c] = ("proj_filled", 2 * (c + 1))
        used[8] = used[9] = ("proj_filled", 20)
        for i in range(4):
            used[C_OUT1 + i] = ("out1_filled", 4 * (i + 1))
        for i in range(8):
            used[C_QKV + i] = ("qkv_filled", 2 * (i + 1))
        for i in range(3):
            used[C_TOK + 2 * i] = used[C_TOK + 2 * i + 1] = ("tok_filled", 4 * (i + 1))
        for g in range(4):
            used[C_BR + 3 * g] = ("br_filled", 8 * g + 7)
            used[C_BR + 3 * g + 1] = ("br_filled", 8 * g + 4)
            used[C_BR + 3 * g + 2] = ("br_filled", 8 * g + 8)
        for i in range(4):
            used[C_OUT2 + i] = ("out2_filled", 4 * (i + 1))
        for i in range(N_UP // 2):
            used[C_UP + 2 * i] = used[C_UP + 2 * i + 1] = ("up_filled", 4 * (i + 1))
        for i in range(12):
            used[C_DOWN + i] = ("down_chunk", i + 1)
        used[C_PLE] = ("ple_filled", 8)
        for i in range(4):
            used[C_PG + i] = ("pg_filled", 4 * (i + 1))

        def wait_chunk(pe, c):
            pe.wait_ge(S(f"chunk_in{c % R}"), 16 * (c // R + 1))


        junk = view(T0 + 12288, D)
        blk = grow[:, 0:7 * P].rearrange("p (l c) -> p l c", c=P)
        maT = view(T0, 4, 512)
        atT = view(T0 + 2048, 4, 512)
        kbg = view(T0 + 4096, 4, 512)
        kdc = view(T0 + 6144, 4, 512)
        vbt = view(T0 + 8192, 4, 512)
        egb = tmp(20)
        dec = tmp(21)
        dms = tmp(22)
        moff = [tmp(20), tmp(21)]
        xw = [tmp(22), tmp(23)]
        tin = view(B, 4, 512)
        tit = view(B + 2048, 4, 512)
        wneg = view(B + 8192, 4, 512)
        vnew = [tmp(20), tmp(21)]
        state = tmp(22)
        egl = gsm[:, 0:16]
        brow, arow, mrow, mxrow = (view(T0 + 512 * i, L) for i in range(4))
        expo = view(T0 + 2048, 1280)
        den = gsm[:, 16:32]
        oTa = view(B + 4096, 4, L)
        oTb = view(B + 6144, 4, L)
        mixed = view(B + 8192, KD, L)
        actT = view(B + 4096, NFT, L)
        pT = view(B + 15360, 2, L)
        pw = view(B + 4096, NT, D)
        NF, N3, N4, N5, NO = range(5)
        nstat = [stat[:, 256 + 4 * i:260 + 4 * i] for i in range(5)]
        hstat = stat[:, 280:312]

        def norm_squares(act, norm, ready, step):
            for i in range(NT):
                act.wait_ge(S(ready), step(i))
                if NT * norm + i:
                    act.wait_ge(S("norm_sq"), NT * norm + i)
                act.activation(junk, x_res[:, i, :], ACT.Square, accum_out=nstat[norm][:, i:i + 1])\
                    .then_inc(S("norm_sq"), 1)
            act.wait_ge(S("norm_var"), norm + 1)
            act.activation(nstat[norm], nstat[norm], ACT.Sqrt).then_inc(S("norm_sd"), 1)

        def norm_rstd(dve, own, norm):
            dve.wait_ge(S("norm_sq"), NT * norm + NT)
            dve.tensor_scalar(nstat[norm], nstat[norm], 1.0 / D, EPS, ALU.mult, ALU.add).then_inc(S("norm_var"), 1)
            dve.wait_ge(S("norm_sd"), norm + 1)
            own(dve.reciprocal(nstat[norm], nstat[norm]))
            own.wait()

        def norm_turn_pe(pe, turn, norm):
            half = KD // 2 * (norm - N3)
            pe.wait_ge(S("norm_scaled"), NT * (norm - N3) + NT)
            for k in range(KD):
                if k >= 2:
                    pe.wait_ge(S("norm_ta" if k % 2 == 0 else "norm_tv"), half + k // 2)
                for i in range(NT):
                    last = turn(bank[6 + k % 2][:, P * i:P * i + P], hn[:, i, P * k:P * k + P], ident)
                last.then_inc(S("norm_turned"), 1)
            pe.wait_ge(S("norm_ta"), half + KD // 2)
            pe.wait_ge(S("norm_tv"), half + KD // 2)

        def norm_turn_act(act, norm, gain):
            for k in range(0, KD, 2):
                act.wait_ge(S("norm_turned"), KD * (norm - N3) + k + 1)
                act.activation(hT[:, k, :], bank[6][:, :], ACT.Copy, scale=col(gain, k)).then_inc(S("norm_ta"), 1)

        def norm_turn_dve(dve, own, norm, gain):
            for i in range(NT):
                dve.tensor_scalar(hn[:, i, :], x_res[:, i, :], nstat[norm][:, i:i + 1], None, ALU.mult)\
                    .then_inc(S("norm_scaled"), 1)
            for k in range(1, KD, 2):
                dve.wait_ge(S("norm_turned"), KD * (norm - N3) + k + 1)
                dve.tensor_scalar(hT[:, k, :], bank[7][:, :], col(gain, k), None, ALU.mult).then_inc(S("norm_tv"), 1)

        def hv(v, h):
            return v[:, P * h:P * h + P]

        def second_pool(pool):
            pool.wait_ge(S("y_part"), NE * NFC)
            pool.memset(mqz, 0.0).then_inc(S("mq_zero"), 1)
            pool.memset(mv.rearrange("p i (h d) -> p (i h) d", d=129)[:, :, 128:129], 1.0).then_inc(S("mv_one"), 1)
            pool.wait_ge(S("x_first"), NT)
            pool.dma_start(blk, A["blk"]).then_inc(S("blk_in"), 16)
            pool.wait_ge(S("blk_in"), 16)
            pool.wait_ge(S("prep_done"), 4)
            for l in range(7):
                for n in range(4):
                    u = 4 * l + n
                    if u >= 2:
                        pool.wait_ge(S("x_filled" if u - 2 >= 4 else "t_made"), u - 2 - 3 if u - 2 >= 4 else u - 1)
                    pool.tensor_tensor(out=moff[n % 2].rearrange("p (h c) -> p h c", c=P),
                                       in0=maT[:, n, :].rearrange("p (h c) -> p h c", c=P),
                                       in1=blk[:, l, :].unsqueeze(1).to_broadcast([P, 4, P]), op=ALU.mult)\
                        .then_inc(S("moff_made"), 1)

        def second_pe(pe, mm, turn):
            norm_turn_pe(pe, turn, N3)
            pe.wait_ge(S("wg_in"), 16)
            for i in range(NT):
                for k in range(KD):
                    last = mm(bank[0][:, 16 * i:16 * i + 16], hT[:, k, P * i:P * i + P], wg[:, k, :],
                              start=k == 0, stop=k == KD - 1)
            last.then_inc(S("gates_filled"), 1)
            for u in range(16):
                c = C_QKV + u // 2
                if u % 2 == 0:
                    wait_chunk(pe, c)
                if u >= 4:
                    pe.wait_ge(S("cv_done" if u - 4 < 12 else "qk_copied"), u - 3)
                w = slot(c).rearrange("p (k n) -> p k n", n=256)
                for k in range(KD):
                    last = mm(bank[1 + u % 4][:, :], w[:, k, P * (u % 2):P * (u % 2) + P], hT[:, k, :],
                              start=k == 0, stop=k == KD - 1)
                last.then_inc(S("qkv_filled"), 1)
            pe.wait_ge(S("gg_made"), 2)
            mm(bank[0][:, 64:80], utri, gg.rearrange("p n h -> p (n h)"), start=True, stop=True).then_inc(S("gc_filled"), 1)
            for v in range(12):
                i = v % 4
                if i == 0:
                    wait_chunk(pe, C_TOK + v // 2)
                    wait_chunk(pe, C_TOK + v // 2 + 1)
                if v < 4:
                    pe.wait_ge(S("qk_copied"), 13 + v)
                else:
                    pe.wait_ge(S("tok_copied"), v - 3)
                for half in range(2):
                    w = slot(C_TOK + 2 * (v // 4) + half).rearrange("p (k n) -> p k n", n=256)
                    for k in range(KD):
                        last = mm(bank[1 + i][:, 256 * half:256 * half + 256], hT[:, k, P * i:P * i + P], w[:, k, :],
                                  start=k == 0, stop=k == KD - 1)
                last.then_inc(S("tok_filled"), 1)
            for t in range(8):
                pe.wait_ge(S("l2_sq"), t + 1)
                if t >= 2:
                    pe.wait_ge(S("l2_sd"), t - 1)
                mm(bank[5 + t % 2][:, :], ones, tmp(t % 2), start=True, stop=True).then_inc(S("l2_filled"), 1)

            pe.wait_ge(S("l2_done"), 8)
            pe.wait_ge(S("cv_silu"), 12)
            pe.wait_ge(S("beta_made"), nth("beta_made", 1))
            pe.wait_ge(S("tok_copied"), 12)
            for n in range(4):
                t = slice(P * n, P * n + P)
                if n:
                    pe.wait_ge(S("prep_done"), n)
                for h in range(4):
                    mm(hv(bank[0], h), gg[:, n, h:h + 1].to_broadcast([P, P]), utri, start=True, stop=True)
                for h in range(4):
                    last = mm(hv(bank[1], h), beta[:, n, h:h + 1].to_broadcast([P, P]), ident, start=True, stop=True)
                last.then_inc(S("gb_filled"), 1)
                for h in range(4):
                    mm(hv(bank[2], h), qkv[:, 4 + h, t], qkv[:, h, t], start=True, stop=True)
                for h in range(4):
                    last = mm(hv(bank[3], h), qkv[:, 4 + h, t], qkv[:, 4 + h, t], start=True, stop=True)
                last.then_inc(S("kk_filled"), 1)
                for h in range(4):
                    turn(hv(bank[4], h), qkv[:, 4 + h, t], ident)
                for h in range(4):
                    last = turn(hv(bank[5], h), qkv[:, 8 + h, t], ident)
                last.then_inc(S("kv_turned"), 1)
            for n in range(4):
                pe.wait_ge(S("tt_made"), n + 1)
                if n == 0:
                    pe.wait_ge(S("prep_done"), 4)
                if n >= 2:
                    pe.wait_ge(S("t_made"), n - 1)
                for h in range(4):
                    last = turn(hv(bank[4 + n % 2], h), hv(tit[:, n, :], h), ident)
                last.then_inc(S("t_filled"), 1)

            def x_of(u):
                n = u % 4
                pe.wait_ge(S("moff_made"), u + 1)
                pe.wait_ge(S("t_made"), u - 3)
                if u >= 6:
                    pe.wait_ge(S("x_made"), u - 5)
                for h in range(4):
                    last = mm(hv(bank[n % 2], h), hv(moff[n % 2], h), hv(tin[:, n, :], h), start=True, stop=True)
                last.then_inc(S("x_filled"), 1)

            x_of(4)
            for u in range(4, 28):
                n = u % 4
                if u < 27:
                    x_of(u + 1)
                pe.wait_ge(S("x_made"), u - 3)
                if u >= 6:
                    pe.wait_ge(S("tt_made"), u - 1)
                for h in range(4):
                    last = mm(hv(bank[2 + n % 2], h), hv(xw[n % 2], h), hv(tit[:, n, :], h), start=True, stop=True)
                last.then_inc(S("tc_filled"), 1)
                if u < 24:
                    pe.wait_ge(S("tt_made"), u + 1)
                    pe.wait_ge(S("t_made"), u - 1)
                    for h in range(4):
                        last = turn(hv(bank[4 + n % 2], h), hv(tit[:, n, :], h), ident)
                    last.then_inc(S("t_filled"), 1)
            for n in range(4):
                pe.wait_ge(S("tt_made"), 25 + n)
                if n:
                    pe.wait_ge(S("w_made"), n)
                for h in range(4):
                    last = mm(hv(bank[6], h), hv(kbg[:, n, :], h), hv(tit[:, n, :], h), start=True, stop=True)
                last.then_inc(S("w_filled"), 1)
            pe.wait_ge(S("w_made"), 4)
            pe.wait_ge(S("st_made"), 1)
            for n in range(4):
                pe.wait_ge(S("st_made"), 4 * n + 1)
                for h in range(4):
                    mm(hv(bank[7], h), hv(tit[:, n, :], h), hv(vbt[:, n, :], h), start=True, stop=False)
                    last = mm(hv(bank[7], h), hv(wneg[:, n, :], h), hv(state, h), start=False, stop=True)
                last.then_inc(S("vn_filled"), 1)
                pe.wait_ge(S("vn_made"), n + 1)
                if n >= 2:
                    pe.wait_ge(S("oa_made"), n - 1)
                for h in range(4):
                    mm(hv(bank[n % 2], h), qkv[:, h, P * n:P * n + P], hv(state, h), start=True, stop=False)
                    last = mm(hv(bank[n % 2], h), hv(atT[:, n, :], h), hv(vnew[n % 2], h), start=False, stop=True)
                last.then_inc(S("oa_filled"), 1)
                if n < 3:
                    for h in range(4):
                        last = mm(hv(bank[6], h), hv(kdc[:, n, :], h), hv(vnew[n % 2], h), start=True, stop=True)
                    last.then_inc(S("sk_filled"), 1)
            pe.wait_ge(S("gg_made"), 4)
            pe.wait_ge(S("oa_made"), 4)
            for i in range(NT):
                turn(bank[0][0:4, P * i:P * i + P], lf[:, i, :], ident)
            for i in range(NT):
                last = turn(bank[1][0:4, P * i:P * i + P], ip[:, i, :], ident)
            last.then_inc(S("rows_filled"), 1)
            pe.wait_ge(S("mrow_made"), nth("mrow_made", 1))
            for i in range(NT):
                turn(bank[2][:, 4 * i:4 * i + 4], arow[0:4, P * i:P * i + P], ident[0:4, 0:4])
                last = turn(bank[2][:, 16 + 4 * i:20 + 4 * i], mrow[0:4, P * i:P * i + P], ident[0:4, 0:4])
            last.then_inc(S("mcol_filled"), 1)
            pe.wait_ge(S("mq_zero"), 1)
            pe.wait_ge(S("mv_one"), 1)
            for h in range(MH):
                if h:
                    pe.wait_ge(S("mp_made"), h)
                mm(bank[3][:, :], ident[0:4, h:h + 1].to_broadcast([4, P]), mxrow[0:4, :], start=True, stop=True)\
                    .then_inc(S("mb_filled"), 1)
                for a, (b, o) in enumerate(((4, 0), (5, 0), (6, 0), (5, 384))):
                    last = mm(bank[b][:, o:o + L - P * a], mk[:, h // 2, P * a:P * a + P], mqz[:, h, P * a:L],
                              start=True, stop=True)
                last.then_inc(S("ms_filled"), 1)
                pe.wait_ge(S("mp_made"), h + 1)
                pe.wait_ge(S("ob_made"), 4 * h)
                for i in range(NT):
                    for a in range(i + 1):
                        o = (0, 512, 896, 1152)[a]
                        last = mm(bank[i // 2][:, 129 * (i % 2):129 * (i % 2) + 129],
                                  expo[:, o + P * (i - a):o + P * (i - a) + P], mv[:, a, 129 * h:129 * h + 129],
                                  start=a == 0, stop=a == i)
                last.then_inc(S("mo_filled"), 1)
            for br in range(2):
                pe.wait_ge(S("on2_made"), NT * (br + 1))
                for m in range(4):
                    u = 4 * br + m
                    if u >= 2:
                        pe.wait_ge(S("oT_made"), u - 1)
                    for i in range(NT):
                        last = turn(bank[4 + u % 2][:, P * i:P * i + P], (oa, ob)[br][:, i, P * m:P * m + P], ident)
                    last.then_inc(S("oT_filled"), 1)
            pe.wait_ge(S("oT_made"), 8)
            for f in range(16):
                br, g = f // 8, f // 4
                if f % 4 == 0:
                    wait_chunk(pe, C_BR + 3 * g)
                if f >= 2:
                    pe.wait_ge(S("br_used"), f - 1)
                w = slot(C_BR + 3 * g).rearrange("p (k n) -> p k n", n=512)
                for k in range(4):
                    last = mm(bank[f % 2][:, :], w[:, k, P * (f % 4):P * (f % 4) + P], (oTa, oTb)[br][:, k, :],
                              start=k == 0, stop=k == 3)
                last.then_inc(S("br_filled"), 1)
                c = C_BR + 3 * g + 1 + (f % 4) // 2
                wait_chunk(pe, c)
                w = slot(c).rearrange("p (k n) -> p k n", n=256)
                for k in range(KD):
                    last = mm(bank[2 + f % 2][:, :], w[:, k, P * (f % 2):P * (f % 2) + P], hT[:, k, :],
                              start=k == 0, stop=k == KD - 1)
                last.then_inc(S("br_filled"), 1)
            pe.wait_ge(S("br_used"), 16)
            for c in range(4):
                wait_chunk(pe, C_OUT2 + c)
                w = slot(C_OUT2 + c).rearrange("p (k n) -> p k n", n=256)
                for i in range(NT):
                    u = 4 * c + i
                    if u >= 4:
                        pe.wait_ge(S("out2_added"), u - 3)
                    for k in range(KD):
                        last = mm(bank[4 + i][:, 0:256], mixed[:, k, P * i:P * i + P], w[:, k, :], start=k == 0, stop=k == KD - 1)
                    last.then_inc(S("out2_filled"), 1)
            norm_turn_pe(pe, turn, N4)

            def up_tile(c, ic, f2, done):
                for which in range(2):
                    pe.wait_ge(S(f"chunk_in{(c + which) % R}"), ic)
                    w = slot(c + which).rearrange("p (k n) -> p k n", n=256)
                    if which == 0:
                        pe.wait_ge(S("act_made"), done)
                    for k in range(KD):
                        last = mm(bank[2 * which + f2][:, :], w[:, k, P * f2:P * f2 + P], hT[:, k, :],
                                  start=k == 0, stop=k == KD - 1)
                    last.then_inc(S("up_filled"), 1)

            pe.sem_inc(S("act_made"), 2)
            with pe.Fori(0, NFT // 4) as r:
                for q in range(4):
                    c = C_UP + 2 * (q // 2)
                    up_tile(c, r * 16 + 16 * (c // R + 1), q % 2, r * 4 + (q + 1))
            for q in range(NFT % 4):
                c = C_UP + NFT // 4 * 4
                up_tile(c, 16 * (c // R + 1), q % 2, NFT // 4 * 4 + q + 1)
            pe.wait_ge(S("act_made"), NFT + 2)
            for n in range(2):
                for d in range(6):
                    c = C_DOWN + 6 * n + d
                    wait_chunk(pe, c)
                    w = slot(c).rearrange("p (k n) -> p k n", n=512)
                    for k in range(4 * d, min(4 * d + 4, NFT)):
                        for i in range(NT):
                            last = mm(bank[4 * (1 - n) + i][:, :], actT[:, k, P * i:P * i + P], w[:, k - 4 * d, :],
                                      start=k == 0, stop=k == NFT - 1)
                    last.then_inc(S("down_chunk"), 1)
            pe.wait_ge(S("pT_in"), 16)
            pe.wait_ge(S("down_added"), 8)
            wait_chunk(pe, C_PLE)
            w = slot(C_PLE).rearrange("p (k n) -> p k n", n=1024)
            for u in range(8):
                i, n = u // 2, u % 2
                if u >= 4:
                    pe.wait_ge(S("pw_made"), u - 3)
                for k in range(2):
                    last = mm(bank[u % 4][:, :], pT[:, k, P * i:P * i + P], w[:, k, 512 * n:512 * n + 512],
                              start=k == 0, stop=k == 1)
                last.then_inc(S("ple_filled"), 1)
            norm_turn_pe(pe, turn, N5)
            pe.wait_ge(S("pw_made"), 8)
            for c in range(4):
                wait_chunk(pe, C_PG + c)
                w = slot(C_PG + c).rearrange("p (k n) -> p k n", n=256)
                for i in range(NT):
                    u = 4 * c + i
                    if u >= 4:
                        pe.wait_ge(S("pg_copied"), u - 3)
                    for k in range(KD):
                        last = mm(bank[i][:, 0:256], hT[:, k, P * i:P * i + P], w[:, k, :], start=k == 0, stop=k == KD - 1)
                    last.then_inc(S("pg_filled"), 1)

        def second_dve(dve, own):
            stt = dve.scalar_tensor_tensor
            tt = dve.tensor_tensor
            ts = dve.tensor_scalar
            norm_rstd(dve, own, NF)
            dve.wait_ge(S("gfirst_in"), 16)
            for i in range(NT):
                stt(out=x_res[:, i, :], in0=x_res[:, i, :], scalar=nstat[NF][:, i:i + 1], in1=grow, op0=ALU.mult,
                    op1=ALU.mult).then_inc(S("x_first"), 1)
            dve.wait_ge(S("x_first"), NT)
            norm_rstd(dve, own, N3)
            norm_turn_dve(dve, own, N3, "gmix2")
            dve.wait_ge(S("gates_filled"), nth("gates_filled", 1))
            dve.wait_ge(S("rows_in"), 16)
            g3 = bank[0][:, 0:64].rearrange("p (i g) -> p i g", g=16)

            def rb(name):
                return row(name).unsqueeze(1).to_broadcast([P, NT, 4])

            own(tt(out=gx[:, :, 0:4], in0=g3[:, :, 4:8], in1=rb("dtb"), op=ALU.add))
            own(tt(out=gx[:, :, 4:8], in0=g3[:, :, 12:16], in1=rb("fb"), op=ALU.add))
            own(tt(out=ip, in0=g3[:, :, 8:12], in1=rb("ib"), op=ALU.add))
            own.wait()
            stt(out=gl_, in0=gx, scalar=-1.0, in1=gx, op0=ALU.mult, op1=ALU.max).then_inc(S("gabs_made"), 1)
            for u in range(12):
                ps = bank[1 + u % 4]
                dve.wait_ge(S("qk_copied"), u + 1)
                for j in (1, 2):
                    own(stt(out=qkv[:, u, j:L], in0=ps[:, 0:L - j], scalar=col(f"cw{3 - j}", u), in1=qkv[:, u, j:L],
                            op0=ALU.mult, op1=ALU.add))
                    own.wait()
                stt(out=qkv[:, u, 3:L], in0=ps[:, 0:L - 3], scalar=col("cw0", u), in1=qkv[:, u, 3:L],
                    op0=ALU.mult, op1=ALU.add).then_inc(S("cv_done"), 1)
                if u == 1:
                    dve.wait_ge(S("glog_made"), nth("glog_made", 1))
                    own(stt(out=gg, in0=gx[:, :, 0:4], scalar=0.0, in1=gl_[:, :, 0:4], op0=ALU.max, op1=ALU.add))
                    own.wait()
                    stt(out=gg, in0=gg, scalar=-1.0, in1=ea.unsqueeze(1).to_broadcast([P, NT, 4]), op0=ALU.mult,
                        op1=ALU.mult).then_inc(S("gg_made"), 1)
                    stt(out=lf, in0=gx[:, :, 4:8], scalar=0.0, in1=gl_[:, :, 4:8], op0=ALU.min, op1=ALU.subtract)\
                        .then_inc(S("gg_made"), 1)
                    dve.wait_ge(S("gg_made"), 2)
                    dve.engine_nop().then_inc(S("gg_made"), 2)
            dve.wait_ge(S("gc_filled"), nth("gc_filled", 1))
            dve.wait_ge(S("eg_made"), nth("eg_made", 1))
            own(dve.tensor_copy(gc.rearrange("p n h -> p (n h)"), bank[0][:, 64:80]))
            dve.wait_ge(S("beta_made"), nth("beta_made", 1))
            own(tt(out=ebg, in0=eg, in1=beta, op=ALU.mult))
            for t in range(8):
                dve.wait_ge(S("l2_sd"), t + 1)
                own(dve.reciprocal(tmp(2 + t % 2), tmp(2 + t % 2)))
                own.wait()
                stt(out=qkv[:, t, :], in0=qkv[:, t, :], scalar=DK ** -0.5 if t < 4 else 1.0, in1=tmp(2 + t % 2),
                    op0=ALU.mult, op1=ALU.mult).then_inc(S("l2_done"), 1)
            dve.wait_ge(S("l2_done"), 8)

            def h3(v):
                return v.rearrange("p (h c) -> p h c", c=P)

            def per_token(v, n):
                return v[:, n, :].unsqueeze(2).to_broadcast([P, 4, P])

            def every_head(m):
                return m.unsqueeze(1).to_broadcast([P, 4, P])

            for n in range(4):
                t = slice(P * n, P * n + P)
                dve.wait_ge(S("gb_filled"), n + 1)
                own(tt(out=h3(dec), in0=h3(bank[0][:, :]), in1=per_token(gc, n), op=ALU.subtract))
                own(tt(out=edec[:, n, :], in0=h3(bank[0][:, :])[:, :, P - 1], in1=gc[:, n, :], op=ALU.subtract))
                own.wait()
                ts(dec, dec, 0.0, None, ALU.min).then_inc(S("dec_ready"), 1)
                dve.wait_ge(S("dec_made"), 3 * n + 3)
                own(dve.tensor_copy(egl[:, 4 * n:4 * n + 4], h3(egb)[:, :, P - 1]))
                own(tt(out=h3(dms), in0=h3(dec), in1=every_head(strict), op=ALU.mult))
                own.wait()
                own(tt(out=dms, in0=dms, in1=bank[1][:, :], op=ALU.mult))
                own(tt(out=h3(dec), in0=h3(dec), in1=every_head(utri), op=ALU.mult))
                own.wait()
                dve.wait_ge(S("kk_filled"), n + 1)
                own(tt(out=atT[:, n, :], in0=bank[2][:, :], in1=dec, op=ALU.mult))
                own(tt(out=maT[:, n, :], in0=bank[3][:, :], in1=dms, op=ALU.mult))
                own(tt(out=qkv[:, 0:4, t], in0=qkv[:, 0:4, t], in1=h3(egb), op=ALU.mult))
                dve.wait_ge(S("kv_turned"), n + 1)
                own(tt(out=h3(kbg[:, n, :]), in0=h3(bank[4][:, :]), in1=per_token(ebg, n), op=ALU.mult))
                own(tt(out=h3(kdc[:, n, :]), in0=h3(bank[4][:, :]), in1=per_token(edec, n), op=ALU.mult))
                own(tt(out=h3(vbt[:, n, :]), in0=h3(bank[5][:, :]), in1=per_token(beta, n), op=ALU.mult))
                own.wait()
                dve.engine_nop().then_inc(S("prep_done"), 1)
            for n in range(4):
                dve.wait_ge(S("moff_made"), n + 1)
                tt(out=h3(tit[:, n, :]), in0=every_head(ident), in1=h3(moff[n % 2]), op=ALU.subtract)\
                    .then_inc(S("tt_made"), 1)
            for u in range(4, 28):
                n = u % 4
                dve.wait_ge(S("tc_filled"), u - 3)
                tt(out=tit[:, n, :], in0=tit[:, n, :], in1=bank[2 + n % 2][:, :], op=ALU.subtract).then_inc(S("tt_made"), 1)
            dve.wait_ge(S("w_filled"), 4)
            dve.memset(state, 0.0).then_inc(S("st_made"), 1)
            for n in range(4):
                dve.wait_ge(S("vn_filled"), n + 1)
                dve.tensor_copy(vnew[n % 2], bank[7][:, :]).then_inc(S("vn_made"), 1)
                if n < 3:
                    dve.wait_ge(S("sk_filled"), n + 1)
                    dve.wait_ge(S("oa_filled"), n + 1)
                    dve.wait_ge(S("st_made"), 4 * n + 1)
                    for h in range(4):
                        stt(out=hv(state, h), in0=hv(state, h), scalar=egl[:, 4 * n + h:4 * n + h + 1],
                            in1=hv(bank[6], h), op0=ALU.mult, op1=ALU.add).then_inc(S("st_made"), 1)
            dve.wait_ge(S("rows_filled"), nth("rows_filled", 1))
            own(dve.tensor_copy(mxrow[0:4, :], bank[0][0:4, :]))
            own.wait()
            own(dve.tensor_tensor_scan(out=brow[0:4, :], data0=mxrow[0:4, :], data1=mxrow[0:4, :], initial=0.0,
                                       op0=ALU.add, op1=ALU.bypass))
            own.wait()
            own(tt(out=arow[0:4, :], in0=bank[1][0:4, :], in1=brow[0:4, :], op=ALU.subtract))
            own.wait()
            own(dve.tensor_tensor_scan(out=mxrow[0:4, :], data0=arow[0:4, :], data1=arow[0:4, :], initial=0.0,
                                       op0=ALU.max, op1=ALU.bypass))
            own.wait()
            tt(out=mrow[0:4, :], in0=brow[0:4, :], in1=mxrow[0:4, :], op=ALU.add).then_inc(S("mrow_made"), 1)
            dve.wait_ge(S("mcol_filled"), nth("mcol_filled", 1))
            dve.wait_ge(S("em_made"), nth("em_made", 1))
            own(dve.tensor_copy(acol.rearrange("p i h -> p (i h)"), bank[2][:, 0:16]))
            own.wait()
            offs = (0, 512, 896, 1152)
            where = ((4, 0), (5, 0), (6, 0), (5, 384))
            for h in range(MH):
                dve.wait_ge(S("mb_filled"), h + 1)
                if h:
                    dve.wait_ge(S("mo_filled"), h)
                for a in range(NT):
                    last = ts(expo[:, offs[a]:offs[a] + L - P * a], bank[3][:, P * a:L], acol[:, a, h:h + 1], 0.0,
                              ALU.subtract, ALU.max)
                    last.then_inc(S("mx_made"), 1)
                dve.wait_ge(S("me_made"), h + 1)
                for a in range(NT):
                    own(tt(out=expo[:, offs[a]:offs[a] + P], in0=expo[:, offs[a]:offs[a] + P], in1=utri, op=ALU.mult))
                own.wait()
                dve.wait_ge(S("ms_filled"), h + 1)
                for a in range(NT):
                    b, o = where[a]
                    e = expo[:, offs[a]:offs[a] + L - P * a]
                    own(tt(out=e, in0=e, in1=bank[b][:, o:o + L - P * a], op=ALU.mult))
                own.wait()
                dve.engine_nop().then_inc(S("mp_made"), 1)
                dve.wait_ge(S("mo_filled"), h + 1)
                for i in range(NT):
                    o = 129 * (i % 2)
                    dn = den[:, i:i + 1]
                    d = bank[i // 2][:, o + 128:o + 129]
                    own(stt(out=dn, in0=d, scalar=-1.0, in1=emcol[:, i, h:h + 1], op0=ALU.mult, op1=ALU.max))
                    own.wait()
                    own(tt(out=dn, in0=dn, in1=d, op=ALU.max))
                own.wait()
                own(dve.reciprocal(den[:, 0:4], den[:, 0:4]))
                own.wait()
                for i in range(NT):
                    o = 129 * (i % 2)
                    ts(ob[:, i, P * h:P * h + P], bank[i // 2][:, o:o + P], den[:, i:i + 1], None, ALU.mult)\
                        .then_inc(S("ob_made"), 1)
            dve.wait_ge(S("ob_made"), 16)
            for br, (o, gate_) in enumerate(((oa, gz), (ob, mo))):
                sq = view(T0 + 4096, NT, 512)
                dve.wait_ge(S("osq_made"), nth("osq_made", br + 1))
                hs = hstat[:, 16 * br:16 * br + 16]
                own(dve.tensor_reduce(out=hs, in_=sq.rearrange("p i (h d) -> p (i h) d", d=P), axis=AX.X, op=ALU.add))
                own.wait()
                ts(hs, hs, 1.0 / P, EPS, ALU.mult, ALU.add).then_inc(S("ovar_made"), 1)
                dve.wait_ge(S("osd_made"), nth("osd_made", br + 1))
                own(dve.reciprocal(hs, hs))
                own.wait()
                for i in range(NT):
                    v = h3(o[:, i, :])
                    own(tt(out=v, in0=v, in1=hs[:, 4 * i:4 * i + 4].unsqueeze(2).to_broadcast([P, 4, P]), op=ALU.mult))
                    own.wait()
                    own(tt(out=v, in0=v, in1=every_head(row("gdn")) if br == 0 else h3(row("mln")), op=ALU.mult))
                    own.wait()
                    tt(out=o[:, i, :], in0=o[:, i, :], in1=gate_[:, i, :], op=ALU.mult).then_inc(S("on2_made"), 1)
            for f in range(16):
                dve.wait_ge(S("br_filled"), 2 * f + 2)
                dve.wait_ge(S("sg_made"), f + 1)
                m = mixed[:, f % 8, :]
                if f < 8:
                    tt(out=m, in0=tmp(f % 2), in1=bank[f % 2][:, :], op=ALU.mult).then_inc(S("br_used"), 1)
                else:
                    own(tt(out=tmp(f % 2), in0=tmp(f % 2), in1=bank[f % 2][:, :], op=ALU.mult))
                    own.wait()
                    tt(out=m, in0=m, in1=tmp(f % 2), op=ALU.add).then_inc(S("br_used"), 1)
            for c in range(4):
                for i in range(NT):
                    dve.wait_ge(S("out2_filled"), 4 * c + i + 1)
                    xs = x_res[:, i, 256 * c:256 * c + 256]
                    tt(out=xs, in0=xs, in1=bank[4 + i][:, 0:256], op=ALU.add).then_inc(S("out2_added"), 1)
            norm_rstd(dve, own, N4)
            norm_turn_dve(dve, own, N4, "gffn")

            def act_tile(f, f2, filled, silus):
                dve.wait_ge(S("up_filled"), filled)
                dve.wait_ge(S("fsilu_made"), silus)
                tt(out=f, in0=tmp(f2), in1=bank[2 + f2][:, :], op=ALU.mult).then_inc(S("act_made"), 1)

            with dve.Fori(0, NFT // 4) as r:
                for q in range(4):
                    act_tile(actT[:, bass.ds(r * 4 + q, 1), :].rearrange("p a t -> p (a t)"), q % 2,
                             r * 8 + (2 * q + 2), r * 4 + (q + 1))
            for f in range(NFT // 4 * 4, NFT):
                act_tile(actT[:, f, :], f % 2, 2 * f + 2, f + 1)
            for n in range(2):
                dve.wait_ge(S("down_chunk"), 6 * n + 6)
                for i in range(NT):
                    xs = x_res[:, i, 512 * n:512 * n + 512]
                    tt(out=xs, in0=xs, in1=bank[4 * (1 - n) + i][:, :], op=ALU.add).then_inc(S("down_added"), 1)
            norm_rstd(dve, own, N5)
            norm_turn_dve(dve, own, N5, "gple")
            dve.wait_ge(S("pw_made"), 8)
            for c in range(4):
                for i in range(NT):
                    u = 4 * c + i
                    dve.wait_ge(S("pg_copied"), u + 1)
                    g = tmp(u % 4)[:, 0:256]
                    own(tt(out=g, in0=g, in1=pw[:, i, 256 * c:256 * c + 256], op=ALU.mult))
                    own.wait()
                    xs = x_res[:, i, 256 * c:256 * c + 256]
                    tt(out=xs, in0=xs, in1=g, op=ALU.add).then_inc(S("pg_added"), 1)
            norm_rstd(dve, own, NO)
            dve.wait_ge(S("gfin_in"), 16)
            for i in range(NT):
                stt(out=hn[:, i, :], in0=x_res[:, i, :], scalar=nstat[NO][:, i:i + 1], in1=grow, op0=ALU.mult,
                    op1=ALU.mult).then_inc(S("out_made"), 1)

        def second_act(act, own):
            fn = act.activation
            norm_squares(act, NF, "sc_added", lambda i: 8 * (NE - 1) + 2 * i + 4)
            norm_squares(act, N3, "x_first", lambda i: i + 1)
            norm_turn_act(act, N3, "gmix2")
            act.wait_ge(S("gabs_made"), nth("gabs_made", 1))
            fn(beta, bank[0][:, 0:64].rearrange("p (i g) -> p i g", g=16)[:, :, 0:4], ACT.Sigmoid).then_inc(S("beta_made"), 1)
            act.wait_ge(S("rows_in"), 16)
            own(fn(ea, row("alog"), ACT.Exp))
            own(fn(gl_, gl_, ACT.Exp, scale=-1.0))
            own.wait()
            fn(gl_, gl_, ACT.Ln, bias=1.0).then_inc(S("glog_made"), 1)

            def conv_silu(u):
                act.wait_ge(S("cv_done"), u + 1)
                fn(qkv[:, u, :], qkv[:, u, :], ACT.Silu).then_inc(S("cv_silu"), 1)

            for u in range(16):
                ps = bank[1 + u % 4]
                act.wait_ge(S("qkv_filled"), u + 1)
                if u < 12:
                    fn(qkv[:, u, :], ps[:, :], ACT.Copy, scale=col("cw3", u)).then_inc(S("qk_copied"), 1)
                elif u < 14:
                    m = u - 12
                    if m == 0:
                        act.wait_ge(S("mq_zero"), 1)
                    for hh in range(2):
                        q = slice(64 * hh, 64 * hh + 64)
                        last = fn(mqz[q, 2 * m + hh, :], ps[q, :], ACT.Copy, scale=MQ ** -0.5)
                        if hh == 0:
                            own(last)
                    last.then_inc(S("qk_copied"), 1)
                else:
                    fn(mk[:, u - 14, :], ps[:, :], ACT.Copy).then_inc(S("qk_copied"), 1)
                if 2 <= u < 14:
                    conv_silu(u - 2)
            act.wait_ge(S("gc_filled"), nth("gc_filled", 1))
            fn(eg.rearrange("p n h -> p (n h)"), bank[0][:, 64:80], ACT.Exp).then_inc(S("eg_made"), 1)
            for v in range(12):
                i = v % 4
                ps = bank[1 + i][:, :]
                act.wait_ge(S("tok_filled"), v + 1)
                if v < 4:
                    fn(gz[:, i, :], ps, ACT.Silu).then_inc(S("tok_copied"), 1)
                elif v < 8:
                    fn(mv[:, i, :].rearrange("p (h d) -> p h d", d=129)[:, :, 0:128],
                       ps.rearrange("p (h d) -> p h d", d=P), ACT.Copy).then_inc(S("tok_copied"), 1)
                else:
                    fn(mo[:, i, :], ps, ACT.Sigmoid).then_inc(S("tok_copied"), 1)
            act.wait_ge(S("cv_silu"), 12)

            def l2_square(t):
                if t >= 2:
                    act.wait_ge(S("l2_filled"), t - 1)
                fn(tmp(t % 2), qkv[:, t, :], ACT.Square).then_inc(S("l2_sq"), 1)

            l2_square(0)
            l2_square(1)
            for t in range(8):
                act.wait_ge(S("l2_filled"), t + 1)
                if t >= 2:
                    act.wait_ge(S("l2_done"), t - 1)
                fn(tmp(2 + t % 2), bank[5 + t % 2][:, :], ACT.Sqrt, bias=EPS).then_inc(S("l2_sd"), 1)
                if t + 2 < 8:
                    l2_square(t + 2)
            for n in range(4):
                act.wait_ge(S("gb_filled"), n + 1)
                if n:
                    act.wait_ge(S("prep_done"), n)
                act.wait_ge(S("dec_ready"), n + 1)
                fn(egb, bank[0][:, :], ACT.Exp).then_inc(S("dec_made"), 1)
                fn(dec, dec, ACT.Exp).then_inc(S("dec_made"), 1)
                fn(edec[:, n, :], edec[:, n, :], ACT.Exp).then_inc(S("dec_made"), 1)
            for n in range(4):
                act.wait_ge(S("t_filled"), n + 1)
                fn(tin[:, n, :], bank[4 + n % 2][:, :], ACT.Copy).then_inc(S("t_made"), 1)

            def x_out(u):
                n = u % 4
                act.wait_ge(S("x_filled"), u - 3)
                if u >= 6:
                    act.wait_ge(S("tc_filled"), u - 5)
                fn(xw[n % 2], bank[n % 2][:, :], ACT.Copy).then_inc(S("x_made"), 1)

            x_out(4)
            for u in range(4, 28):
                n = u % 4
                if u < 27:
                    x_out(u + 1)
                if u < 24:
                    act.wait_ge(S("t_filled"), u + 1)
                    fn(tin[:, n, :], bank[4 + n % 2][:, :], ACT.Copy).then_inc(S("t_made"), 1)
            for n in range(4):
                act.wait_ge(S("w_filled"), n + 1)
                fn(wneg[:, n, :], bank[6][:, :], ACT.Copy, scale=-1.0).then_inc(S("w_made"), 1)
            for n in range(4):
                act.wait_ge(S("oa_filled"), n + 1)
                fn(oa[:, n, :], bank[n % 2][:, :], ACT.Copy).then_inc(S("oa_made"), 1)
            act.wait_ge(S("mcol_filled"), nth("mcol_filled", 1))
            fn(emcol.rearrange("p i h -> p (i h)"), bank[2][:, 16:32], ACT.Exp, scale=-1.0).then_inc(S("em_made"), 1)
            for h in range(MH):
                act.wait_ge(S("mx_made"), 4 * h + 4)
                fn(expo, expo, ACT.Exp, scale=-1.0).then_inc(S("me_made"), 1)
            for br, o in enumerate((oa, ob)):
                if br == 0:
                    act.wait_ge(S("oa_made"), 4)
                    act.wait_ge(S("mo_filled"), MH)
                else:
                    act.wait_ge(S("ob_made"), 16)
                    act.wait_ge(S("ovar_made"), nth("ovar_made", 1))
                fn(view(T0 + 4096, 2048), o.rearrange("p i d -> p (i d)"), ACT.Square).then_inc(S("osq_made"), 1)
                act.wait_ge(S("ovar_made"), nth("ovar_made", br + 1))
                hs = hstat[:, 16 * br:16 * br + 16]
                fn(hs, hs, ACT.Sqrt).then_inc(S("osd_made"), 1)
            for u in range(8):
                act.wait_ge(S("oT_filled"), u + 1)
                fn((oTa, oTb)[u // 4][:, u % 4, :], bank[4 + u % 2][:, :], ACT.Copy).then_inc(S("oT_made"), 1)
            for f in range(16):
                act.wait_ge(S("br_filled"), 2 * f + 2)
                if f >= 2:
                    act.wait_ge(S("br_used"), f - 1)
                fn(tmp(f % 2), bank[2 + f % 2][:, :], ACT.Sigmoid).then_inc(S("sg_made"), 1)
            norm_squares(act, N4, "out2_added", lambda i: 13 + i)
            norm_turn_act(act, N4, "gffn")

            def up_silu(f2, filled, made):
                act.wait_ge(S("up_filled"), filled)
                act.wait_ge(S("act_made"), made)
                fn(tmp(f2), bank[f2][:, :], ACT.Silu).then_inc(S("fsilu_made"), 1)

            with act.Fori(0, NFT // 4) as r:
                for q in range(4):
                    up_silu(q % 2, r * 8 + (2 * q + 1), r * 4 + (q + 1))
            for f in range(NFT // 4 * 4, NFT):
                up_silu(f % 2, 2 * f + 1, f + 1)
            act.wait_ge(S("down_chunk"), 12)
            for u in range(8):
                i, n = u // 2, u % 2
                act.wait_ge(S("ple_filled"), u + 1)
                fn(pw[:, i, 512 * n:512 * n + 512], bank[u % 4][:, :], ACT.Copy).then_inc(S("pw_made"), 1)
            norm_squares(act, N5, "down_added", lambda i: 5 + i)
            norm_turn_act(act, N5, "gple")
            for c in range(4):
                for i in range(NT):
                    u = 4 * c + i
                    act.wait_ge(S("pg_filled"), u + 1)
                    if u >= 4:
                        act.wait_ge(S("pg_added"), u - 3)
                    fn(tmp(u % 4)[:, 0:256], bank[i][:, 0:256], ACT.Sigmoid).then_inc(S("pg_copied"), 1)
            norm_squares(act, NO, "pg_added", lambda i: 13 + i)

        wpack = A["wpack"]

        @block.sync
        def _(sp):
            def chunk(c):
                if c >= R:
                    name, v = used[c - R]
                    sp.wait_ge(S(name), v)
                sp.dma_start(slot(c), wpack[c]).then_inc(S(f"chunk_in{c % R}"), 16)

            sp.dma_start(hT, A["xT"].rearrange("(k p) t -> p k t", p=P)).then_inc(S("xT_in"), 16)
            chunk(0)
            chunk(1)
            chunk(2)
            chunk(3)
            for c in range(4, C_OUT1):
                chunk(c)
            sp.wait_ge(S("proj_filled"), 20)
            sp.dma_start(x_res, A["x"].rearrange("(i p) d -> p i d", p=P)).then_inc(S("x_in"), 16)
            for i in range(3):
                sp.wait_ge(S("proj_copied"), 16 + i + 2)
                sp.dma_start(vb_[0:64, i, :], va[64:P, i, :]).then_inc(S("vb_in"), 16)
                sp.dma_start(vb_[64:P, i, :], va[0:64, i + 1, :]).then_inc(S("vb_in"), 16)
            for c in range(C_OUT1, C_QKV):
                chunk(c)

            g_v = A["w_gate"].rearrange("e (k p) (c n) -> e c p k n", p=P, n=FC)
            u_v = A["w_up"].rearrange("e (k p) (c n) -> e c p k n", p=P, n=FC)
            d_v = A["w_down"].rearrange("e (c k p) n -> e c p k n", p=P, k=FC // P)

            def expert_chunk(e, c):
                s = 3 * (c % 2)
                sp.dma_start(mslot[s].rearrange("p (k n) -> p k n", n=FC), g_v[e, c]).then_inc(S(f"ew_in{s}"), 16)
                sp.dma_start(mslot[s + 1].rearrange("p (k n) -> p k n", n=FC), u_v[e, c]).then_inc(S(f"ew_in{s + 1}"), 16)

            def expert_down(e, c):
                s = 3 * (c % 2) + 2
                sp.dma_start(mslot[s].rearrange("p (k n) -> p k n", n=D), d_v[e, c]).then_inc(S(f"ew_in{s}"), 16)

            sp.wait_ge(S("out1_filled"), 16)
            for c in range(2):
                expert_chunk(0, c)
                expert_down(0, c)
            with sp.Fori(0, NE - 1) as e:
                for c in range(NFC):
                    sp.wait_ge(S("ab_filled"), e * NFC + (c + 2))
                    expert_chunk(e + (c + 2) // NFC, (c + 2) % NFC)
                    sp.wait_ge(S("y_part"), e * NFC + (c + 1))
                    expert_down(e + (c + 2) // NFC, (c + 2) % NFC)
            for c in range(2):
                sp.wait_ge(S("ab_filled"), (NE - 1) * NFC + c + 2)
                expert_chunk(NE - 1, c + 2)
                sp.wait_ge(S("y_part"), (NE - 1) * NFC + c + 1)
                expert_down(NE - 1, c + 2)

            sp.wait_ge(S("y_part"), NE * NFC)
            sp.dma_start(wg, A["w_gates"].rearrange("(k p) n -> p k n", p=P)).then_inc(S("wg_in"), 16)
            for c in range(C_QKV, N_CHUNKS):
                if c >= C_QKV + R:
                    name, v = used[c - R]
                    sp.wait_ge(S(name), v)
                sp.dma_start(slot(c), wpack[c]).then_inc(S(f"chunk_in{c % R}"), 16)
                if c == C_DOWN:
                    sp.dma_start(view(B + 15360, 2, L), A["pT"].rearrange("(k p) t -> p k t", p=P)).then_inc(S("pT_in"), 16)
                    sp.dma_start(grow, A["gfin"].partition_broadcast(P)).then_inc(S("gfin_in"), 16)
            for i in range(NT):
                sp.wait_ge(S("out_made"), i + 1)
                sp.dma_start(out.rearrange("a (i p) d -> i p (a d)", p=P)[i], hn[:, i, :]).then_inc(S("stored"), 16)
            sp.wait_ge(S("stored"), 16 * NT)

        @block.gpsimd
        def _(pool):
            own = Own(pool, "pool_own")
            pool.dma_start(cols[:, 0:N_COLS], A["cols"]).then_inc(S("cols_in"), 16)
            pool.dma_start(pos, A["pos"]).then_inc(S("fnet_in"), 16)
            pool.dma_start(fw1, A["fw1"]).then_inc(S("fnet_in"), 16)
            pool.dma_start(fw2, A["fw2"]).then_inc(S("fnet_in"), 16)
            pool.dma_start(fwo, A["fwo"]).then_inc(S("fnet_in"), 16)
            pool.dma_start(decay[:, 0, :], A["deltas"].partition_broadcast(P)).then_inc(S("fnet_in"), 16)
            pool.dma_start(view(8192, 3 * P + P), A["consts"]).then_inc(S("const_in"), 16)
            pool.dma_start(rows, A["rows"].partition_broadcast(P)).then_inc(S("rows_in"), 16)
            pool.dma_start(invc, A["invc"]).then_inc(S("invc_in"), 16)
            pool.dma_start(pwbd, A["pwbd"].rearrange("a p d -> p a d")).then_inc(S("pw_in"), 16)
            pool.memset(qz, 0.0).then_inc(S("qz_zero"), 1)
            mask = stat[:, 0:3 * KC].rearrange("p (a b) -> p a b", b=KC)
            pool.dma_start(mask, A["mask"]).then_inc(S("mask_in"), 16)
            for c in range(QC):
                pool.dma_start(table[ROWS * c:ROWS * (c + 1)], A["rpbw"][:, :, QC - 1 - c:QC - 1 - c + TABW])\
                    .then_inc(S("table_in"), 16)
            pool.wait_ge(S("table_in"), 16 * QC)
            pool.wait_ge(S("mask_in"), 16)
            for a in range(3):
                w0 = 16 + KOFF[a]
                for h in range(NH):
                    src = table[:, ROWS * h:ROWS * (h + 1), w0:w0 + KC].rearrange("p r c -> p c r")
                    dst = bias[:, a, NKEY * h:NKEY * (h + 1)].rearrange("p (c r) -> p c r", r=ROWS)
                    m = mask[:, a, :].unsqueeze(2).to_broadcast([P, KC, ROWS])
                    pool.tensor_tensor(out=dst, in0=src, in1=m, op=ALU.add).then_inc(S("bias_made"), 1)
            pool.wait_ge(S("hT_ready"), KD)
            for j in range(NT):
                src = hT.rearrange("p k (r c) -> p k c r", c=GW)[:, :, QC * j:QC * j + QC, :]
                pool.tensor_copy(hperm[:, j, :].rearrange("p (k c r) -> p k c r", k=KD, r=ROWS), src)\
                    .then_inc(S("hp_made"), 1)
            pool.wait_ge(S("bias_made"), 3 * NH)
            pool.dma_start(cosm, A["cosm"].rearrange("(i p) k -> p i k", p=P)).then_inc(S("four_in"), 16)
            pool.dma_start(sinm, A["sinm"].rearrange("(i p) k -> p i k", p=P)).then_inc(S("four_in"), 16)
            pool.wait_ge(S("filt_made"), nth("filt_made", NT))
            pool.memset(pu[:, :, 0:16], 0.0).then_inc(S("pu_zero"), 1)
            pool.memset(pu[:, :, 16 + L:PADW], 0.0).then_inc(S("pu_zero"), 1)
            pool.wait_ge(S("proj_copied"), 16)
            pool.wait_ge(S("pu_zero"), 2)
            mid = slice(16, 16 + L)
            for m in range(2):
                u = pu[:, m, :]
                chain = [(p2, u, 1, 0, 1), (p4, p2, 2, 1, 1), (p8, p4, 4, 2, 2), (p2, p8, 8, 4, 4)]
                if m == 1:
                    own.wait()
                for n, (dst, src, lo, back, fore) in enumerate(chain[:2 if m == 0 else 4]):
                    hi = PADW - (0, 1, 3, 7)[n]
                    if n == 0:
                        a, b = src[:, 0:PADW - 1], src[:, 1:PADW]
                    else:
                        a, b = src[:, lo - back:hi - back], src[:, lo + fore:hi + fore]
                    own(pool.tensor_tensor(out=dst[:, lo:hi], in0=a, in1=b, op=ALU.add))
                    own.wait()
                halves = [(0, p2), (64, p4)] if m == 0 else [(0, p8), (64, p2)]
                if m == 0:
                    pool.wait_ge(S("invc_in"), 16)
                for p0, s in halves:
                    q = slice(p0, p0 + 64)
                    own(pool.tensor_tensor(out=pooled[q, m, :], in0=s[q, mid], in1=invc[q, m, :], op=ALU.mult))
                own.wait()
                pool.tensor_tensor(out=pooled[:, m, :], in0=pooled[:, m, :], in1=u[:, mid], op=ALU.subtract)\
                    .then_inc(S("pooled_made"), 1)
            pool.wait_ge(S("pooled_made"), 2)
            pool.dma_start(grow, A["g2"].partition_broadcast(P)).then_inc(S("g2_in"), 16)
            pool.wait_ge(S("out1_filled"), 16)
            pool.dma_start(wr, A["w_router"].rearrange("(k p) e -> p k e", p=P)).then_inc(S("wr_in"), 16)
            pool.dma_start(iota, A["iota"].partition_broadcast(P)).then_inc(S("iota_in"), 16)
            pool.wait_ge(S("h2_made"), NT)
            pool.dma_start(grow, A["gfirst"].partition_broadcast(P)).then_inc(S("gfirst_in"), 16)
            pool.wait_ge(S("onehot_made"), NT)
            oh = onehot.rearrange("p i (e s) -> p i e s", s=CAP)
            with pool.Fori(0, NE) as e:
                pool.wait_ge(S("gt_filled"), e + 1)
                for half in range(2):
                    pool.tensor_tensor(out=pg[:, :, 64 * half:64 * half + 64],
                                       in0=oh[:, :, bass.ds(e, 1), :].rearrange("p i e s -> p i (e s)"),
                                       in1=aff[:, :, bass.ds(e, 1)].to_broadcast([P, NT, CAP]), op=ALU.mult)\
                        .then_inc(S("pg_made"), 1)
            second_pool(pool)


        @block.tensor
        def _(pe):
            mm = nc.tensor.matmul
            turn = nc.tensor.transpose
            pe.wait_ge(S("fnet_in"), 16 * 5)
            mm(bank[1][:, :], fw1, pos, start=True, stop=True).then_inc(S("net1_filled"), 1)
            pe.wait_ge(S("const_in"), 16)
            for k in range(KD):
                pe.wait_ge(S("sq1_made"), nth("sq1_made", k + 1))
                mm(bank[0][:, :], ones, hyt[:, k % 2, :], start=k == 0, stop=k == KD - 1).then_inc(S("sq1_summed"), 1)
            pe.wait_ge(S("hT_ready"), KD)

            def proj(u):
                if u % 2 == 0:
                    wait_chunk(pe, u // 2)
                if u >= 4:
                    pe.wait_ge(S("conv_done" if u - 4 < 6 else "proj_copied"), u - 3)
                w = slot(u // 2).rearrange("p (k n) -> p k n", n=256)
                for k in range(KD):
                    last = mm(bank[2 + u % 4][:, :], w[:, k, P * (u % 2):P * (u % 2) + P], hT[:, k, :],
                              start=k == 0, stop=k == KD - 1)
                last.then_inc(S("proj_filled"), 1)

            for u in range(4):
                proj(u)
            pe.wait_ge(S("fh_made"), nth("fh_made", 1))
            mm(bank[1][:, :], fw2, fh, start=True, stop=True).then_inc(S("net2_filled"), 1)
            for u in range(4, 10):
                proj(u)
            pe.wait_ge(S("fh_made"), nth("fh_made", 2))
            for i in range(NT):
                if i >= 2:
                    pe.wait_ge(S("filt_made"), nth("filt_made", i - 1))
                mm(bank[6 + i % 2][:, :], fh[:, P * i:P * i + P], fwo, start=True, stop=True)\
                    .then_inc(S("filt_filled"), 1)
            pe.wait_ge(S("z_made"), nth("z_made", 2))
            for i in range(NT):
                if i >= 2:
                    pe.wait_ge(S("z_copied"), nth("z_copied", i - 1))
                for m in range(2):
                    last = turn(bank[i % 2][:, P * m:P * m + P], hz[:, m, P * i:P * i + P], ident)
                last.then_inc(S("z_turned"), 1)
            for u in range(10, 16):
                proj(u)
            for j in range(NT):
                if j == 0:
                    wait_chunk(pe, 8)
                    wait_chunk(pe, 9)
                pe.wait_ge(S("proj_copied"), 13 + j)
                pe.wait_ge(S("hp_made"), j + 1)
                for half in range(2):
                    w = slot(8 + half).rearrange("p (k n) -> p k n", n=256)
                    for k in range(KD):
                        last = mm(bank[2 + j][:, 256 * half:256 * half + 256], hperm[:, j, P * k:P * k + P], w[:, k, :],
                                  start=k == 0, stop=k == KD - 1)
                last.then_inc(S("proj_filled"), 1)
            pe.wait_ge(S("four_in"), 32)
            pe.wait_ge(S("pq_made"), nth("pq_made", 2))
            pe.wait_ge(S("z_copied"), nth("z_copied", NT))
            for f in range(NT):
                if f >= 2:
                    pe.wait_ge(S("ywf_made"), f - 1)
                b = (6, 0)[f % 2]
                for i in range(NT):
                    mm(bank[b][:, :], cosm[:, i, P * f:P * f + P], zqp[:, i, 0:512], start=i == 0, stop=i == NT - 1)
                for i in range(NT):
                    last = mm(bank[b + 1][:, :], sinm[:, i, P * f:P * f + P], zqp[:, i, 256:768],
                              start=i == 0, stop=i == NT - 1)
                    if f == 0 and i == 0:
                        for n in range(NT):
                            mm(bank[b + 1][0:1, 256:512], col("alt2"), filt[:, n, 256:512], start=False, stop=False)
                last.then_inc(S("four_filled"), 1)
            pe.wait_ge(S("pooled_made"), 2)
            pe.wait_ge(S("pw_in"), 16)
            pe.wait_ge(S("proj_copied"), 20)
            for m in range(2):
                mm(bank[2 + m][:, :], pwbd[:, m, :], pooled[:, m, :], start=True, stop=True)\
                    .then_inc(S("pmix_filled"), 1)
            pe.wait_ge(S("ywf_made"), NT)
            pe.wait_ge(S("sin_turned"), 3)
            for m in range(2):
                for f in range(NT):
                    mm(bank[4 + m][:, :], ywf[:, f, P * m:P * m + P], cosm[:, f, :], start=f == 0, stop=False)
                    last = mm(bank[4 + m][:, :], ywf[:, f, 256 + P * m:256 + P * m + P], sinm[:, f, :],
                              start=False, stop=f == NT - 1)
                last.then_inc(S("yhy_filled"), 1)

            def scores(n):
                j, m = divmod(n, 4)
                if n >= 2:
                    pe.wait_ge(S("s_made"), n - 1)
                for hh in range(2):
                    last = mm(bank[6 + n % 2][:, NKEY * hh:NKEY * hh + NKEY], qz[:, 2 * m + hh, P * j:P * j + P],
                              kT[:, m, ROWS * KSTART[j]:ROWS * KSTART[j] + NKEY], start=True, stop=True)
                last.then_inc(S("s_filled"), 1)

            pe.wait_ge(S("qz_zero"), 1)
            scores(0)
            for n in range(16):
                j, m = divmod(n, 4)
                if n < 15:
                    scores(n + 1)
                pe.wait_ge(S("p_made"), 2 * n + 2)
                if n >= 2:
                    pe.wait_ge(S("pt_copied"), n - 1)
                for a in range(4):
                    last = turn(bank[n % 2][:, P * a:P * a + P], sc[n % 2][:, P * a:P * a + P], ident)
                last.then_inc(S("pt_filled"), 1)
                if n == 0:
                    pe.wait_ge(S("pmix_copied"), nth("pmix_copied", 2))
                    pe.wait_ge(S("vb_in"), 16 * 6)
                if m == 0 and j >= 2:
                    pe.wait_ge(S("o_made"), j - 1)
                pe.wait_ge(S("pt_copied"), n + 1)
                off = ROWS * KSTART[j]
                for hh in range(2):
                    h = 2 * m + hh
                    for a in range(2):
                        v = va[:, off // P + a, :] if off % P == 0 else vb_[:, off // P + a, :]
                        last = mm(bank[2 + j % 2][:, HD * h:HD * h + HD], pt[n % 2][:, P * (2 * hh + a):P * (2 * hh + a) + P],
                                  v[:, HD * h:HD * h + HD], start=a == 0, stop=a == 1)
                last.then_inc(S("pv_filled"), 1)
                if n == 3:
                    pe.wait_ge(S("hsq_made"), nth("hsq_made", 2))
                    for q in range(2):
                        last = mm(bank[4][:, :], ones, hyt[:, q, :], start=q == 0, stop=q == 1)
                    last.then_inc(S("hsum_filled"), 1)
                    pe.wait_ge(S("psq_made"), nth("psq_made", 2))
                    for q in range(2):
                        last = mm(bank[5][:, :], ones, ywf.rearrange("p a b -> p (a b)")[:, 512 * q:512 * q + 512],
                                  start=q == 0, stop=q == 1)
                    last.then_inc(S("hsum_filled"), 1)
            pe.wait_ge(S("on_made"), NT)
            for m in range(4):
                if m >= 2:
                    pe.wait_ge(S("ot_copied"), nth("ot_copied", m - 1))
                for j in range(NT):
                    last = turn(bank[6 + m % 2][:, P * j:P * j + P], ona[:, j, P * m:P * m + P], ident)
                last.then_inc(S("ot_filled"), 1)
            pe.wait_ge(S("ot_copied"), nth("ot_copied", 4))
            pe.wait_ge(S("mix_made"), 4)
            for c in range(N_OUT1):
                wait_chunk(pe, C_OUT1 + c)
                w = slot(C_OUT1 + c).rearrange("p (k n) -> p k n", n=256)
                for i in range(NT):
                    u = 4 * c + i
                    if u >= 4:
                        pe.wait_ge(S("out1_added"), u - 3)
                    for k in range(KD):
                        last = mm(bank[i][:, 0:256], mixT[:, k, P * i:P * i + P], w[:, k, :], start=k == 0, stop=k == KD - 1)
                    last.then_inc(S("out1_filled"), 1)
            pe.wait_ge(S("h2_made"), NT)
            for k in range(KD):
                if k >= 2:
                    pe.wait_ge(S("h2t_a" if k % 2 == 0 else "h2t_v"), k // 2)
                for i in range(NT):
                    last = turn(bank[4 + k % 2][:, P * i:P * i + P], h2[:, i, P * k:P * k + P], ident)
                last.then_inc(S("h2_turned"), 1)
            pe.wait_ge(S("h2t_a"), 4)
            pe.wait_ge(S("h2t_v"), 4)
            pe.wait_ge(S("wr_in"), 16)
            for i in range(NT):
                for k in range(KD):
                    last = mm(bank[6][:, NE * i:NE * i + NE], hT[:, k, P * i:P * i + P], wr[:, k, :],
                              start=k == 0, stop=k == KD - 1)
            last.then_inc(S("lg_filled"), 1)
            pe.wait_ge(S("aff_made"), nth("aff_made", 1))
            for i in range(NT):
                last = turn(bank[7][0:NE, P * i:P * i + P], aff[:, i, :], ident)
            last.then_inc(S("aff_turned"), 1)
            pe.wait_ge(S("rank_made"), nth("rank_made", 1))
            for i in range(NT):
                last = turn(bank[6][:, NE * i:NE * i + NE], rank[0:NE, P * i:P * i + P], ident[0:NE, 0:NE])
            last.then_inc(S("rank_turned"), 1)

            pe.wait_ge(S("onehot_made"), NT)
            pe.sem_inc(S("hid_turned"), 2)
            for name in ("gt_filled", "gt_made", "y_copied", "sc_filled", "ab_filled"):
                pe.sem_inc(S(name), 1)
            with pe.Fori(0, NE) as e:
                pe.wait_ge(S("gt_made"), e + 1)
                for k in range(KD):
                    for i in range(NT):
                        last = mm(bank[3][:, CAP * k:CAP * k + CAP], h2[:, i, P * k:P * k + P],
                                  onehot[:, i, bass.ds(e * CAP, CAP)], start=i == 0, stop=i == NT - 1)
                last.then_inc(S("xs_filled"), 1)

                def gate_up(c):
                    ab = bank[c % 2]
                    pe.wait_ge(S("h_made"), e * NFC + (c + 1))
                    for which in range(2):
                        s = 3 * (c % 2) + which
                        pe.wait_ge(S(f"ew_in{s}"), e * 32 + 16 * (c // 2 + 1))
                        w = mslot[s].rearrange("p (k n) -> p k n", n=FC)
                        for k in range(KD):
                            for half in range(2):
                                last = mm(ab[64 * half:64 * half + 64, 256 * which:256 * which + 256], xsT[:, k, :],
                                          w[:, k, 256 * half:256 * half + 256], start=k == 0, stop=k == KD - 1)
                    last.then_inc(S("ab_filled"), 1)

                def down(c):
                    pe.wait_ge(S("h_made"), e * NFC + (c + 3))
                    for t in range(2):
                        last = turn(bank[2][:, 256 * (c % 2) + P * t:256 * (c % 2) + P * t + P],
                                    hid[c % 2][:, P * t:P * t + P], ident)
                    last.then_inc(S("hid_turned"), 1)
                    s = 3 * (c % 2) + 2
                    pe.wait_ge(S(f"ew_in{s}"), e * 32 + 16 * (c // 2 + 1))
                    pe.wait_ge(S("hidT_made"), e * NFC + (c + 1))
                    w = mslot[s].rearrange("p (k n) -> p k n", n=D)
                    for t in range(2):
                        for n in range(2):
                            for half in range(2):
                                last = mm(bank[4 + n][64 * half:64 * half + 64, :],
                                          hidT[c % 2][:, P * t + 64 * half:P * t + 64 * half + 64],
                                          w[:, 2 * half + t, 512 * n:512 * n + 512],
                                          start=(c == 0 and t == 0), stop=(c == NFC - 1 and t == 1))
                    last.then_inc(S("y_part"), 1)

                pe.wait_ge(S("xs_made"), e + 1)
                pe.wait_ge(S("pg_made"), e * 2 + 2)
                for i in range(NT):
                    last = turn(bank[3][:, P * i:P * i + P], pg[:, i, :], ident)
                last.then_inc(S("gt_filled"), 1)
                gate_up(0)
                gate_up(1)
                pe.wait_ge(S("y_copied"), e * 2 + 1)
                down(0)
                gate_up(2)
                down(1)
                gate_up(3)
                down(2)
                down(3)
                pe.wait_ge(S("gt_made"), e + 2)
                pe.wait_ge(S("y_copied"), e * 2 + 3)
                for u in range(8):
                    i, n = u // 2, u % 2
                    pe.wait_ge(S("sc_added"), e * 8 + (u + 1))
                    mm(bank[6 + u % 2][:, :], gt[:, P * i:P * i + P], ysb[:, 512 * n:512 * n + 512], start=True, stop=True)\
                        .then_inc(S("sc_filled"), 1)
            second_pe(pe, mm, turn)

        def two_pi_fold(dve, own, src, bcol, n):
            own(dve.tensor_scalar(fa, src, col(bcol), col("freq"), ALU.add, ALU.mult))
            own.wait()
            own(dve.tensor_scalar(fk, fa, 1.0 / (2 * np.pi), MAGIC, ALU.mult, ALU.add))
            own.wait()
            own(dve.tensor_scalar(fk, fk, MAGIC, None, ALU.subtract))
            own.wait()
            own(dve.scalar_tensor_tensor(out=fa, in0=fk, scalar=-TWO_PI_HI, in1=fa, op0=ALU.mult, op1=ALU.add))
            own.wait()
            own(dve.scalar_tensor_tensor(out=fa, in0=fk, scalar=-TWO_PI_LO, in1=fa, op0=ALU.mult, op1=ALU.add))
            own.wait()
            dve.tensor_scalar(fa, fa, PI, -PI, ALU.min, ALU.max).then_inc(S("angle_made"), 1)

        @block.vector
        def _(dve):
            own = Own(dve, "dve_own")
            stt = dve.scalar_tensor_tensor
            tt = dve.tensor_tensor
            ts = dve.tensor_scalar
            dve.wait_ge(S("xT_in"), 16)
            for k in range(KD):
                if k >= 2:
                    dve.wait_ge(S("sq1_summed"), k - 1)
                tt(out=hyt[:, k % 2, :], in0=hT[:, k, :], in1=hT[:, k, :], op=ALU.mult).then_inc(S("sq1_made"), 1)
            dve.wait_ge(S("sq1_summed"), KD)
            ts(hyt[:, 0, :], bank[0][:, :], 1.0 / D, EPS, ALU.mult, ALU.add).then_inc(S("var1_made"), 1)
            dve.wait_ge(S("net1_filled"), nth("net1_filled", 1))
            dve.wait_ge(S("cols_in"), 16)
            two_pi_fold(dve, own, bank[1][:, :], "fb1", 1)
            dve.wait_ge(S("sd1_made"), nth("sd1_made", 1))
            own(dve.reciprocal(hyt[:, 1, :], hyt[:, 0, :]))
            own.wait()
            for k in range(KD):
                stt(out=hT[:, k, :], in0=hT[:, k, :], scalar=col("norm1", k), in1=hyt[:, 1, :], op0=ALU.mult, op1=ALU.mult)\
                    .then_inc(S("hT_ready"), 1)
            for u in range(6):
                dve.wait_ge(S("proj_copied"), u + 1)
                ps = bank[2 + u % 4]
                own(stt(out=hyu[:, u, 1:L], in0=ps[:, 0:L - 1], scalar=col("hw0", u), in1=hyu[:, u, 1:L],
                        op0=ALU.mult, op1=ALU.add))
                own.wait()
                stt(out=hyu[:, u, 0:L - 1], in0=ps[:, 1:L], scalar=col("hw2", u), in1=hyu[:, u, 0:L - 1],
                    op0=ALU.mult, op1=ALU.add).then_inc(S("conv_done"), 1)
            dve.wait_ge(S("net2_filled"), nth("net2_filled", 1))
            dve.wait_ge(S("fh_made"), nth("fh_made", 1))
            two_pi_fold(dve, own, bank[1][:, :], "fb2", 2)
            dve.wait_ge(S("conv_done"), 6)
            for m in range(2):
                tt(out=hz[:, m, :], in0=hyu[:, 4 + m, :], in1=hyu[:, 2 + m, :], op=ALU.mult).then_inc(S("z_made"), 1)
            dve.wait_ge(S("decay_made"), nth("decay_made", NT))
            for i in range(NT):
                dve.wait_ge(S("filt_filled"), nth("filt_filled", i + 1))
                own(tt(out=filt[:, i, 0:256], in0=bank[6 + i % 2][:, 0:256], in1=decay[:, i, :], op=ALU.mult))
                tt(out=filt[:, i, 256:512], in0=bank[6 + i % 2][:, 256:512], in1=decay[:, i, :], op=ALU.mult)\
                    .then_inc(S("filt_made"), 1)
            dve.wait_ge(S("filt_made"), nth("filt_made", NT))
            own(dve.memset(filt[0:1, 0, 256:512], 0.0))
            own.wait()
            tt(out=zqp[:, :, 0:256], in0=filt[:, :, 0:256], in1=filt[:, :, 256:512], op=ALU.add).then_inc(S("pq_made"), 1)
            tt(out=zqp[:, :, 512:768], in0=filt[:, :, 0:256], in1=filt[:, :, 256:512], op=ALU.subtract)\
                .then_inc(S("pq_made"), 1)
            for f in range(NT):
                b = (6, 0)[f % 2]
                dve.wait_ge(S("rs_made"), nth("rs_made", 2 * f + 2))
                zr, zs = bank[b][:, 256:512], bank[b + 1][:, 0:256]
                for o, x, y in ((0, zr, 0), (1, zs, 256), (2, zr, 256), (3, zs, 0)):
                    own(tt(out=pr[o], in0=x, in1=rs[:, y:y + 256], op=ALU.mult))
                own.wait()
                n = own(tt(out=ywf[:, f, 0:256], in0=pr[0], in1=pr[1], op=ALU.subtract))
                if f == 0:
                    own.wait()
                    own(dve.tensor_copy(ywf[0:1, 0, 0:256], pr[0][0:1, :]))
                    own(tt(out=ywf[:, f, 256:512], in0=pr[2], in1=pr[3], op=ALU.add))
                    own.wait()
                    dve.tensor_copy(ywf[0:1, 0, 256:512], pr[1][0:1, :]).then_inc(S("ywf_made"), 1)
                else:
                    tt(out=ywf[:, f, 256:512], in0=pr[2], in1=pr[3], op=ALU.add).then_inc(S("ywf_made"), 1)
                dve.wait_ge(S("ywf_made"), f + 1)
            dve.wait_ge(S("four_filled"), nth("four_filled", NT))
            dve.memset(sinm[:, :, 0:1], 0.0).then_inc(S("sin_turned"), 1)
            dve.wait_ge(S("sin_turned"), 1)
            alt = sinm[0:1, 0, :].rearrange("p (n a) -> p n a", a=2)
            dve.memset(alt[:, :, 0], 1.0).then_inc(S("sin_turned"), 1)
            dve.memset(alt[:, :, 1], -1.0).then_inc(S("sin_turned"), 1)
            for m in range(2):
                dve.wait_ge(S("yhy_filled"), nth("yhy_filled", m + 1))
                own(stt(out=hz[:, m, :], in0=hz[:, m, :], scalar=col("skip", m), in1=bank[4 + m][:, :],
                        op0=ALU.mult, op1=ALU.add))
                own.wait()
                own(tt(out=hyu[:, m, :], in0=hz[:, m, :], in1=hyu[:, m, :], op=ALU.mult))
                own.wait()
                tt(out=hyt[:, m, :], in0=hyu[:, m, :], in1=hyu[:, m, :], op=ALU.mult).then_inc(S("hsq_made"), 1)

            smax = stat[:, 100:132]
            sneg = stat[:, 132:164]
            lsum = stat[:, 164:196]
            linv = stat[:, 196:228]

            def attend(n):
                j, m = divmod(n, 4)
                dve.wait_ge(S("s_filled"), n + 1)
                if n >= 2:
                    dve.wait_ge(S("pt_filled"), n - 1)
                tt(out=sc[n % 2], in0=bank[6 + n % 2][:, :], in1=bias[:, KIND[j], 512 * m:512 * m + 512], op=ALU.add)\
                    .then_inc(S("s_made"), 1)
                dve.wait_ge(S("s_made"), n + 1)
                own(dve.tensor_reduce(out=smax[:, 2 * n:2 * n + 2], in_=sc[n % 2].rearrange("p (h k) -> p h k", h=2),
                                      axis=AX.X, op=ALU.max))
                own.wait()
                ts(sneg[:, 2 * n:2 * n + 2], smax[:, 2 * n:2 * n + 2], -1.0, None, ALU.mult).then_inc(S("neg_made"), 1)

            def weigh(j):
                dve.wait_ge(S("p_made"), 8 * (j + 1))
                own(dve.reciprocal(linv[:, 8 * j:8 * j + 8], lsum[:, 8 * j:8 * j + 8]))
                own.wait()
                dve.wait_ge(S("pv_filled"), 4 * (j + 1))
                tt(out=ona[:, j, :].rearrange("p (h d) -> p h d", d=HD),
                   in0=bank[2 + j % 2][:, :].rearrange("p (h d) -> p h d", d=HD),
                   in1=linv[:, 8 * j:8 * j + 8].unsqueeze(2).to_broadcast([P, NH, HD]), op=ALU.mult)\
                    .then_inc(S("o_made"), 1)

            dve.wait_ge(S("bias_made"), 3 * NH)
            dve.wait_ge(S("four_filled"), nth("four_filled", NT))
            hvar = [sc, None]
            for n in range(16):
                attend(n)
                if n % 4 == 1 and n > 4:
                    weigh(n // 4 - 1)
                if n == 6:
                    dve.wait_ge(S("hsum_filled"), nth("hsum_filled", 2))
                    for q in range(2):
                        ts(filt[:, 2 + q, :], bank[4 + q][:, :], 1.0 / 256, EPS, ALU.mult, ALU.add).then_inc(S("hvar_made"), 1)
                if n == 9:
                    dve.wait_ge(S("hsd_made"), nth("hsd_made", 2))
                    for q in range(2):
                        own(dve.reciprocal(hyt[:, q, :], filt[:, 2 + q, :]))
                    own.wait()
                    for q in range(2):
                        for m in range(2):
                            src = hyu[:, m, :] if q == 0 else pooled[:, m, :]
                            at = m if q == 0 else 6 + m
                            stt(out=mixT[:, at, :], in0=src, scalar=col("mixg", at), in1=hyt[:, q, :],
                                op0=ALU.mult, op1=ALU.mult).then_inc(S("mix_made"), 1)
            weigh(3)
            nss = stat[:, 228:232]
            nrs = stat[:, 232:236]
            dve.wait_ge(S("nsq_made"), nth("nsq_made", NT))
            own(ts(nss, nss, 1.0 / NAW, EPS, ALU.mult, ALU.add))
            own.wait()
            dve.engine_nop().then_inc(S("nvar_made"), 1)
            dve.wait_ge(S("nsd_made"), nth("nsd_made", 1))
            own(dve.reciprocal(nrs, nss))
            own.wait()
            for j in range(NT):
                ts(ona[:, j, :], ona[:, j, :], nrs[:, j:j + 1], None, ALU.mult).then_inc(S("on_made"), 1)
            dve.wait_ge(S("x_in"), 16)
            for c in range(N_OUT1):
                for i in range(NT):
                    u = 4 * c + i
                    dve.wait_ge(S("out1_filled"), u + 1)
                    xs = x_res[:, i, 256 * c:256 * c + 256]
                    tt(out=xs, in0=xs, in1=bank[i][:, 0:256], op=ALU.add).then_inc(S("out1_added"), 1)
            v2 = stat[:, 236:240]
            r2 = stat[:, 240:244]
            dve.wait_ge(S("n2sq_made"), nth("n2sq_made", NT))
            ts(v2, v2, 1.0 / D, EPS, ALU.mult, ALU.add).then_inc(S("n2var_made"), 1)
            dve.wait_ge(S("n2sd_made"), nth("n2sd_made", 1))
            own(dve.reciprocal(r2, v2))
            own.wait()
            dve.wait_ge(S("g2_in"), 16)
            for i in range(NT):
                stt(out=h2[:, i, :], in0=x_res[:, i, :], scalar=r2[:, i:i + 1], in1=grow, op0=ALU.mult, op1=ALU.mult)\
                    .then_inc(S("h2_made"), 1)
            for k in range(1, KD, 2):
                dve.wait_ge(S("h2_turned"), nth("h2_turned", k + 1))
                dve.tensor_copy(hT[:, k, :], bank[5][:, :]).then_inc(S("h2t_v"), 1)
            rmx = stat[:, 244:248]
            dve.wait_ge(S("lg_filled"), nth("lg_filled", 1))
            l3 = bank[6][:, 0:NT * NE].rearrange("p (i e) -> p i e", e=NE)
            own(dve.tensor_reduce(out=rmx, in_=l3, axis=AX.X, op=ALU.max))
            own.wait()
            tt(out=lg, in0=l3, in1=rmx.unsqueeze(2).to_broadcast([P, NT, NE]), op=ALU.subtract).then_inc(S("lg_made"), 1)
            dve.wait_ge(S("lg_exp"), nth("lg_exp", 1))
            own(dve.tensor_reduce(out=rmx, in_=lg, axis=AX.X, op=ALU.add))
            own.wait()
            own(dve.reciprocal(rmx, rmx))
            own.wait()
            tt(out=aff, in0=lg, in1=rmx.unsqueeze(2).to_broadcast([P, NT, NE]), op=ALU.mult).then_inc(S("aff_made"), 1)
            dve.wait_ge(S("aff_turned"), nth("aff_turned", 1))
            w16 = work[0:NE, :]
            top = stat[0:NE, 248:256]
            own(dve.tensor_copy(w16, bank[7][0:NE, :]))
            own.wait()
            for _ in range(CAP // 8):
                own(dve.max(out=top, in_=w16))
                own.wait()
                own(dve.match_replace(out=w16, in_to_replace=top, in_values=w16, imm_value=-1.0))
                own.wait()
            own(ts(sel[0:NE, :], w16, 0.0, None, ALU.is_lt))
            own.wait()
            own(dve.tensor_tensor_scan(out=rank[0:NE, :], data0=sel[0:NE, :], data1=sel[0:NE, :], initial=0.0,
                                       op0=ALU.add, op1=ALU.bypass))
            own.wait()
            own(tt(out=rank[0:NE, :], in0=rank[0:NE, :], in1=sel[0:NE, :], op=ALU.mult))
            own.wait()
            ts(rank[0:NE, :], rank[0:NE, :], -1.0, None, ALU.add).then_inc(S("rank_made"), 1)
            dve.wait_ge(S("rank_turned"), nth("rank_turned", 1))
            own(dve.tensor_copy(rankc, l3))
            own.wait()
            dve.wait_ge(S("iota_in"), 16)
            for i in range(NT):
                tt(out=onehot[:, i, :].rearrange("p (e s) -> p e s", s=CAP),
                   in0=iota.unsqueeze(1).to_broadcast([P, NE, CAP]),
                   in1=rankc[:, i, :].unsqueeze(2).to_broadcast([P, NE, CAP]), op=ALU.is_equal)\
                    .then_inc(S("onehot_made"), 1)
            dve.sem_inc(S("h_made"), 2)
            dve.sem_inc(S("sc_added"), 2)
            with dve.Fori(0, NE) as e:
                for c in range(NFC):
                    dve.wait_ge(S("silu_made"), e * NFC + (c + 1))
                    dve.wait_ge(S("hid_turned"), e * NFC + (c + 1))
                    tt(out=hid[c % 2], in0=silu[c % 2], in1=bank[c % 2][:, 256:512], op=ALU.mult).then_inc(S("h_made"), 1)
                dve.wait_ge(S("y_part"), e * NFC + NFC)
                dve.wait_ge(S("sc_filled"), e * 8 + 1)
                dve.tensor_copy(ysb[:, 512:1024], bank[5][:, :]).then_inc(S("y_copied"), 1)
                for u in range(8):
                    i, n = u // 2, u % 2
                    dve.wait_ge(S("sc_filled"), e * 8 + (u + 2))
                    xs = x_res[:, i, 512 * n:512 * n + 512]
                    tt(out=xs, in0=xs, in1=bank[6 + u % 2][:, :], op=ALU.add).then_inc(S("sc_added"), 1)
            second_dve(dve, own)

        @block.scalar
        def _(act):
            own = Own(act, "act_own")
            fn = act.activation
            act.wait_ge(S("fnet_in"), 16 * 5)
            act.wait_ge(S("cols_in"), 16)
            for i in (3, 2, 1, 0):
                fn(decay[:, i, :], decay[:, 0, :], ACT.Exp, scale=col("negt", i)).then_inc(S("decay_made"), 1)
            act.wait_ge(S("var1_made"), nth("var1_made", 1))
            fn(hyt[:, 0, :], hyt[:, 0, :], ACT.Sqrt).then_inc(S("sd1_made"), 1)
            act.wait_ge(S("angle_made"), 1)
            fn(fh, fa, ACT.Sin).then_inc(S("fh_made"), 1)

            def proj_out(u):
                act.wait_ge(S("proj_filled"), u + 1)
                if u < 16:
                    ps = bank[2 + u % 4][:, :]
                grid = ps.rearrange("p (r c) -> p r c", c=GW) if u < 16 else None
                if u < 6:
                    last = fn(hyu[:, u, :], ps, ACT.Identity, bias=col("hb", u), scale=col("hw1", u))
                elif u < 10:
                    m = u - 6
                    if m == 0:
                        act.wait_ge(S("qz_zero"), 1)
                    for hh in range(2):
                        q = slice(64 * hh, 64 * hh + 64)
                        last = fn(qz[q, 2 * m + hh, :].rearrange("p (c r) -> p r c", r=ROWS), grid[q], ACT.Copy,
                                  scale=HD ** -0.5)
                        if hh == 0:
                            own(last)
                elif u < 14:
                    last = fn(kT[:, u - 10, :].rearrange("p (c r) -> p r c", r=ROWS), grid, ACT.Copy)
                elif u < 16:
                    act.wait_ge(S("filt_made"), nth("filt_made", NT))
                    last = fn(pu[:, u - 14, 16:16 + L], ps, ACT.Copy)
                else:
                    last = fn(va[:, u - 16, :], bank[2 + u - 16][:, :], ACT.Copy)
                last.then_inc(S("proj_copied"), 1)

            for u in range(6):
                proj_out(u)
            act.wait_ge(S("angle_made"), 2)
            act.wait_ge(S("net2_filled"), nth("net2_filled", 1))
            fn(fh, fa, ACT.Sin).then_inc(S("fh_made"), 1)
            for u in range(6, 10):
                proj_out(u)
            for i in range(NT):
                act.wait_ge(S("z_turned"), nth("z_turned", i + 1))
                fn(zqp[:, i, 256:512], bank[i % 2][:, 0:256], ACT.Copy).then_inc(S("z_copied"), 1)
            for u in range(10, 20):
                proj_out(u)
            for f in range(NT):
                b = (6, 0)[f % 2]
                act.wait_ge(S("four_filled"), nth("four_filled", f + 1))
                act.wait_ge(S("ywf_made"), f)
                fn(rs[:, 0:256], bank[b][:, 0:256], ACT.Copy, scale=col("wk", f)).then_inc(S("rs_made"), 1)
                fn(rs[:, 256:512], bank[b + 1][:, 256:512], ACT.Copy, scale=col("wk", f)).then_inc(S("rs_made"), 1)
            act.wait_ge(S("pmix_filled"), nth("pmix_filled", 2))
            for m in range(2):
                fn(pooled[:, m, :], bank[2 + m][:, :], ACT.Copy, scale=col("pscale", m)).then_inc(S("pmix_copied"), 1)
            act.wait_ge(S("yhy_filled"), nth("yhy_filled", 2))
            act.wait_ge(S("pmix_copied"), nth("pmix_copied", 2))
            for m in range(2):
                fn(ywf[:, m, :], pooled[:, m, :], ACT.Square).then_inc(S("psq_made"), 1)
            lsum = stat[:, 164:196]
            sneg = stat[:, 132:164]

            def exps(n):
                act.wait_ge(S("neg_made"), n + 1)
                for hh in range(2):
                    at = 2 * n + hh
                    s = sc[n % 2][:, NKEY * hh:NKEY * hh + NKEY]
                    fn(s, s, ACT.Exp, bias=sneg[:, at:at + 1], accum_out=lsum[:, at:at + 1]).then_inc(S("p_made"), 1)

            exps(0)
            for n in range(16):
                if n < 15:
                    exps(n + 1)
                act.wait_ge(S("pt_filled"), n + 1)
                if n >= 2:
                    act.wait_ge(S("pv_filled"), n - 1)
                fn(pt[n % 2], bank[n % 2][:, :], ACT.Copy).then_inc(S("pt_copied"), 1)
                if n == 7:
                    act.wait_ge(S("hvar_made"), nth("hvar_made", 2))
                    for q in range(2):
                        fn(filt[:, 2 + q, :], filt[:, 2 + q, :], ACT.Sqrt).then_inc(S("hsd_made"), 1)
            nss = stat[:, 228:232]
            for j in range(NT):
                act.wait_ge(S("o_made"), j + 1)
                if j:
                    act.wait_ge(S("nsq_made"), nth("nsq_made", j))
                fn(filt[:, 0, :], ona[:, j, :], ACT.Square, accum_out=nss[:, j:j + 1]).then_inc(S("nsq_made"), 1)
            act.wait_ge(S("nvar_made"), nth("nvar_made", 1))
            fn(nss, nss, ACT.Sqrt).then_inc(S("nsd_made"), 1)
            for m in range(4):
                act.wait_ge(S("ot_filled"), nth("ot_filled", m + 1))
                fn(mixT[:, 2 + m, :].rearrange("p (r c) -> p c r", c=GW),
                   bank[6 + m % 2][:, :].rearrange("p (c r) -> p c r", r=ROWS), ACT.Copy, scale=col("mixg", 2 + m))\
                    .then_inc(S("ot_copied"), 1)
            v2 = stat[:, 236:240]
            for i in range(NT):
                act.wait_ge(S("out1_added"), 13 + i)
                if i:
                    act.wait_ge(S("n2sq_made"), nth("n2sq_made", i))
                fn(sqd, x_res[:, i, :], ACT.Square, accum_out=v2[:, i:i + 1]).then_inc(S("n2sq_made"), 1)
            act.wait_ge(S("n2var_made"), nth("n2var_made", 1))
            fn(v2, v2, ACT.Sqrt).then_inc(S("n2sd_made"), 1)
            for k in range(0, KD, 2):
                act.wait_ge(S("h2_turned"), nth("h2_turned", k + 1))
                fn(hT[:, k, :], bank[4][:, :], ACT.Copy).then_inc(S("h2t_a"), 1)
            act.wait_ge(S("lg_made"), nth("lg_made", 1))
            fn(lg, lg, ACT.Exp).then_inc(S("lg_exp"), 1)
            with act.Fori(0, NE) as e:
                act.wait_ge(S("xs_filled"), e + 1)
                act.wait_ge(S("ab_filled"), e * NFC + 1)
                fn(xsT.rearrange("p k s -> p (k s)"), bank[3][:, :], ACT.Copy).then_inc(S("xs_made"), 1)
                act.wait_ge(S("gt_filled"), e + 2)
                act.wait_ge(S("sc_filled"), e * 8 + 1)
                fn(gt, bank[3][:, :], ACT.Copy).then_inc(S("gt_made"), 1)

                def silu_of(c):
                    act.wait_ge(S("ab_filled"), e * NFC + (c + 2))
                    act.wait_ge(S("h_made"), e * NFC + (c + 1))
                    fn(silu[c % 2], bank[c % 2][:, 0:256], ACT.Silu).then_inc(S("silu_made"), 1)

                def turned(c):
                    act.wait_ge(S("hid_turned"), e * NFC + (c + 3))
                    fn(hidT[c % 2], bank[2][:, 256 * (c % 2):256 * (c % 2) + 256], ACT.Copy).then_inc(S("hidT_made"), 1)

                silu_of(0)
                silu_of(1)
                turned(0)
                silu_of(2)
                turned(1)
                silu_of(3)
                turned(2)
                turned(3)
                act.wait_ge(S("y_part"), e * NFC + NFC)
                fn(ysb[:, 0:512], bank[4][:, :], ACT.Copy).then_inc(S("y_copied"), 1)
            second_act(act, own)


def tables():
    f = np.float32
    k = np.arange(L)
    ang = 2 * np.pi * ((k[:, None] * k[None, :]) % (2 * L)) / (2 * L)
    cosm, sinm = np.cos(ang).astype(f), np.sin(ang).astype(f)
    sinm[:, 0] = (-1.0) ** k
    consts = np.concatenate([np.eye(P), np.ones((P, P)), np.triu(np.ones((P, P))), np.triu(np.ones((P, P)), 1)], 1)
    inv = np.zeros((P, 2, L), f)
    for g, w in enumerate((2, 4, 8, 16)):
        cnt = np.clip(k + w // 2, 0, L) - np.clip(k - w // 2, 0, L)
        inv[64 * (g % 2):64 * (g % 2) + 64, g // 2] = (1.0 / cnt).astype(f)
    mask = np.zeros((P, 3, KC), f)
    for a, j in ((0, 0), (1, 1), (2, 3)):
        c = QC * j + np.arange(QC)
        start = np.clip(c - KWIN // 2, 0, GW - KWIN)
        key = KSTART[j] + np.arange(KC)
        ok = (key[None] >= start[:, None]) & (key[None] < start[:, None] + KWIN)
        mask[:, a] = np.repeat(np.where(ok, 0.0, -1e30), ROWS, axis=0)
    t = np.linspace(0.0, 1.0, L, dtype=f)[:, None]
    a = (2.0 * np.pi * np.arange(L, dtype=f)[:, None] / L).astype(f)
    fr = np.linspace(1e-4, 15, 16, dtype=f)[None]
    pos = np.zeros((P, L), f)
    pos[:33] = np.concatenate([t, np.cos(fr * a), -np.sin(fr * a)], -1).T
    deltas = np.abs(np.linspace(np.log(1e-2) / 0.3, np.log(1e-2) / 1.5, HY, dtype=f))
    wk = np.full(L, 2.0 / (2 * L), f)
    wk[0] = 1.0 / (2 * L)
    b = np.arange(P)
    blk = np.zeros((P, 7, P), f)
    for lv in range(7):
        w = 2 << lv
        blk[:, lv] = (b[:, None] // w == b[None] // w) & (b[:, None] % w < w // 2) & (b[None] % w >= w // 2)
    return dict(blk=blk, cosm=cosm, sinm=sinm, consts=consts.astype(f), invc=inv.reshape(P, 2 * L), mask=mask, pos=pos,
                deltas=deltas, wk=wk, negt=-t[:, 0], iota=np.arange(CAP, dtype=f))


def lay_out(a):
    f = np.float32
    c = tables()
    a = {k: np.asarray(v) for k, v in a.items()}

    def chunks(w, n):
        kk, nn = w.shape
        r = w.reshape(kk // P, P, nn // n, n).transpose(2, 1, 0, 3).reshape(nn // n, P, -1)
        return r

    w = a["w_in"][0]
    hy, q, k, v, pu = np.split(w, [768, 1280, 1792, 2304], axis=1)
    parts = [chunks(np.concatenate([hy, q, k, pu, v], 1), 256), chunks(a["w_out"][0], 256)]
    w2 = a["w_in_2"][0]
    at = np.cumsum([0, 512, 512, 512, 512, 4, 4, 256, 256, 512, 512, 4, 4, 1024, 1024])
    (gq, gk, gv, gz, gb, ga, mq, mk, mv, mo, mi, mf, sa, sb) = [w2[:, at[i]:at[i + 1]] for i in range(14)]
    parts.append(chunks(np.concatenate([gq, gk, gv, mq, mk, gz, mv, mo], 1), 256))
    for br, gt in ((a["w_branch_a_2"][0], sa), (a["w_branch_b_2"][0], sb)):
        b, g = chunks(br, 512), chunks(gt, 256)
        parts.append(np.concatenate([b[0:1], g[0:2], b[1:2], g[2:4]]))
    parts.append(chunks(a["w_out_2"][0], 256))
    up = np.stack([chunks(a["w1_2"][0], 256), chunks(a["w3_2"][0], 256)], 1)
    parts.append(up.reshape(-1, P, WCH))
    down = np.pad(a["w2_2"][0], ((0, 2 * P), (0, 0)))
    for n in range(2):
        d = down[:, 512 * n:512 * n + 512].reshape(6, 4, P, 512).transpose(0, 2, 1, 3).reshape(6, P, WCH)
        parts.append(d)
    parts.append(chunks(a["w_ple_2"][0], 1024))
    parts.append(chunks(a["w_ple_gate_2"][0], 256))
    wpack = np.concatenate(parts)
    assert wpack.shape == (N_CHUNKS, P, WCH), wpack.shape

    cols = np.zeros((P, N_COLS), f)

    def put(name, v):
        v = np.asarray(v).reshape(-1)
        if v.size < P:
            v = np.pad(v, (0, P - v.size))
        n = v.size // P
        cols[:, COLS[name]:COLS[name] + n] = v.reshape(n, P).T

    put("norm1", a["norm1_g"])
    for i in range(3):
        put(f"hw{i}", a["hy_short_w"][0, i])
    put("hb", a["hy_short_b"])
    put("skip", a["hy_skip"])
    put("pscale", a["pool_scale"])
    put("mixg", a["mix_norm_g"])
    put("gmix2", a["g_mix_2"])
    for i in range(4):
        put(f"cw{i}", a["conv_w_2"][0, i])
    put("gffn", a["g_ffn_2"])
    put("gple", a["g_ple_2"])
    put("fb1", a["hy_f_b1"])
    put("fb2", a["hy_f_b2"])
    put("freq", a["hy_f_freq"])
    put("wk", c["wk"])
    put("negt", c["negt"])
    put("alt2", 2.0 * (-1.0) ** np.arange(P))
    rows = np.concatenate([a["gdn_norm_2"][0], a["ml_norm_2"][0].reshape(-1), a["a_log_2"][0], a["dt_bias_2"][0],
                           a["ml_i_bias_2"][0], a["ml_f_bias_2"][0]])
    pw = np.zeros((2, P, P), f)
    for g in range(4):
        s = slice(64 * (g % 2), 64 * (g % 2) + 64)
        pw[g // 2, s, s] = a["pool_w"][0, g]
    pad2 = lambda v, r, q: np.pad(v, ((0, r - v.shape[0]), (0, q - v.shape[1])))
    pad = np.pad(a["na_rpb"][0], ((0, 0), (0, 0), (16, 17)))
    d = dict(
        x=a["x"][0], xT=a["x"][0].T, wpack=wpack, cols=cols, rows=rows, pwbd=pw,
        w_gate=a["w_gate"][0], w_up=a["w_up"][0], w_down=a["w_down"][0], w_router=a["w_router"][0],
        w_gates=np.concatenate([gb, ga, mi, mf], 1), pT=a["p_2"][0, 0].T,
        g2=a["norm2_g"][0], gfin=a["g_final_2"],
        fw1=pad2(a["hy_f_w1"][0], P, P), fw2=pad2(a["hy_f_w2"][0], P, P), fwo=pad2(a["hy_f_wout"][0], P, 512),
        rpbw=np.stack([pad[:, ROWS - 1 - r:2 * ROWS - 1 - r].reshape(NH * ROWS, 64) for r in range(ROWS)]),
        gfirst=a["final_g"],
    )
    for n in ("cosm", "sinm", "consts", "invc", "mask", "pos", "deltas", "iota", "blk"):
        d[n] = c[n]
    return {k: np.ascontiguousarray(v) for k, v in d.items()}


def kernel(**inputs):
    import concourse.bacc as bacc
    from concourse.bass_utils import run_bass_kernel_spmd

    nc = bacc.Bacc("TRN2", target_bir_lowering=False, num_devices=1)
    arrays, args = {}, {}
    for name, a in lay_out(inputs).items():
        arrays[f"in_{name}_dram"] = a
        args[name] = nc.dram_tensor(f"in_{name}_dram", a.shape, mybir.dt.from_np(a.dtype), kind="ExternalInput").ap()
    out = nc.dram_tensor("out_0_dram", (1, L, D), F32, kind="ExternalOutput").ap()
    program(nc, args, out)
    r = run_bass_kernel_spmd(nc, [arrays], core_ids=[0])
    return r.results[0]["out_0_dram"]
```

```python
from contextlib import ExitStack

import numpy as np

import concourse.bass as bass
from concourse import mybir

F32 = mybir.dt.float32
F32R = mybir.dt.float32r
ACT = mybir.ActivationFunctionType
ALU = mybir.AluOpType
AX = mybir.AxisListType

P = 128
D = 1024
L = 512
NT = L // P
KD = D // P
EPS = 1e-6
HY, NAW, PW = D // 4, D // 2, D // 4
NH, HD = 8, 64
GW = 64
ROWS = L // GW
KWIN = 16
QC = P // ROWS
KC = 32
NKEY = KC * ROWS
KSTART = [0, 8, 24, 32]
KIND = [0, 1, 1, 2]
KOFF = [0, -8, -16]
TABW = 48
NE, CAP, FF = 16, 64, 2048
FC = 512
NFC = FF // FC
DK = 128
MH, MQ, MV = 4, 64, 128
DFF = 2816
NFT = DFF // P
MAGIC = 12582912.0
TWO_PI_HI = 6.28125
TWO_PI_LO = 0.0019353071795864769
PI = 3.1415925
R = 4
WCH = 2048
MSLOT = 4096

N_IN1, N_OUT1 = 10, 4
N_QKV, N_MQK, N_TOK = 6, 2, 6
N_SG, N_BR = 8, 4
N_OUT2, N_UP, N_DOWN, N_PLE, N_PG = 4, NFT, 12, 1, 4
C_OUT1 = N_IN1
C_QKV = C_OUT1 + N_OUT1
C_TOK = C_QKV + N_QKV
C_MQK = C_TOK + N_TOK
C_SG = C_MQK + N_MQK
C_BR = C_SG + N_SG
C_OUT2 = C_BR + N_BR
C_UP = C_OUT2 + N_OUT2
C_DOWN = C_UP + N_UP
C_PLE = C_DOWN + N_DOWN
C_PG = C_PLE + N_PLE
N_CHUNKS = C_PG + N_PG

COLS = {}


def lay_columns():
    at = 0
    for name, n in (("norm1", 8), ("hw0", 6), ("hw1", 6), ("hw2", 6), ("hb", 6), ("skip", 2),
        ("pscale", 2), ("mixg", 8), ("gmix2", 8), ("cw0", 12), ("cw1", 12),
                    ("cw2", 12), ("cw3", 12), ("gffn", 8), ("gple", 8), ("norm2", 8), ("fb1", 1), ("fb2", 1),
                    ("freq", 1), ("wk", 4), ("negt", 4), ("alt2", 1)):
        COLS[name] = at
        at += n
    return at


N_COLS = lay_columns()
ROW = {"gdn": (0, 128), "mln": (128, 512), "alog": (640, 4), "dtb": (644, 4), "ib": (648, 4), "fb": (652, 4)}
N_ROW = 656


SHARED = {
    "dve_variances": (("var1_made", 1), ("hvar_made", 2), ("nvar_made", 1), ("n2var_made", 1),
        ("ovar_made", 2)),
    "act_roots": (("sd1_made", 1), ("hsd_made", 2), ("nsd_made", 1), ("n2sd_made", 1), ("osd_made", 2)),
    "act_squares": (("psq_made", 2), ("nsq_made", 4), ("n2sq_made", 4), ("osq_made", 2)),
    "dve_squares": (("sq1_made", 8), ("hsq_made", 2)),
    "act_steps": (("decay_made", 4), ("fh_made", 2), ("z_copied", 4), ("rs_made", 8), ("pmix_copied", 2),
        ("ot_copied", 4), ("lg_exp", 1), ("beta_made", 1), ("glog_made", 1), ("eg_made", 1),
        ("em_made", 1)),
    "pe_steps": (("net1_filled", 1), ("net2_filled", 1), ("filt_filled", 4), ("z_turned", 4),
        ("four_filled", 4), ("pmix_filled", 2), ("yhy_filled", 2), ("hsum_filled", 2), ("ot_filled", 4),
        ("h2_turned", 8), ("lg_filled", 1), ("aff_turned", 1), ("rank_turned", 1), ("gates_filled", 1),
        ("gc_filled", 1), ("rows_filled", 1), ("mcol_filled", 1)),
    "dve_steps": (("z_made", 2), ("filt_made", 4), ("pq_made", 2), ("lg_made", 1), ("aff_made", 1),
        ("rank_made", 1), ("gabs_made", 1), ("mrow_made", 1)),
}
SHARED_AT = {}
for _sem, _signals in SHARED.items():
    _base = 0
    for _name, _count in _signals:
        SHARED_AT[_name] = (_sem, _base)
        _base += _count


def program(nc, A, out):
    ctx = ExitStack()
    with ctx:
        arena_at = -(-nc.sbuf_base // 32) * 32
        arena = ctx.enter_context(nc.sbuf_tensor("arena", [P, 53200], F32))
        bank = [ctx.enter_context(nc.psum_tensor(f"bank{i}", [P, 512], F32)) for i in range(8)]
        named = {}

        def S(name):
            sem = SHARED_AT[name][0] if name in SHARED_AT else name
            if sem not in named:
                named[sem] = ctx.enter_context(nc.semaphore(sem))
            return named[sem]

        def nth(name, n):
            return SHARED_AT[name][1] + n

        def view(start, *dims):
            n = int(np.prod(dims))
            v = arena[:, start:start + n]
            if len(dims) == 2:
                v = v.rearrange("p (a b) -> p a b", b=dims[1])
            elif len(dims) == 3:
                v = v.rearrange("p (a b c) -> p a b c", b=dims[1], c=dims[2])
            return v

        def rounded(name, start, n):
            return nc.alloc_sbuf_tensor_at(name, [P, n], F32R, offset=arena_at + 4 * start)[:, :]

        x_res = view(0, NT, D)
        hT = view(4096, KD, L)
        ident = view(8192, P)
        ones = view(8320, P)
        utri = view(8448, P)
        strict = view(8576, P)
        cols = view(8704, 192)
        rows = view(8896, N_ROW)
        grow = view(9600, D)
        stat = view(10624, 400)
        wring = [view(11024 + WCH * s, WCH) for s in range(R)]
        B = 11024 + WCH * R

        def col(name, i=0, p0=0, p1=P):
            c = COLS[name] + i
            return cols[p0:p1, c:c + 1]

        def row(name):
            a, n = ROW[name]
            return rows[:, a:a + n]

        def slot(c):
            return wring[c % R]

        def slot_pair(c):
            return arena[:, 11024 + WCH * (c % R):11024 + WCH * (c % R + 2)].rearrange("p (s k n) -> p s k n", s=2, n=256)

        hyu = view(B, 6, L)
        hz = view(B + 2 * L, 2, L)
        zqp = view(B + 3072, NT, 768)
        rs = view(B + 6144, 512)
        filt = view(B + 6656, NT, 512)
        ywf = view(B + 6656, NT, 512)
        hyt = view(B + 8704, 2, 512)
        pr = [view(B + 8704 + 256 * i, 256) for i in range(4)]
        cosm = view(B + 9728, NT, 512)
        sinm = view(B + 11776, NT, 512)
        table = view(B + 9728, NH * ROWS, TABW)
        pos = view(B + 13824, 512)
        fw1 = view(B + 14336, P)
        fw2 = view(B + 14464, P)
        fwo = view(B + 14592, 512)
        fa = view(B + 15104, 512)
        fk = view(B + 15616, 512)
        fh = view(B + 16128, 512)
        decay = view(B + 16640, NT, 256)
        PADW = 544
        pu = view(B + 13824, 2, PADW)
        p2 = view(B + 13824 + 1088, PADW)
        p4 = view(B + 13824 + 1632, PADW)
        p8 = view(B + 13824 + 2176, PADW)
        pooled = view(B + 13824 + 2720, 2, L)
        pwbd = view(B + 17664, 2, P)
        qz = view(B + 17920, NH, L)
        kT = view(B + 22016, 4, L)
        va = view(B + 24064, NT, NAW)
        vb_ = view(B + 26112, 3, NAW)
        bias = view(B + 27648, 3, NH * NKEY)
        sc = [view(B + 3072 + 512 * i, 512) for i in range(3)]
        pt = [view(B + 4608 + 512 * i, 512) for i in range(3)]
        sbank = [bank[6], bank[7], bank[4]]
        ona = view(B + 9728, NT, NAW)
        mixT = hT
        hperm = view(0, NT, KD * P)
        invc = view(9600, 2, L)

        mslot = [view(11024 + MSLOT * s, MSLOT) for s in range(6)]
        M0 = 11024 + 6 * MSLOT
        h2 = view(M0, NT, D)
        onehot = view(M0 + 4096, NT, NE * CAP)
        xsT = view(M0 + 8192, KD, CAP)
        pg = view(M0 + 8704, NT, P)
        gt = view(M0 + 9216, L)
        silu = [view(M0 + 9728 + 256 * i, 256) for i in range(2)]
        hid = [view(M0 + 10240 + 256 * i, 256) for i in range(2)]
        hidT = [view(M0 + 10752 + 256 * i, 256) for i in range(2)]
        ysb = view(M0 + 11264, 1024)
        wr = view(M0 + 12288, KD, NE)
        aff = view(M0 + 12416, NT, NE)
        work = view(M0 + 12480, L)
        rank = view(M0 + 12992, L)
        sel = view(M0 + 13504, L)
        rankc = view(M0 + 14016, NT, NE)
        iota = view(M0 + 14080, CAP)
        lg = view(M0 + 14144, NT, NE)
        sqd = view(M0 + 14208, D)

        hn = view(B, NT, D)
        oa = view(B, NT, 512)
        ob = view(B + 2048, NT, 512)
        qkv = view(B + 4096, 12, L)
        gz = view(B + 10240, NT, 512)
        mo = view(B + 12288, NT, 512)
        mqz = view(B + 14336, MH, L)
        mk = view(B + 16384, 2, L)
        mv = view(B + 17408, NT, MH * 129)
        GS = B + 19472
        wg = view(GS, KD, 16)
        gate = view(GS + 128, NT, 16)
        gx = view(GS + 192, NT, 8)
        gl_ = view(GS + 224, NT, 8)
        beta = view(GS + 256, NT, 4)
        gg = view(GS + 272, NT, 4)
        lf = view(GS + 288, NT, 4)
        ip = view(GS + 304, NT, 4)
        gc = view(GS + 320, NT, 4)
        eg = view(GS + 336, NT, 4)
        ebg = view(GS + 352, NT, 4)
        edec = view(GS + 368, NT, 4)
        ea = view(GS + 384, 4)
        acol = view(GS + 388, NT, 4)
        emcol = view(GS + 404, NT, 4)
        gsm = view(GS + 420, 64)
        T0 = B + 20480

        def tmp(i, n=1):
            return view(T0 + 512 * i, 512 * n)

        class Own:

            def __init__(self, eng, name):
                self.eng, self.name, self.n = eng, name, 0

            def __call__(self, ins):
                ins.then_inc(S(self.name), 1)
                self.n += 1
                return self.n

            def wait(self, n=None):
                self.eng.wait_ge(S(self.name), self.n if n is None else n)

        block = ctx.enter_context(nc.Block())

        used = {}
        for c in range(8):
            used[c] = ("proj_filled", 2 * (c + 1))
        used[8] = used[9] = ("proj_filled", 20)
        for i in range(4):
            used[C_OUT1 + i] = ("out1_filled", 4 * (i // 2 + 1))
        for i in range(N_QKV):
            used[C_QKV + i] = ("qkv_filled", 2 * (i + 1))
        for i in range(N_TOK):
            used[C_TOK + i] = ("tok_filled", 4 * (i // 2 + 1))
        for i in range(N_MQK):
            used[C_MQK + i] = ("mqk_filled", 2 * (i + 1))
        for i in range(N_SG):
            used[C_SG + i] = ("sg_filled", 2 * (i + 1))
        for i in range(N_BR):
            used[C_BR + i] = ("br_filled", 4 * (i + 1))
        for i in range(4):
            used[C_OUT2 + i] = ("out2_filled", 4 * (i // 2 + 1))
        for i in range(N_UP // 2):
            used[C_UP + 2 * i] = used[C_UP + 2 * i + 1] = ("up_filled", 4 * (i + 1))
        for i in range(12):
            used[C_DOWN + i] = ("down_chunk", i + 1)
        used[C_PLE] = ("ple_filled", 8)
        for i in range(4):
            used[C_PG + i] = ("pg_filled", 4 * (i + 1))

        def wait_chunk(pe, c):
            pe.wait_ge(S(f"chunk_in{c % R}"), 16 * (c // R + 1))

        junk = view(T0 + 12288, D)
        blk = grow[:, 0:7 * P].rearrange("p (l c) -> p l c", c=P)
        maT = view(T0, 4, 512)
        atT = view(T0 + 2048, 4, 512)
        kbg = view(T0 + 4096, 4, 512)
        kdc = view(T0 + 6144, 4, 512)
        vbt = view(T0 + 8192, 4, 512)
        egb = tmp(20)
        dec = tmp(21)
        dms = tmp(22)
        moff = [tmp(20), tmp(21)]
        xw = [tmp(22), tmp(23)]
        tin = view(B, 4, 512)
        tit = view(B + 2048, 4, 512)
        wneg = view(B + 8192, 4, 512)
        vnew = [tmp(20), tmp(21)]
        state = tmp(22)
        egl = gsm[:, 0:16]
        hlo = [rounded(f"input_rest{k}", T0 + 512 * k, L) for k in range(KD)]
        hhi = [rounded(f"input_rounded{k}", 4096 + 512 * k, L) for k in range(KD)]
        wlo = [rounded(f"weight_rest{i}", 11024 + WCH * i, WCH) for i in range(R)]
        whi = [rounded(f"weight_rounded{i}", T0 + 4096 + WCH * i, WCH) for i in range(R)]
        ahi = [rounded(f"hidden_rounded{k}", B + 512 * k if k < 8 else B + 13312 + 512 * k, L) for k in range(NFT)]
        fsilu = [view(B + 16384 + 512 * i, 512) for i in range(2)]
        brbank = [bank[3], bank[6], bank[0], bank[1]]
        sg = [view(T0 + 4096 + 512 * f, 512) for f in range(16)]
        brow, arow, mrow, mxrow = (view(T0 + 512 * i, L) for i in range(4))
        expo = view(T0 + 2048, 1280)
        den = gsm[:, 16:32]
        oTa = view(B + 4096, 4, L)
        oTb = view(B + 6144, 4, L)
        mixed = view(B + 8192, KD, L)
        actT = view(B + 4096, NFT, L)
        alo = [rounded(f"hidden_rest{k}", B + 4096 + 512 * k, L) for k in range(NFT)]
        pT = view(B + 15360, 2, L)
        pw = view(B + 4096, NT, D)
        N3, N4, N5, NO = range(4)
        nstat = [stat[:, 256 + 4 * i:260 + 4 * i] for i in range(5)]
        hstat = stat[:, 280:312]
        r_both = stat[:, 320:328]
        r13 = stat[:, 328:332]

        def norm_squares(act, norm, ready, step):
            for i in range(NT + 1):
                if i < NT:
                    act.wait_ge(S(ready), step(i))
                    if NT * norm + i:
                        act.wait_ge(S("norm_sq"), NT * norm + i)
                    act.activation(junk, x_res[:, i, :], ACT.Square, accum_out=nstat[norm][:, i:i + 1])\
                        .then_inc(S("norm_sq"), 1)
                if i:
                    act.wait_ge(S("norm_var"), NT * norm + i)
                    v = nstat[norm][:, i - 1:i]
                    act.activation(v, v, ACT.Sqrt).then_inc(S("norm_sd"), 1)

        def norm_var(dve, norm, i):
            dve.wait_ge(S("norm_sq"), NT * norm + i + 1)
            v = nstat[norm][:, i:i + 1]
            dve.tensor_scalar(v, v, 1.0 / D, EPS, ALU.mult, ALU.add).then_inc(S("norm_var"), 1)

        def norm_rstd(dve, own, norm, i):
            dve.wait_ge(S("norm_sd"), NT * norm + i + 1)
            v = nstat[norm][:, i:i + 1]
            own(dve.reciprocal(v, v))
            own.wait()

        def norm_turn_pe(pe, turn, norm):
            done = (0, KD // 2, KD // 2 + KD)[norm]
            pe.wait_ge(S("norm_scaled"), NT * (norm - N3) + NT)
            for k in range(KD):
                if k >= 2 and norm == N4:
                    pe.wait_ge(S("norm_tv"), done + k - 1)
                elif k >= 2:
                    pe.wait_ge(S("norm_ta" if k % 2 == 0 else "norm_tv"), done + k // 2)
                for i in range(NT):
                    last = turn(bank[6 + k % 2][:, P * i:P * i + P], hn[:, i, P * k:P * k + P], ident)
                last.then_inc(S("norm_turned"), 1)
            pe.wait_ge(S("norm_ta"), done + (KD if norm == N4 else KD // 2))
            pe.wait_ge(S("norm_tv"), done + (KD if norm == N4 else KD // 2))

        def norm_turn_act(act, norm, gain):
            for k in range(0, KD, 2):
                act.wait_ge(S("norm_turned"), KD * (norm - N3) + k + 1)
                act.activation(hT[:, k, :], bank[6][:, :], ACT.Copy, scale=col(gain, k)).then_inc(S("norm_ta"), 1)

        def split_turn_act(act, gain):
            for k in range(KD):
                act.wait_ge(S("norm_turned"), KD * (N4 - N3) + k + 1)
                act.activation(hhi[k], bank[6 + k % 2][:, :], ACT.Copy, scale=col(gain, k)).then_inc(S("norm_ta"), 1)

        def split_turn_dve(dve, gain):
            for k in range(KD):
                dve.wait_ge(S("norm_ta"), KD // 2 + k + 1)
                dve.scalar_tensor_tensor(out=hlo[k], in0=bank[6 + k % 2][:, :], scalar=col(gain, k),
                                         in1=hhi[k], op0=ALU.mult, op1=ALU.subtract).then_inc(S("norm_tv"), 1)

        def norm_scale(dve, own, norm):
            for i in range(NT):
                if i == NT - 1:
                    norm_var(dve, norm, i)
                norm_rstd(dve, own, norm, i)
                dve.tensor_scalar(hn[:, i, :], x_res[:, i, :], nstat[norm][:, i:i + 1], None, ALU.mult)\
                    .then_inc(S("norm_scaled"), 1)

        def norm_turn_dve(dve, norm, gain):
            for k in range(1, KD, 2):
                dve.wait_ge(S("norm_turned"), KD * (norm - N3) + k + 1)
                dve.tensor_scalar(hT[:, k, :], bank[7][:, :], col(gain, k), None, ALU.mult).then_inc(S("norm_tv"), 1)

        def hv(v, h):
            return v[:, P * h:P * h + P]

        def second_pool(pool):
            pool.wait_ge(S("y_part"), NE * NFC)
            pool.memset(mqz, 0.0).then_inc(S("mq_zero"), 1)
            pool.memset(mv.rearrange("p i (h d) -> p (i h) d", d=129)[:, :, 128:129], 1.0).then_inc(S("mv_one"), 1)
            pool.wait_ge(S("xg_made"), NT)
            pool.dma_start(blk, A["blk"]).then_inc(S("gfirst_in"), 16)
            pool.wait_ge(S("gfirst_in"), 32)
            pool.wait_ge(S("prep_done"), 4)
            for l in range(7):
                for n in range(4):
                    u = 4 * l + n
                    if u >= 2:
                        pool.wait_ge(S("x_filled" if u - 2 >= 4 else "t_made"), u - 2 - 3 if u - 2 >= 4 else u - 1)
                    pool.tensor_tensor(out=moff[n % 2].rearrange("p (h c) -> p h c", c=P),
                                       in0=maT[:, n, :].rearrange("p (h c) -> p h c", c=P),
                                       in1=blk[:, l, :].unsqueeze(1).to_broadcast([P, 4, P]), op=ALU.mult)\
                        .then_inc(S("moff_made"), 1)

        def second_pe(pe, mm, turn):
            norm_turn_pe(pe, turn, N3)
            pe.wait_ge(S("wg_in"), 16)
            for i in range(NT):
                for k in range(KD):
                    last = mm(bank[0][:, 16 * i:16 * i + 16], hT[:, k, P * i:P * i + P], wg[:, k, :],
                              start=k == 0, stop=k == KD - 1)
            last.then_inc(S("gates_filled"), 1)
            for u in range(12):
                c = C_QKV + u // 2
                if u % 2 == 0:
                    wait_chunk(pe, c)
                if u >= 4:
                    pe.wait_ge(S("cv_done"), u - 3)
                w = slot(c).rearrange("p (k n) -> p k n", n=256)
                for k in range(KD):
                    last = mm(bank[1 + u % 4][:, :], w[:, k, P * (u % 2):P * (u % 2) + P], hT[:, k, :],
                              start=k == 0, stop=k == KD - 1)
                last.then_inc(S("qkv_filled"), 1)
            pe.wait_ge(S("gg_made"), 2)
            mm(bank[0][:, 64:80], utri, gg.rearrange("p n h -> p (n h)"), start=True, stop=True).then_inc(S("gc_filled"), 1)

            def aside(j):
                v, half = j // 2, j % 2
                b = bank[6 + v % 2]
                if v >= 2 and half == 0:
                    pe.wait_ge(S("aside_copied"), v - 1)
                if v < 12:
                    c = C_TOK + 2 * (v // 4)
                    if v % 4 == 0 and half == 0:
                        wait_chunk(pe, c)
                        wait_chunk(pe, c + 1)
                else:
                    c = C_MQK + (v - 12) // 2
                    if v % 2 == 0 and half == 0:
                        wait_chunk(pe, c)
                for k in range(4 * half, 4 * half + 4):
                    if v < 12:
                        last = mm(b[:, :], hT[:, k, P * (v % 4):P * (v % 4) + P], slot_pair(c)[:, :, k, :],
                                  start=k == 0, stop=k == KD - 1)
                    else:
                        w = slot(c).rearrange("p (k n) -> p k n", n=256)
                        last = mm(b[:, :], w[:, k, P * (v % 2):P * (v % 2) + P], hT[:, k, :], start=k == 0, stop=k == KD - 1)
                if half == 1:
                    last.then_inc(S("tok_filled" if v < 12 else "mqk_filled"), 1)

            for t in range(8):
                pe.wait_ge(S("l2_sq"), t + 1)
                if t >= 2:
                    pe.wait_ge(S("l2_sd"), t - 1)
                if t == 0:
                    pe.wait_ge(S("cv_done"), 12)
                mm(bank[4 + t % 2][:, :], ones, tmp(t % 2), start=True, stop=True).then_inc(S("l2_filled"), 1)
                aside(t)

            pe.wait_ge(S("l2_done"), 8)
            pe.wait_ge(S("cv_silu"), 12)
            pe.wait_ge(S("beta_made"), nth("beta_made", 1))
            for n in range(4):
                t = slice(P * n, P * n + P)
                if n:
                    pe.wait_ge(S("prep_done"), n)
                for h in range(4):
                    mm(hv(bank[0], h), gg[:, n, h:h + 1].to_broadcast([P, P]), utri, start=True, stop=True)
                for h in range(4):
                    last = mm(hv(bank[1], h), beta[:, n, h:h + 1].to_broadcast([P, P]), ident, start=True, stop=True)
                last.then_inc(S("gb_filled"), 1)
                for h in range(4):
                    mm(hv(bank[2], h), qkv[:, 4 + h, t], qkv[:, h, t], start=True, stop=True)
                for h in range(4):
                    last = mm(hv(bank[3], h), qkv[:, 4 + h, t], qkv[:, 4 + h, t], start=True, stop=True)
                last.then_inc(S("kk_filled"), 1)
                for h in range(4):
                    turn(hv(bank[4], h), qkv[:, 4 + h, t], ident)
                for h in range(4):
                    last = turn(hv(bank[5], h), qkv[:, 8 + h, t], ident)
                last.then_inc(S("kv_turned"), 1)
                for j in range(3):
                    aside(8 + 3 * n + j)
            for n in range(4):
                pe.wait_ge(S("tt_made"), n + 1)
                if n == 0:
                    pe.wait_ge(S("prep_done"), 4)
                if n >= 2:
                    pe.wait_ge(S("t_made"), n - 1)
                for h in range(4):
                    last = turn(hv(bank[4 + n % 2], h), hv(tit[:, n, :], h), ident)
                last.then_inc(S("t_filled"), 1)

            def x_of(u):
                n = u % 4
                pe.wait_ge(S("moff_made"), u + 1)
                pe.wait_ge(S("t_made"), u - 3)
                if u >= 6:
                    pe.wait_ge(S("x_made"), u - 5)
                for h in range(4):
                    last = mm(hv(bank[n % 2], h), hv(moff[n % 2], h), hv(tin[:, n, :], h), start=True, stop=True)
                last.then_inc(S("x_filled"), 1)

            x_of(4)
            for u in range(4, 28):
                n = u % 4
                if u < 27:
                    x_of(u + 1)
                pe.wait_ge(S("x_made"), u - 3)
                if u >= 6:
                    pe.wait_ge(S("tt_made"), u - 1)
                for h in range(4):
                    last = mm(hv(bank[2 + n % 2], h), hv(xw[n % 2], h), hv(tit[:, n, :], h), start=True, stop=True)
                last.then_inc(S("tc_filled"), 1)
                if u % 2 == 0:
                    aside(20 + (u - 4) // 2)
                if u < 24:
                    pe.wait_ge(S("tt_made"), u + 1)
                    pe.wait_ge(S("t_made"), u - 1)
                    for h in range(4):
                        last = turn(hv(bank[4 + n % 2], h), hv(tit[:, n, :], h), ident)
                    last.then_inc(S("t_filled"), 1)

            def gate_half(f, half):
                b = bank[(4 + f % 2) if f < 4 else (7, 2)[f % 2]]
                if half == 0:
                    if f % 2 == 0:
                        wait_chunk(pe, C_SG + f // 2)
                    if f >= 2:
                        pe.wait_ge(S("sg_made"), f - 1)
                w = slot(C_SG + f // 2).rearrange("p (k n) -> p k n", n=256)
                for k in range(4 * half, 4 * half + 4):
                    last = mm(b[:, :], w[:, k, P * (f % 2):P * (f % 2) + P], hT[:, k, :], start=k == 0, stop=k == KD - 1)
                if half == 1:
                    last.then_inc(S("sg_filled"), 1)

            for n in range(4):
                pe.wait_ge(S("tt_made"), 25 + n)
                if n == 0:
                    pe.wait_ge(S("aside_copied"), 16)
                if n:
                    pe.wait_ge(S("w_made"), n)
                for h in range(4):
                    last = mm(hv(bank[6], h), hv(kbg[:, n, :], h), hv(tit[:, n, :], h), start=True, stop=True)
                last.then_inc(S("w_filled"), 1)
            pe.wait_ge(S("w_made"), 4)
            pe.wait_ge(S("st_made"), 1)
            for n in range(4):
                pe.wait_ge(S("st_made"), 4 * n + 1)
                for h in range(4):
                    mm(hv(bank[7], h), hv(tit[:, n, :], h), hv(vbt[:, n, :], h), start=True, stop=False)
                    last = mm(hv(bank[7], h), hv(wneg[:, n, :], h), hv(state, h), start=False, stop=True)
                last.then_inc(S("vn_filled"), 1)
                gate_half(n, 0)
                pe.wait_ge(S("vn_made"), n + 1)
                if n >= 2:
                    pe.wait_ge(S("oa_made"), n - 1)
                for h in range(4):
                    mm(hv(bank[n % 2], h), qkv[:, h, P * n:P * n + P], hv(state, h), start=True, stop=False)
                    last = mm(hv(bank[n % 2], h), hv(atT[:, n, :], h), hv(vnew[n % 2], h), start=False, stop=True)
                last.then_inc(S("oa_filled"), 1)
                if n < 3:
                    for h in range(4):
                        last = mm(hv(bank[6], h), hv(kdc[:, n, :], h), hv(vnew[n % 2], h), start=True, stop=True)
                    last.then_inc(S("sk_filled"), 1)
                gate_half(n, 1)
            pe.wait_ge(S("gg_made"), 4)
            pe.wait_ge(S("oa_made"), 4)
            for i in range(NT):
                turn(bank[0][0:4, P * i:P * i + P], lf[:, i, :], ident)
            for i in range(NT):
                last = turn(bank[1][0:4, P * i:P * i + P], ip[:, i, :], ident)
            last.then_inc(S("rows_filled"), 1)
            gate_half(4, 0)
            gate_half(4, 1)
            pe.wait_ge(S("mrow_made"), nth("mrow_made", 1))
            for i in range(NT):
                turn(bank[2][:, 4 * i:4 * i + 4], arow[0:4, P * i:P * i + P], ident[0:4, 0:4])
                last = turn(bank[2][:, 16 + 4 * i:20 + 4 * i], mrow[0:4, P * i:P * i + P], ident[0:4, 0:4])
            last.then_inc(S("mcol_filled"), 1)
            pe.wait_ge(S("mv_one"), 1)
            pe.wait_ge(S("sg_made"), 4)
            for h in range(MH):
                if h:
                    pe.wait_ge(S("mp_made"), h)
                mm(bank[3][:, :], ident[0:4, h:h + 1].to_broadcast([4, P]), mxrow[0:4, :], start=True, stop=True)\
                    .then_inc(S("mb_filled"), 1)
                for a, (b, o) in enumerate(((4, 0), (5, 0), (6, 0), (5, 384))):
                    last = mm(bank[b][:, o:o + L - P * a], mk[:, h // 2, P * a:P * a + P], mqz[:, h, P * a:L],
                              start=True, stop=True)
                last.then_inc(S("ms_filled"), 1)
                if h == 0:
                    pe.wait_ge(S("mx_made"), 1)
                gate_half(5 + 2 * h, 0)
                gate_half(5 + 2 * h, 1)
                pe.wait_ge(S("mp_made"), h + 1)
                pe.wait_ge(S("ob_made"), 4 * h)
                for i in range(NT):
                    for a in range(i + 1):
                        o = (0, 512, 896, 1152)[a]
                        last = mm(bank[i // 2][:, 129 * (i % 2):129 * (i % 2) + 129],
                                  expo[:, o + P * (i - a):o + P * (i - a) + P], mv[:, a, 129 * h:129 * h + 129],
                                  start=a == 0, stop=a == i)
                last.then_inc(S("mo_filled"), 1)
                gate_half(6 + 2 * h, 0)
                gate_half(6 + 2 * h, 1)
            for br in range(2):
                pe.wait_ge(S("on2_made"), NT * (br + 1))
                for m in range(4):
                    u = 4 * br + m
                    if u >= 2:
                        pe.wait_ge(S("oT_made"), u - 1)
                    for i in range(NT):
                        last = turn(bank[4 + u % 2][:, P * i:P * i + P], (oa, ob)[br][:, i, P * m:P * m + P], ident)
                    last.then_inc(S("oT_filled"), 1)
                if br == 0:
                    for f in range(13, 16):
                        gate_half(f, 0)
                        gate_half(f, 1)
                pe.wait_ge(S("oT_made"), 4 * br + 4)
                for f in range(8 * br, 8 * br + 8):
                    if f % 4 == 0:
                        wait_chunk(pe, C_BR + f // 4)
                    if f == 0:
                        pe.wait_ge(S("ob_made"), 16)
                    if f >= 4:
                        pe.wait_ge(S("br_used"), f - 3)
                    w = slot(C_BR + f // 4).rearrange("p (k n) -> p k n", n=512)
                    for k in range(4):
                        last = mm(brbank[f % 4][:, :], w[:, k, P * (f % 4):P * (f % 4) + P], (oTa, oTb)[br][:, k, :],
                                  start=k == 0, stop=k == 3)
                    last.then_inc(S("br_filled"), 1)
            pe.wait_ge(S("br_used"), 16)
            for c in range(N_OUT2 // 2):
                wait_chunk(pe, C_OUT2 + 2 * c)
                wait_chunk(pe, C_OUT2 + 2 * c + 1)
                w = slot_pair(C_OUT2 + 2 * c)
                for i in range(NT):
                    u = 4 * c + i
                    if u >= 4:
                        pe.wait_ge(S("out2_added"), u - 3)
                    for k in range(KD):
                        last = mm(bank[4 + i][:, :], mixed[:, k, P * i:P * i + P], w[:, :, k, :], start=k == 0, stop=k == KD - 1)
                    last.then_inc(S("out2_filled"), 1)
            norm_turn_pe(pe, turn, N4)

            def up_tile(c, parts, f2, done):
                for which in range(2):
                    pe.wait_ge(S("wlo_made"), parts + which)
                    wh = whi[(c + which) % R].rearrange("p (k n) -> p k n", n=256)
                    wl = wlo[(c + which) % R].rearrange("p (k n) -> p k n", n=256)
                    m = slice(P * f2, P * f2 + P)
                    if which == 0:
                        pe.wait_ge(S("act_made"), done)
                    for k in range(KD):
                        b = bank[2 * which + f2][:, :]
                        mm(b, wl[:, k, m], hhi[k], start=k == 0, stop=False)
                        mm(b, wh[:, k, m], hlo[k], start=False, stop=False)
                        last = mm(b, wh[:, k, m], hhi[k], start=False, stop=k == KD - 1)
                    last.then_inc(S("up_filled"), 1)

            pe.sem_inc(S("act_made"), 2)
            with pe.Fori(0, NFT // 4) as r:
                for q in range(4):
                    up_tile(C_UP + 2 * (q // 2), r * 4 + (2 * (q // 2) + 1), q % 2, r * 4 + (q + 1))
            for q in range(NFT % 4):
                up_tile(C_UP + NFT // 4 * 4, NFT // 4 * 4 + 1, q % 2, NFT // 4 * 4 + q + 1)
            pe.wait_ge(S("act_made"), NFT + 2)
            for n in range(2):
                for d in range(6):
                    c = C_DOWN + 6 * n + d
                    ks = range(4 * d, min(4 * d + 4, NFT))
                    pe.wait_ge(S("wlo_made"), NFT + 6 * n + d + 1)
                    if n == 0:
                        pe.wait_ge(S("alo_made"), ks[-1] + 1)
                    wh = whi[c % R].rearrange("p (k n) -> p k n", n=512)
                    wl = wlo[c % R].rearrange("p (k n) -> p k n", n=512)
                    for k in ks:
                        for i in range(NT):
                            b, t = bank[4 * (1 - n) + i][:, :], slice(P * i, P * i + P)
                            mm(b, alo[k][:, t], wh[:, k - 4 * d, :], start=k == 0, stop=False)
                            mm(b, ahi[k][:, t], wl[:, k - 4 * d, :], start=False, stop=False)
                            last = mm(b, ahi[k][:, t], wh[:, k - 4 * d, :], start=False, stop=k == NFT - 1)
                    last.then_inc(S("down_chunk"), 1)
            pe.wait_ge(S("wg_in"), 48)
            pe.wait_ge(S("down_added"), 4)
            wait_chunk(pe, C_PLE)
            w = slot(C_PLE).rearrange("p (k n) -> p k n", n=1024)
            for u in range(8):
                i, n = u // 2, u % 2
                if u >= 4:
                    pe.wait_ge(S("pw_made"), u - 3)
                for k in range(2):
                    last = mm(bank[4 + u % 4][:, :], pT[:, k, P * i:P * i + P], w[:, k, 512 * n:512 * n + 512],
                              start=k == 0, stop=k == 1)
                last.then_inc(S("ple_filled"), 1)
            pe.wait_ge(S("pw_made"), 8)
            norm_turn_pe(pe, turn, N5)
            pe.wait_ge(S("down_added"), 8)
            for c in range(4):
                wait_chunk(pe, C_PG + c)
                w = slot(C_PG + c).rearrange("p (k n) -> p k n", n=256)
                for i in range(NT):
                    u = 4 * c + i
                    if u >= 4:
                        pe.wait_ge(S("pg_copied"), u - 3)
                    for k in range(KD):
                        last = mm(bank[i][:, 0:256], hT[:, k, P * i:P * i + P], w[:, k, :], start=k == 0, stop=k == KD - 1)
                    last.then_inc(S("pg_filled"), 1)

        def second_dve(dve, own):
            stt = dve.scalar_tensor_tensor
            tt = dve.tensor_tensor
            ts = dve.tensor_scalar
            dve.wait_ge(S("gfirst_in"), 16)
            for i in range(NT):
                dve.wait_ge(S("first_sq"), i + 1)
                tt(out=x_res[:, i, :], in0=x_res[:, i, :], in1=grow, op=ALU.mult).then_inc(S("xg_made"), 1)
            s1, s3, v1, v3 = (stat[:, 312 + 4 * i:316 + 4 * i] for i in range(4))
            own(ts(v1, s1, 1.0 / D, EPS, ALU.mult, ALU.add))
            own.wait()
            own(dve.reciprocal(s1, v1))
            own.wait()
            dve.wait_ge(S("norm_sq"), NT)
            own(tt(out=s3, in0=s3, in1=s1, op=ALU.mult))
            own.wait()
            ts(v3, s3, 1.0 / D, EPS, ALU.mult, ALU.add).then_inc(S("norm_var"), NT)
            dve.wait_ge(S("norm_sd"), NT)
            own(dve.reciprocal(r_both, r_both))
            own.wait()
            tt(out=r13, in0=v1, in1=v3, op=ALU.mult).then_inc(S("r_made"), 1)
            dve.wait_ge(S("r_made"), 1)
            for i in range(NT):
                ts(hn[:, i, :], x_res[:, i, :], r13[:, i:i + 1], None, ALU.mult).then_inc(S("norm_scaled"), 1)
            norm_turn_dve(dve, N3, "gmix2")
            dve.wait_ge(S("gates_filled"), nth("gates_filled", 1))
            dve.wait_ge(S("rows_in"), 48)
            g3 = bank[0][:, 0:64].rearrange("p (i g) -> p i g", g=16)

            def rb(name):
                return row(name).unsqueeze(1).to_broadcast([P, NT, 4])

            own(tt(out=gx[:, :, 0:4], in0=g3[:, :, 4:8], in1=rb("dtb"), op=ALU.add))
            own(tt(out=gx[:, :, 4:8], in0=g3[:, :, 12:16], in1=rb("fb"), op=ALU.add))
            own(tt(out=ip, in0=g3[:, :, 8:12], in1=rb("ib"), op=ALU.add))
            own.wait()
            stt(out=gl_, in0=gx, scalar=-1.0, in1=gx, op0=ALU.mult, op1=ALU.max).then_inc(S("gabs_made"), 1)
            for u in range(12):
                ps = bank[1 + u % 4]
                dve.wait_ge(S("qk_copied"), u + 1)
                for j in (1, 2):
                    own(stt(out=qkv[:, u, j:L], in0=ps[:, 0:L - j], scalar=col(f"cw{3 - j}", u), in1=qkv[:, u, j:L],
                            op0=ALU.mult, op1=ALU.add))
                    own.wait()
                stt(out=qkv[:, u, 3:L], in0=ps[:, 0:L - 3], scalar=col("cw0", u), in1=qkv[:, u, 3:L],
                    op0=ALU.mult, op1=ALU.add).then_inc(S("cv_done"), 1)
                if u == 1:
                    dve.wait_ge(S("glog_made"), nth("glog_made", 1))
                    own(stt(out=gg, in0=gx[:, :, 0:4], scalar=0.0, in1=gl_[:, :, 0:4], op0=ALU.max, op1=ALU.add))
                    own.wait()
                    stt(out=gg, in0=gg, scalar=-1.0, in1=ea.unsqueeze(1).to_broadcast([P, NT, 4]), op0=ALU.mult,
                        op1=ALU.mult).then_inc(S("gg_made"), 1)
                    stt(out=lf, in0=gx[:, :, 4:8], scalar=0.0, in1=gl_[:, :, 4:8], op0=ALU.min, op1=ALU.subtract)\
                        .then_inc(S("gg_made"), 1)
                    dve.wait_ge(S("gg_made"), 2)
                    dve.engine_nop().then_inc(S("gg_made"), 2)
            dve.wait_ge(S("gc_filled"), nth("gc_filled", 1))
            dve.wait_ge(S("eg_made"), nth("eg_made", 1))
            own(dve.tensor_copy(gc.rearrange("p n h -> p (n h)"), bank[0][:, 64:80]))
            dve.wait_ge(S("beta_made"), nth("beta_made", 1))
            own(tt(out=ebg, in0=eg, in1=beta, op=ALU.mult))
            for t in range(8):
                dve.wait_ge(S("l2_sd"), t + 1)
                own(dve.reciprocal(tmp(2 + t % 2), tmp(2 + t % 2)))
                own.wait()
                stt(out=qkv[:, t, :], in0=qkv[:, t, :], scalar=DK ** -0.5 if t < 4 else 1.0, in1=tmp(2 + t % 2),
                    op0=ALU.mult, op1=ALU.mult).then_inc(S("l2_done"), 1)
            dve.wait_ge(S("l2_done"), 8)

            def h3(v):
                return v.rearrange("p (h c) -> p h c", c=P)

            def per_token(v, n):
                return v[:, n, :].unsqueeze(2).to_broadcast([P, 4, P])

            def every_head(m):
                return m.unsqueeze(1).to_broadcast([P, 4, P])

            for n in range(4):
                t = slice(P * n, P * n + P)
                dve.wait_ge(S("gb_filled"), n + 1)
                own(tt(out=h3(dec), in0=h3(bank[0][:, :]), in1=per_token(gc, n), op=ALU.subtract))
                own(tt(out=edec[:, n, :], in0=h3(bank[0][:, :])[:, :, P - 1], in1=gc[:, n, :], op=ALU.subtract))
                own.wait()
                ts(dec, dec, 0.0, None, ALU.min).then_inc(S("dec_ready"), 1)
                dve.wait_ge(S("dec_made"), 3 * n + 3)
                own(dve.tensor_copy(egl[:, 4 * n:4 * n + 4], h3(egb)[:, :, P - 1]))
                own(tt(out=h3(dms), in0=h3(dec), in1=every_head(strict), op=ALU.mult))
                own.wait()
                own(tt(out=dms, in0=dms, in1=bank[1][:, :], op=ALU.mult))
                own(tt(out=h3(dec), in0=h3(dec), in1=every_head(utri), op=ALU.mult))
                own.wait()
                dve.wait_ge(S("kk_filled"), n + 1)
                own(tt(out=atT[:, n, :], in0=bank[2][:, :], in1=dec, op=ALU.mult))
                own(tt(out=maT[:, n, :], in0=bank[3][:, :], in1=dms, op=ALU.mult))
                own(tt(out=qkv[:, 0:4, t], in0=qkv[:, 0:4, t], in1=h3(egb), op=ALU.mult))
                dve.wait_ge(S("kv_turned"), n + 1)
                own(tt(out=h3(kbg[:, n, :]), in0=h3(bank[4][:, :]), in1=per_token(ebg, n), op=ALU.mult))
                own(tt(out=h3(kdc[:, n, :]), in0=h3(bank[4][:, :]), in1=per_token(edec, n), op=ALU.mult))
                own(tt(out=h3(vbt[:, n, :]), in0=h3(bank[5][:, :]), in1=per_token(beta, n), op=ALU.mult))
                own.wait()
                dve.engine_nop().then_inc(S("prep_done"), 1)
            for n in range(4):
                dve.wait_ge(S("moff_made"), n + 1)
                tt(out=h3(tit[:, n, :]), in0=every_head(ident), in1=h3(moff[n % 2]), op=ALU.subtract)\
                    .then_inc(S("tt_made"), 1)
            for u in range(4, 28):
                n = u % 4
                dve.wait_ge(S("tc_filled"), u - 3)
                tt(out=tit[:, n, :], in0=tit[:, n, :], in1=bank[2 + n % 2][:, :], op=ALU.subtract).then_inc(S("tt_made"), 1)
            dve.wait_ge(S("w_filled"), 4)
            dve.memset(state, 0.0).then_inc(S("st_made"), 1)
            for n in range(4):
                dve.wait_ge(S("vn_filled"), n + 1)
                dve.tensor_copy(vnew[n % 2], bank[7][:, :]).then_inc(S("vn_made"), 1)
                if n < 3:
                    dve.wait_ge(S("sk_filled"), n + 1)
                    dve.wait_ge(S("oa_filled"), n + 1)
                    dve.wait_ge(S("st_made"), 4 * n + 1)
                    for h in range(4):
                        stt(out=hv(state, h), in0=hv(state, h), scalar=egl[:, 4 * n + h:4 * n + h + 1],
                            in1=hv(bank[6], h), op0=ALU.mult, op1=ALU.add).then_inc(S("st_made"), 1)

            def head_var(br):
                sq = view(B + 8192, NT, 512)
                dve.wait_ge(S("osq_made"), nth("osq_made", br + 1))
                hs = hstat[:, 16 * br:16 * br + 16]
                own(dve.tensor_reduce(out=hs, in_=sq.rearrange("p i (h d) -> p (i h) d", d=P), axis=AX.X, op=ALU.add))
                own.wait()
                ts(hs, hs, 1.0 / P, EPS, ALU.mult, ALU.add).then_inc(S("ovar_made"), 1)

            def head_norm(br, i):
                o, gate_ = ((oa, gz), (ob, mo))[br]
                hs = hstat[:, 16 * br:16 * br + 16]
                if i == 0:
                    dve.wait_ge(S("osd_made"), nth("osd_made", br + 1))
                    own(dve.reciprocal(hs, hs))
                    own.wait()
                v = h3(o[:, i, :])
                own(tt(out=v, in0=v, in1=hs[:, 4 * i:4 * i + 4].unsqueeze(2).to_broadcast([P, 4, P]), op=ALU.mult))
                own.wait()
                own(tt(out=v, in0=v, in1=every_head(row("gdn")) if br == 0 else h3(row("mln")), op=ALU.mult))
                own.wait()
                tt(out=o[:, i, :], in0=o[:, i, :], in1=gate_[:, i, :], op=ALU.mult).then_inc(S("on2_made"), 1)

            def mix_tile(f):
                dve.wait_ge(S("br_filled"), f + 1)
                dve.wait_ge(S("sg_made"), f + 1)
                m = mixed[:, f % 8, :]
                ps = brbank[f % 4][:, :]
                if f < 8:
                    tt(out=m, in0=sg[f], in1=ps, op=ALU.mult).then_inc(S("br_used"), 1)
                else:
                    own(tt(out=sg[f], in0=sg[f], in1=ps, op=ALU.mult))
                    own.wait()
                    tt(out=m, in0=m, in1=sg[f], op=ALU.add).then_inc(S("br_used"), 1)

            dve.wait_ge(S("rows_filled"), nth("rows_filled", 1))
            own(dve.tensor_copy(mxrow[0:4, :], bank[0][0:4, :]))
            own.wait()
            own(dve.tensor_tensor_scan(out=brow[0:4, :], data0=mxrow[0:4, :], data1=mxrow[0:4, :], initial=0.0,
                                       op0=ALU.add, op1=ALU.bypass))
            own.wait()
            own(tt(out=arow[0:4, :], in0=bank[1][0:4, :], in1=brow[0:4, :], op=ALU.subtract))
            own.wait()
            own(dve.tensor_tensor_scan(out=mxrow[0:4, :], data0=arow[0:4, :], data1=arow[0:4, :], initial=0.0,
                                       op0=ALU.max, op1=ALU.bypass))
            own.wait()
            tt(out=mrow[0:4, :], in0=brow[0:4, :], in1=mxrow[0:4, :], op=ALU.add).then_inc(S("mrow_made"), 1)
            dve.wait_ge(S("mcol_filled"), nth("mcol_filled", 1))
            dve.wait_ge(S("em_made"), nth("em_made", 1))
            own(dve.tensor_copy(acol.rearrange("p i h -> p (i h)"), bank[2][:, 0:16]))
            own.wait()
            offs = (0, 512, 896, 1152)
            where = ((4, 0), (5, 0), (6, 0), (5, 384))
            for h in range(MH):
                dve.wait_ge(S("mb_filled"), h + 1)
                if h:
                    dve.wait_ge(S("mo_filled"), h)
                for a in range(NT):
                    last = ts(expo[:, offs[a]:offs[a] + L - P * a], bank[3][:, P * a:L], acol[:, a, h:h + 1], 0.0,
                              ALU.subtract, ALU.max)
                    last.then_inc(S("mx_made"), 1)
                dve.wait_ge(S("me_made"), h + 1)
                for a in range(NT):
                    own(tt(out=expo[:, offs[a]:offs[a] + P], in0=expo[:, offs[a]:offs[a] + P], in1=utri, op=ALU.mult))
                own.wait()
                dve.wait_ge(S("ms_filled"), h + 1)
                for a in range(NT):
                    b, o = where[a]
                    e = expo[:, offs[a]:offs[a] + L - P * a]
                    own(tt(out=e, in0=e, in1=bank[b][:, o:o + L - P * a], op=ALU.mult))
                own.wait()
                dve.engine_nop().then_inc(S("mp_made"), 1)
                dve.wait_ge(S("mo_filled"), h + 1)
                for i in range(NT):
                    o = 129 * (i % 2)
                    dn = den[:, i:i + 1]
                    d = bank[i // 2][:, o + 128:o + 129]
                    own(stt(out=dn, in0=d, scalar=-1.0, in1=emcol[:, i, h:h + 1], op0=ALU.mult, op1=ALU.max))
                    own.wait()
                    own(tt(out=dn, in0=dn, in1=d, op=ALU.max))
                own.wait()
                own(dve.reciprocal(den[:, 0:4], den[:, 0:4]))
                own.wait()
                for i in range(NT):
                    o = 129 * (i % 2)
                    ts(ob[:, i, P * h:P * h + P], bank[i // 2][:, o:o + P], den[:, i:i + 1], None, ALU.mult)\
                        .then_inc(S("ob_made"), 1)
                if h == 0:
                    head_var(0)
                elif h < 3:
                    head_norm(0, 2 * h - 2)
                    head_norm(0, 2 * h - 1)
            head_var(1)
            for i in range(NT):
                head_norm(1, i)
                mix_tile(2 * i)
                mix_tile(2 * i + 1)
            for f in range(8, 16):
                mix_tile(f)
            dve.wait_ge(S("x_first"), NT)
            for c in range(N_OUT2 // 2):
                for i in range(NT):
                    dve.wait_ge(S("out2_filled"), 4 * c + i + 1)
                    xs = x_res[:, i, 512 * c:512 * c + 512]
                    tt(out=xs, in0=xs, in1=bank[4 + i][:, :], op=ALU.add).then_inc(S("out2_added"), 1)
                    if c == 1 and i:
                        norm_var(dve, N4, i - 1)
            norm_scale(dve, own, N4)
            split_turn_dve(dve, "gffn")

            def weight_rests(c, n):
                for which in range(2):
                    dve.wait_ge(S("whi_made"), n + which)
                    w = slot(c + which)
                    tt(out=wlo[(c + which) % R], in0=w, in1=whi[(c + which) % R], op=ALU.subtract)\
                        .then_inc(S("wlo_made"), 1)

            def act_tile(f, f2, filled, silus):
                dve.wait_ge(S("up_filled"), filled)
                dve.wait_ge(S("fsilu_made"), silus)
                tt(out=f, in0=fsilu[f2], in1=bank[2 + f2][:, :], op=ALU.mult).then_inc(S("act_made"), 1)

            weight_rests(C_UP, 1)
            with dve.Fori(0, NFT // 4) as r:
                for q in range(4):
                    if q == 0:
                        weight_rests(C_UP + 2, r * 4 + 3)
                    if q == 2:
                        weight_rests(C_UP, r * 4 + 5)
                    act_tile(actT[:, bass.ds(r * 4 + q, 1), :].rearrange("p a t -> p (a t)"), q % 2,
                             r * 8 + (2 * q + 2), r * 4 + (q + 1))

            def down_rests(n, d):
                j = 6 * n + d
                if n == 0:
                    for k in range(4 * d, min(4 * d + 4, NFT)):
                        dve.wait_ge(S("ahi_made"), k + 1)
                        tt(out=alo[k], in0=actT[:, k, :], in1=ahi[k], op=ALU.subtract)\
                            .then_inc(S("alo_made"), 1)
                dve.wait_ge(S("whi_made"), NFT + j + 1)
                w = slot(C_DOWN + j)
                tt(out=wlo[(C_DOWN + j) % R], in0=w, in1=whi[(C_DOWN + j) % R], op=ALU.subtract)\
                    .then_inc(S("wlo_made"), 1)

            def add_down(n, i):
                xs = x_res[:, i, 512 * n:512 * n + 512]
                tt(out=xs, in0=xs, in1=bank[4 * (1 - n) + i][:, :], op=ALU.add).then_inc(S("down_added"), 1)

            down_rests(0, 0)
            for f in range(NFT // 4 * 4, NFT):
                act_tile(actT[:, f, :], f % 2, 2 * f + 2, f + 1)
            for j in range(1, 8):
                down_rests(j // 6, j % 6)
            dve.wait_ge(S("down_chunk"), 6)
            for i in range(NT):
                add_down(0, i)
            for j in range(8, 12):
                down_rests(j // 6, j % 6)
            dve.wait_ge(S("down_chunk"), 12)
            for i in range(NT):
                add_down(1, i)
                if i:
                    norm_var(dve, N5, i - 1)
            norm_scale(dve, own, N5)
            norm_turn_dve(dve, N5, "gple")
            dve.wait_ge(S("pw_made"), 8)
            for c in range(4):
                for i in range(NT):
                    u = 4 * c + i
                    dve.wait_ge(S("pg_copied"), u + 1)
                    g = tmp(u % 4)[:, 0:256]
                    own(tt(out=g, in0=g, in1=pw[:, i, 256 * c:256 * c + 256], op=ALU.mult))
                    own.wait()
                    xs = x_res[:, i, 256 * c:256 * c + 256]
                    tt(out=xs, in0=xs, in1=g, op=ALU.add).then_inc(S("pg_added"), 1)
                    if c == 3 and i:
                        norm_var(dve, NO, i - 1)
            dve.wait_ge(S("wg_in"), 48)
            for i in range(NT):
                if i == NT - 1:
                    norm_var(dve, NO, i)
                norm_rstd(dve, own, NO, i)
                stt(out=hn[:, i, :], in0=x_res[:, i, :], scalar=nstat[NO][:, i:i + 1], in1=grow, op0=ALU.mult,
                    op1=ALU.mult).then_inc(S("out_made"), 1)

        def second_act(act, own):
            fn = act.activation
            for i in range(NT + 1):
                for which in range(2):
                    t = i - which
                    if not 0 <= t < NT:
                        continue
                    if which == 0:
                        act.wait_ge(S("sc_added"), 8 * (NE - 1) + 2 * t + 4)
                    else:
                        act.wait_ge(S("xg_made"), t + 1)
                    sq = view(T0 + 10240 + 1024 * which, D)
                    if t:
                        act.wait_ge(S("norm_sq" if which else "first_sq"), t)
                    fn(sq, x_res[:, t, :], ACT.Square, accum_out=stat[:, 312 + 4 * which + t:313 + 4 * which + t])\
                        .then_inc(S("norm_sq" if which else "first_sq"), 1)
            act.wait_ge(S("norm_var"), NT)
            fn(r_both, r_both, ACT.Sqrt).then_inc(S("norm_sd"), NT)
            norm_turn_act(act, N3, "gmix2")
            act.wait_ge(S("r_made"), 1)
            for i in range(NT):
                act.wait_ge(S("norm_scaled"), i + 1)
                fn(x_res[:, i, :], x_res[:, i, :], ACT.Copy, scale=r_both[:, i:i + 1]).then_inc(S("x_first"), 1)
            act.wait_ge(S("gabs_made"), nth("gabs_made", 1))
            fn(beta, bank[0][:, 0:64].rearrange("p (i g) -> p i g", g=16)[:, :, 0:4], ACT.Sigmoid).then_inc(S("beta_made"), 1)
            act.wait_ge(S("rows_in"), 48)
            own(fn(ea, row("alog"), ACT.Exp))
            own(fn(gl_, gl_, ACT.Exp, scale=-1.0))
            own.wait()
            fn(gl_, gl_, ACT.Ln, bias=1.0).then_inc(S("glog_made"), 1)

            def conv_silu(u):
                act.wait_ge(S("cv_done"), u + 1)
                fn(qkv[:, u, :], qkv[:, u, :], ACT.Silu).then_inc(S("cv_silu"), 1)

            for u in range(12):
                ps = bank[1 + u % 4]
                act.wait_ge(S("qkv_filled"), u + 1)
                fn(qkv[:, u, :], ps[:, :], ACT.Copy, scale=col("cw3", u)).then_inc(S("qk_copied"), 1)
                if u >= 2:
                    conv_silu(u - 2)
            conv_silu(10)
            conv_silu(11)
            act.wait_ge(S("gc_filled"), nth("gc_filled", 1))
            fn(eg.rearrange("p n h -> p (n h)"), bank[0][:, 64:80], ACT.Exp).then_inc(S("eg_made"), 1)

            def aside_out(v):
                ps = bank[6 + v % 2]
                act.wait_ge(*((S("tok_filled"), v + 1) if v < 12 else (S("mqk_filled"), v - 11)))
                if v < 4:
                    last = fn(gz[:, v, :], ps[:, :], ACT.Silu)
                elif v < 8:
                    if v == 4:
                        act.wait_ge(S("mv_one"), 1)
                    last = fn(mv[:, v - 4, :].rearrange("p (h d) -> p h d", d=129)[:, :, 0:128],
                              ps[:, :].rearrange("p (h d) -> p h d", d=P), ACT.Copy)
                elif v < 12:
                    last = fn(mo[:, v - 8, :], ps[:, :], ACT.Sigmoid)
                elif v < 14:
                    m = v - 12
                    if m == 0:
                        act.wait_ge(S("mq_zero"), 1)
                    for hh in range(2):
                        q = slice(64 * hh, 64 * hh + 64)
                        last = fn(mqz[q, 2 * m + hh, :], ps[q, :], ACT.Copy, scale=MQ ** -0.5)
                        if hh == 0:
                            own(last)
                else:
                    last = fn(mk[:, v - 14, :], ps[:, :], ACT.Copy)
                last.then_inc(S("aside_copied"), 1)

            act.wait_ge(S("cv_silu"), 12)

            def l2_square(t):
                if t >= 2:
                    act.wait_ge(S("l2_filled"), t - 1)
                fn(tmp(t % 2), qkv[:, t, :], ACT.Square).then_inc(S("l2_sq"), 1)

            l2_square(0)
            l2_square(1)
            for t in range(8):
                act.wait_ge(S("l2_filled"), t + 1)
                if t >= 2:
                    act.wait_ge(S("l2_done"), t - 1)
                fn(tmp(2 + t % 2), bank[4 + t % 2][:, :], ACT.Sqrt, bias=EPS).then_inc(S("l2_sd"), 1)
                if t + 2 < 8:
                    l2_square(t + 2)
                if t % 2 == 1:
                    aside_out(t // 2)
            for n in range(4):
                act.wait_ge(S("gb_filled"), n + 1)
                if n:
                    act.wait_ge(S("prep_done"), n)
                act.wait_ge(S("dec_ready"), n + 1)
                fn(egb, bank[0][:, :], ACT.Exp).then_inc(S("dec_made"), 1)
                fn(dec, dec, ACT.Exp).then_inc(S("dec_made"), 1)
                fn(edec[:, n, :], edec[:, n, :], ACT.Exp).then_inc(S("dec_made"), 1)
                for v in ((4,), (5, 6), (7,), (8, 9))[n]:
                    aside_out(v)
            for n in range(4):
                act.wait_ge(S("t_filled"), n + 1)
                fn(tin[:, n, :], bank[4 + n % 2][:, :], ACT.Copy).then_inc(S("t_made"), 1)

            def x_out(u):
                n = u % 4
                act.wait_ge(S("x_filled"), u - 3)
                if u >= 6:
                    act.wait_ge(S("tc_filled"), u - 5)
                fn(xw[n % 2], bank[n % 2][:, :], ACT.Copy).then_inc(S("x_made"), 1)

            x_out(4)
            for u in range(4, 28):
                n = u % 4
                if u < 27:
                    x_out(u + 1)
                if u < 24:
                    act.wait_ge(S("t_filled"), u + 1)
                    fn(tin[:, n, :], bank[4 + n % 2][:, :], ACT.Copy).then_inc(S("t_made"), 1)
                if u % 4 == 2:
                    aside_out(10 + (u - 6) // 4)

            def gate_out(f):
                b = bank[(4 + f % 2) if f < 4 else (7, 2)[f % 2]]
                act.wait_ge(S("sg_filled"), f + 1)
                fn(sg[f], b[:, :], ACT.Sigmoid).then_inc(S("sg_made"), 1)

            for n in range(4):
                act.wait_ge(S("w_filled"), n + 1)
                fn(wneg[:, n, :], bank[6][:, :], ACT.Copy, scale=-1.0).then_inc(S("w_made"), 1)
            for n in range(4):
                act.wait_ge(S("oa_filled"), n + 1)
                fn(oa[:, n, :], bank[n % 2][:, :], ACT.Copy).then_inc(S("oa_made"), 1)
                gate_out(n)
            gate_out(4)
            act.wait_ge(S("mcol_filled"), nth("mcol_filled", 1))
            fn(emcol.rearrange("p i h -> p (i h)"), bank[2][:, 16:32], ACT.Exp, scale=-1.0).then_inc(S("em_made"), 1)

            def head_squares(br):
                if br:
                    act.wait_ge(S("ob_made"), 16)
                    act.wait_ge(S("ovar_made"), nth("ovar_made", 1))
                else:
                    act.wait_ge(S("oa_made"), 4)
                fn(view(B + 8192, 2048), (oa, ob)[br].rearrange("p i d -> p (i d)"), ACT.Square).then_inc(S("osq_made"), 1)

            def head_roots(br):
                act.wait_ge(S("ovar_made"), nth("ovar_made", br + 1))
                hs = hstat[:, 16 * br:16 * br + 16]
                fn(hs, hs, ACT.Sqrt).then_inc(S("osd_made"), 1)

            def turned_out(u):
                act.wait_ge(S("oT_filled"), u + 1)
                fn((oTa, oTb)[u // 4][:, u % 4, :], bank[4 + u % 2][:, :], ACT.Copy).then_inc(S("oT_made"), 1)

            for h in range(MH):
                act.wait_ge(S("mx_made"), 4 * h + 4)
                fn(expo, expo, ACT.Exp, scale=-1.0).then_inc(S("me_made"), 1)
                if h == 1:
                    head_roots(0)
                gate_out(5 + 2 * h)
                if h == 0:
                    head_squares(0)
                gate_out(6 + 2 * h)
            for u in range(4):
                turned_out(u)
            head_squares(1)
            head_roots(1)
            for f in range(13, 16):
                gate_out(f)
            for u in range(4, 8):
                turned_out(u)
            norm_squares(act, N4, "out2_added", lambda i: 5 + i)
            split_turn_act(act, "gffn")

            def round_weights(c, loads):
                for which in range(2):
                    act.wait_ge(S(f"chunk_in{(c + which) % R}"), loads * 16)
                    fn(whi[(c + which) % R], slot(c + which), ACT.Copy).then_inc(S("whi_made"), 1)

            def up_silu(f2, filled, made):
                act.wait_ge(S("up_filled"), filled)
                act.wait_ge(S("act_made"), made)
                fn(fsilu[f2], bank[f2][:, :], ACT.Silu).then_inc(S("fsilu_made"), 1)

            round_weights(C_UP, C_UP // R + 1)
            with act.Fori(0, NFT // 4) as r:
                for q in range(4):
                    if q == 0:
                        round_weights(C_UP + 2, r + ((C_UP + 2) // R + 1))
                    if q == 2:
                        round_weights(C_UP, r + (C_UP // R + 2))
                    up_silu(q % 2, r * 8 + (2 * q + 1), r * 4 + (q + 1))

            def round_down(n, d):
                j = 6 * n + d
                if n == 0:
                    for k in range(4 * d, min(4 * d + 4, NFT)):
                        act.wait_ge(S("act_made"), k + 3)
                        if k == 14:
                            act.wait_ge(S("up_filled"), 2 * NFT)
                        fn(ahi[k], actT[:, k, :], ACT.Copy).then_inc(S("ahi_made"), 1)
                c = C_DOWN + j
                act.wait_ge(S(f"chunk_in{c % R}"), 16 * (c // R + 1))
                fn(whi[c % R], slot(c), ACT.Copy).then_inc(S("whi_made"), 1)

            round_down(0, 0)
            for f in range(NFT // 4 * 4, NFT):
                up_silu(f % 2, 2 * f + 1, f + 1)
            for j in range(1, 12):
                round_down(j // 6, j % 6)
            norm_squares(act, N5, "down_added", lambda i: 5 + i)
            act.wait_ge(S("down_chunk"), 12)
            for u in range(8):
                i, n = u // 2, u % 2
                act.wait_ge(S("ple_filled"), u + 1)
                fn(pw[:, i, 512 * n:512 * n + 512], bank[4 + u % 4][:, :], ACT.Copy).then_inc(S("pw_made"), 1)
            norm_turn_act(act, N5, "gple")
            for c in range(4):
                for i in range(NT):
                    u = 4 * c + i
                    act.wait_ge(S("pg_filled"), u + 1)
                    if u >= 4:
                        act.wait_ge(S("pg_added"), u - 3)
                    fn(tmp(u % 4)[:, 0:256], bank[i][:, 0:256], ACT.Sigmoid).then_inc(S("pg_copied"), 1)
            norm_squares(act, NO, "pg_added", lambda i: 13 + i)

        wpack = A["wpack"]

        @block.sync
        def _(sp):
            def chunk(c):
                if c >= R:
                    name, v = used[c - R]
                    sp.wait_ge(S(name), v)
                sp.dma_start(slot(c), wpack[c]).then_inc(S(f"chunk_in{c % R}"), 16)

            xT = A["xT"].rearrange("(k p) t -> p k t", p=P)
            sp.dma_start(hT[:, 0:4, :], xT[:, 0:4]).then_inc(S("xT_in0"), 16)
            sp.dma_start(view(8192, 3 * P + P), A["consts"]).then_inc(S("cols_in"), 16)
            sp.dma_start(hT[:, 4:8, :], xT[:, 4:8]).then_inc(S("xT_in1"), 16)
            sp.dma_start(cols[:, 0:N_COLS], A["cols"]).then_inc(S("cols_in"), 16)
            chunk(0)
            chunk(1)
            chunk(2)
            chunk(3)
            for c in range(4, C_OUT1):
                chunk(c)
            sp.wait_ge(S("proj_filled"), 20)
            sp.dma_start(x_res, A["x"].rearrange("(i p) d -> p i d", p=P)).then_inc(S("x_in"), 16)
            for i in range(3):
                sp.wait_ge(S("proj_copied"), 16 + i + 2)
                sp.dma_start(vb_[0:64, i, :], va[64:P, i, :]).then_inc(S("vb_in"), 16)
                sp.dma_start(vb_[64:P, i, :], va[0:64, i + 1, :]).then_inc(S("vb_in"), 16)
            for c in range(C_OUT1, C_QKV):
                chunk(c)

            g_v = A["w_gate"].rearrange("e (k p) (c n) -> e c p k n", p=P, n=FC)
            u_v = A["w_up"].rearrange("e (k p) (c n) -> e c p k n", p=P, n=FC)
            d_v = A["w_down"].rearrange("e (c k p) n -> e c p k n", p=P, k=FC // P)

            def expert_chunk(e, c):
                s = 3 * (c % 2)
                sp.dma_start(mslot[s].rearrange("p (k n) -> p k n", n=FC), g_v[e, c]).then_inc(S(f"ew_in{s}"), 16)
                sp.dma_start(mslot[s + 1].rearrange("p (k n) -> p k n", n=FC), u_v[e, c]).then_inc(S(f"ew_in{s + 1}"), 16)

            def expert_down(e, c):
                s = 3 * (c % 2) + 2
                sp.dma_start(mslot[s].rearrange("p (k n) -> p k n", n=D), d_v[e, c]).then_inc(S(f"ew_in{s}"), 16)

            sp.wait_ge(S("out1_filled"), 8)
            for c in range(2):
                expert_chunk(0, c)
                expert_down(0, c)

            def refill(e, steps):
                for kind, c in steps:
                    if kind == "u":
                        sp.wait_ge(S("ab_filled"), e * NFC + (c + 1))
                        expert_chunk(e + (c + 2) // NFC, (c + 2) % NFC)
                    else:
                        sp.wait_ge(S("y_part"), e * NFC + (c + 1))
                        expert_down(e + (c + 2) // NFC, (c + 2) % NFC)

            with sp.Fori(0, NE - 1) as e:
                refill(e, (("u", 0), ("u", 1), ("d", 0), ("u", 2), ("d", 1), ("u", 3), ("d", 2), ("d", 3)))
            refill(NE - 1, (("u", 0), ("u", 1), ("d", 0), ("d", 1)))

            sp.wait_ge(S("y_part"), NE * NFC)
            sp.dma_start(wg, A["w_gates"].rearrange("(k p) n -> p k n", p=P)).then_inc(S("wg_in"), 16)
            for c in range(C_QKV, N_CHUNKS):
                if c >= C_QKV + R:
                    name, v = used[c - R]
                    sp.wait_ge(S(name), v)
                sp.dma_start(slot(c), wpack[c]).then_inc(S(f"chunk_in{c % R}"), 16)
                if c == C_DOWN:
                    sp.dma_start(view(B + 15360, 2, L), A["pT"].rearrange("(k p) t -> p k t", p=P)).then_inc(S("wg_in"), 16)
                    sp.dma_start(grow, A["gfin"].partition_broadcast(P)).then_inc(S("wg_in"), 16)
            for i in range(NT):
                sp.wait_ge(S("out_made"), i + 1)
                sp.dma_start(out.rearrange("a (i p) d -> i p (a d)", p=P)[i], hn[:, i, :]).then_inc(S("stored"), 16)
            sp.wait_ge(S("stored"), 16 * NT)

        @block.gpsimd
        def _(pool):
            own = Own(pool, "pool_own")
            pool.dma_start(pos, A["pos"]).then_inc(S("fnet_in"), 16)
            pool.dma_start(fw1, A["fw1"]).then_inc(S("fnet_in"), 16)
            pool.dma_start(fw2, A["fw2"]).then_inc(S("fnet_in"), 16)
            pool.dma_start(fwo, A["fwo"]).then_inc(S("fnet_in"), 16)
            pool.dma_start(decay[:, 0, :], A["deltas"].partition_broadcast(P)).then_inc(S("fnet_in"), 16)
            pool.dma_start(rows, A["rows"].partition_broadcast(P)).then_inc(S("rows_in"), 16)
            pool.dma_start(invc, A["invc"]).then_inc(S("rows_in"), 16)
            pool.dma_start(pwbd, A["pwbd"].rearrange("a p d -> p a d")).then_inc(S("rows_in"), 16)
            pool.memset(qz, 0.0).then_inc(S("qz_zero"), 1)
            mask = stat[:, 0:3 * KC].rearrange("p (a b) -> p a b", b=KC)
            pool.dma_start(mask, A["mask"]).then_inc(S("mask_in"), 16)
            for c in range(QC):
                pool.dma_start(table[ROWS * c:ROWS * (c + 1)], A["rpbw"][:, :, QC - 1 - c:QC - 1 - c + TABW])\
                    .then_inc(S("table_in"), 16)
            pool.wait_ge(S("table_in"), 16 * QC)
            pool.wait_ge(S("mask_in"), 16)
            for a in range(3):
                w0 = 16 + KOFF[a]
                for h in range(NH):
                    src = table[:, ROWS * h:ROWS * (h + 1), w0:w0 + KC].rearrange("p r c -> p c r")
                    dst = bias[:, a, NKEY * h:NKEY * (h + 1)].rearrange("p (c r) -> p c r", r=ROWS)
                    m = mask[:, a, :].unsqueeze(2).to_broadcast([P, KC, ROWS])
                    pool.tensor_tensor(out=dst, in0=src, in1=m, op=ALU.add).then_inc(S("bias_made"), 1)
            pool.wait_ge(S("hT_ready"), KD)
            for j in range(NT):
                src = hT.rearrange("p k (r c) -> p k c r", c=GW)[:, :, QC * j:QC * j + QC, :]
                pool.tensor_copy(hperm[:, j, :].rearrange("p (k c r) -> p k c r", k=KD, r=ROWS), src)\
                    .then_inc(S("hp_made"), 1)
            pool.wait_ge(S("bias_made"), 3 * NH)
            pool.dma_start(cosm, A["cosm"].rearrange("(i p) k -> p i k", p=P)).then_inc(S("four_in"), 16)
            pool.dma_start(sinm, A["sinm"].rearrange("(i p) k -> p i k", p=P)).then_inc(S("four_in"), 16)
            pool.wait_ge(S("filt_made"), nth("filt_made", NT))
            pool.memset(pu[:, :, 0:16], 0.0).then_inc(S("pu_zero"), 1)
            pool.memset(pu[:, :, 16 + L:PADW], 0.0).then_inc(S("pu_zero"), 1)
            pool.wait_ge(S("proj_copied"), 16)
            pool.wait_ge(S("pu_zero"), 2)
            mid = slice(16, 16 + L)
            for m in range(2):
                u = pu[:, m, :]
                chain = [(p2, u, 1, 0, 1), (p4, p2, 2, 1, 1), (p8, p4, 4, 2, 2), (p2, p8, 8, 4, 4)]
                if m == 1:
                    own.wait()
                for n, (dst, src, lo, back, fore) in enumerate(chain[:2 if m == 0 else 4]):
                    hi = PADW - (0, 1, 3, 7)[n]
                    if n == 0:
                        a, b = src[:, 0:PADW - 1], src[:, 1:PADW]
                    else:
                        a, b = src[:, lo - back:hi - back], src[:, lo + fore:hi + fore]
                    own(pool.tensor_tensor(out=dst[:, lo:hi], in0=a, in1=b, op=ALU.add))
                    own.wait()
                halves = [(0, p2), (64, p4)] if m == 0 else [(0, p8), (64, p2)]
                if m == 0:
                    pool.wait_ge(S("rows_in"), 48)
                for p0, s in halves:
                    q = slice(p0, p0 + 64)
                    own(pool.tensor_tensor(out=pooled[q, m, :], in0=s[q, mid], in1=invc[q, m, :], op=ALU.mult))
                own.wait()
                pool.tensor_tensor(out=pooled[:, m, :], in0=pooled[:, m, :], in1=u[:, mid], op=ALU.subtract)\
                    .then_inc(S("pooled_made"), 1)
            pool.wait_ge(S("pooled_made"), 2)
            pool.dma_start(grow, A["g2"].partition_broadcast(P)).then_inc(S("g2_in"), 16)
            pool.wait_ge(S("s_made"), 16)
            pool.dma_start(wr, A["w_router"].rearrange("(k p) e -> p k e", p=P)).then_inc(S("wr_in"), 16)
            pool.dma_start(iota, A["iota"].partition_broadcast(P)).then_inc(S("wr_in"), 16)
            pool.wait_ge(S("h2_made"), NT)
            pool.dma_start(grow, A["gfirst"].partition_broadcast(P)).then_inc(S("gfirst_in"), 16)
            pool.wait_ge(S("onehot_made"), NT)
            oh = onehot.rearrange("p i (e s) -> p i e s", s=CAP)

            def weigh_choice(e):
                for half in range(2):
                    pool.tensor_tensor(out=pg[:, :, 64 * half:64 * half + 64],
                                       in0=oh[:, :, bass.ds(e, 1), :].rearrange("p i e s -> p i (e s)"),
                                       in1=aff[:, :, bass.ds(e, 1)].to_broadcast([P, NT, CAP]), op=ALU.mult)\
                        .then_inc(S("pg_made"), 1)

            weigh_choice(0)
            pool.wait_ge(S("onehot_made"), 2 * NT)
            with pool.Fori(1, NE) as e:
                pool.wait_ge(S("gt_filled"), e)
                weigh_choice(e)
            second_pool(pool)


        @block.tensor
        def _(pe):
            mm = nc.tensor.matmul
            turn = nc.tensor.transpose
            pe.wait_ge(S("cols_in"), 32)
            for k in range(KD):
                pe.wait_ge(S("sq1_made"), nth("sq1_made", k + 1))
                mm(bank[0][:, :], ones, hyt[:, k % 2, :], start=k == 0, stop=k == KD - 1).then_inc(S("sq1_summed"), 1)
            pe.wait_ge(S("fnet_in"), 16 * 5)
            mm(bank[1][:, :], fw1, pos, start=True, stop=True).then_inc(S("net1_filled"), 1)

            def proj(u):
                if u % 2 == 0:
                    wait_chunk(pe, u // 2)
                if u >= 4:
                    pe.wait_ge(S("conv_done" if u - 4 < 6 else "proj_copied"), u - 3)
                w = slot(u // 2).rearrange("p (k n) -> p k n", n=256)
                for k in range(KD):
                    if u == 0:
                        pe.wait_ge(S("hT_ready"), k + 1)
                    last = mm(bank[2 + u % 4][:, :], w[:, k, P * (u % 2):P * (u % 2) + P], hT[:, k, :],
                              start=k == 0, stop=k == KD - 1)
                last.then_inc(S("proj_filled"), 1)

            for u in range(4):
                proj(u)
            pe.wait_ge(S("fh_made"), nth("fh_made", 1))
            mm(bank[1][:, :], fw2, fh, start=True, stop=True).then_inc(S("net2_filled"), 1)
            for u in range(4, 10):
                proj(u)
            pe.wait_ge(S("fh_made"), nth("fh_made", 2))
            for i in range(NT):
                if i >= 2:
                    pe.wait_ge(S("filt_made"), nth("filt_made", i - 1))
                mm(bank[6 + i % 2][:, :], fh[:, P * i:P * i + P], fwo, start=True, stop=True)\
                    .then_inc(S("filt_filled"), 1)
            pe.wait_ge(S("z_made"), nth("z_made", 2))
            for i in range(NT):
                if i >= 2:
                    pe.wait_ge(S("z_copied"), nth("z_copied", i - 1))
                for m in range(2):
                    last = turn(bank[i % 2][:, P * m:P * m + P], hz[:, m, P * i:P * i + P], ident)
                last.then_inc(S("z_turned"), 1)
            for u in range(10, 16):
                proj(u)
            for j in range(NT):
                if j == 0:
                    wait_chunk(pe, 8)
                    wait_chunk(pe, 9)
                pe.wait_ge(S("proj_copied"), 13 + j)
                pe.wait_ge(S("hp_made"), j + 1)
                w = slot_pair(8)
                for k in range(KD):
                    last = mm(bank[2 + j][:, :], hperm[:, j, P * k:P * k + P], w[:, :, k, :],
                              start=k == 0, stop=k == KD - 1)
                last.then_inc(S("proj_filled"), 1)
            pe.wait_ge(S("four_in"), 32)
            pe.wait_ge(S("pq_made"), nth("pq_made", 2))
            pe.wait_ge(S("z_copied"), nth("z_copied", NT))
            for f in range(NT):
                if f >= 2:
                    pe.wait_ge(S("ywf_made"), f - 1)
                b = (6, 0)[f % 2]
                for i in range(NT):
                    mm(bank[b][:, :], cosm[:, i, P * f:P * f + P], zqp[:, i, 0:512], start=i == 0, stop=i == NT - 1)
                for i in range(NT):
                    last = mm(bank[b + 1][:, :], sinm[:, i, P * f:P * f + P], zqp[:, i, 256:768],
                              start=i == 0, stop=i == NT - 1)
                    if f == 0 and i == 0:
                        for n in range(NT):
                            mm(bank[b + 1][0:1, 256:512], col("alt2"), filt[:, n, 256:512], start=False, stop=False)
                last.then_inc(S("four_filled"), 1)
            pe.wait_ge(S("pooled_made"), 2)
            pe.wait_ge(S("rows_in"), 48)
            pe.wait_ge(S("proj_copied"), 20)
            for m in range(2):
                mm(bank[2 + m][:, :], pwbd[:, m, :], pooled[:, m, :], start=True, stop=True)\
                    .then_inc(S("pmix_filled"), 1)
            pe.wait_ge(S("ywf_made"), NT)
            pe.wait_ge(S("sin_turned"), 3)
            for m in range(2):
                for f in range(NT):
                    mm(bank[4 + m][:, :], ywf[:, f, P * m:P * m + P], cosm[:, f, :], start=f == 0, stop=False)
                    last = mm(bank[4 + m][:, :], ywf[:, f, 256 + P * m:256 + P * m + P], sinm[:, f, :],
                              start=False, stop=f == NT - 1)
                last.then_inc(S("yhy_filled"), 1)

            def scores(n):
                j, m = divmod(n, 4)
                if n == 2:
                    pe.wait_ge(S("hsq_made"), nth("hsq_made", 2))
                if n >= 3:
                    pe.wait_ge(S("s_made"), n - 2)
                for hh in range(2):
                    last = mm(sbank[n % 3][:, NKEY * hh:NKEY * hh + NKEY], qz[:, 2 * m + hh, P * j:P * j + P],
                              kT[:, m, ROWS * KSTART[j]:ROWS * KSTART[j] + NKEY], start=True, stop=True)
                last.then_inc(S("s_filled"), 1)

            def turn_weights(n):
                pe.wait_ge(S("p_made"), 2 * n + 2)
                if n >= 2:
                    pe.wait_ge(S("pt_copied"), n - 1)
                for a in range(4):
                    last = turn(bank[n % 2][:, P * a:P * a + P], sc[n % 3][:, P * a:P * a + P], ident)
                last.then_inc(S("pt_filled"), 1)

            def channel_sums(q):
                for m in range(2):
                    sq = hyt[:, m, :] if q == 0 else ywf[:, m, :]
                    last = mm(bank[5][:, :], ones, sq, start=m == 0, stop=m == 1)
                last.then_inc(S("hsum_filled"), 1)

            pe.wait_ge(S("qz_zero"), 1)
            scores(0)
            scores(1)
            scores(2)
            turn_weights(0)
            for n in range(16):
                j, m = divmod(n, 4)
                if n < 13:
                    scores(n + 3)
                if n < 15:
                    turn_weights(n + 1)
                if n == 0:
                    pe.wait_ge(S("pmix_copied"), nth("pmix_copied", 2))
                    pe.wait_ge(S("vb_in"), 16 * 6)
                if m == 0 and j >= 2:
                    pe.wait_ge(S("o_made"), j - 1)
                pe.wait_ge(S("pt_copied"), n + 1)
                off = ROWS * KSTART[j]
                for hh in range(2):
                    h = 2 * m + hh
                    for a in range(2):
                        v = va[:, off // P + a, :] if off % P == 0 else vb_[:, off // P + a, :]
                        last = mm(bank[2 + j % 2][:, HD * h:HD * h + HD], pt[n % 3][:, P * (2 * hh + a):P * (2 * hh + a) + P],
                                  v[:, HD * h:HD * h + HD], start=a == 0, stop=a == 1)
                last.then_inc(S("pv_filled"), 1)
                if n == 3:
                    channel_sums(0)
                if n == 9:
                    pe.wait_ge(S("hvar_made"), nth("hvar_made", 1))
                    pe.wait_ge(S("psq_made"), nth("psq_made", 2))
                    channel_sums(1)
            pe.wait_ge(S("on_made"), NT)
            for m in range(4):
                if m >= 2:
                    pe.wait_ge(S("ot_copied"), nth("ot_copied", m - 1))
                for j in range(NT):
                    last = turn(bank[6 + m % 2][:, P * j:P * j + P], ona[:, j, P * m:P * m + P], ident)
                last.then_inc(S("ot_filled"), 1)
            pe.wait_ge(S("ot_copied"), nth("ot_copied", 4))
            pe.wait_ge(S("mix_made"), 4)
            for c in range(N_OUT1 // 2):
                wait_chunk(pe, C_OUT1 + 2 * c)
                wait_chunk(pe, C_OUT1 + 2 * c + 1)
                w = slot_pair(C_OUT1 + 2 * c)
                for i in range(NT):
                    u = 4 * c + i
                    if u >= 4:
                        pe.wait_ge(S("out1_added"), u - 3)
                    for k in range(KD):
                        last = mm(bank[i][:, :], mixT[:, k, P * i:P * i + P], w[:, :, k, :], start=k == 0, stop=k == KD - 1)
                    last.then_inc(S("out1_filled"), 1)
            pe.wait_ge(S("out1_added"), 8)
            for k in range(KD):
                if k >= 2:
                    pe.wait_ge(S("h2t_a" if k % 2 == 0 else "h2t_v"), k // 2)
                for i in range(NT):
                    last = turn(bank[4 + k % 2][:, P * i:P * i + P], x_res[:, i, P * k:P * k + P], ident)
                last.then_inc(S("h2_turned"), 1)
            pe.wait_ge(S("h2t_a"), 4)
            pe.wait_ge(S("h2t_v"), 4)
            pe.wait_ge(S("wr_in"), 32)
            for i in range(NT):
                for k in range(KD):
                    last = mm(bank[6][:, NE * i:NE * i + NE], hT[:, k, P * i:P * i + P], wr[:, k, :],
                              start=k == 0, stop=k == KD - 1)
            last.then_inc(S("lg_filled"), 1)
            pe.wait_ge(S("aff_made"), nth("aff_made", 1))
            for i in range(NT):
                last = turn(bank[7][0:NE, P * i:P * i + P], aff[:, i, :], ident)
            last.then_inc(S("aff_turned"), 1)
            pe.wait_ge(S("rank_made"), nth("rank_made", 1))
            for i in range(NT):
                last = turn(bank[6][:, NE * i:NE * i + NE], rank[0:NE, P * i:P * i + P], ident[0:NE, 0:NE])
            last.then_inc(S("rank_turned"), 1)

            pe.wait_ge(S("h2_made"), NT)
            pe.wait_ge(S("onehot_made"), NT)
            pe.sem_inc(S("hid_turned"), 2)

            def gather(e):
                for k in range(KD):
                    for i in range(NT):
                        last = mm(bank[3][:, CAP * k:CAP * k + CAP], h2[:, i, P * k:P * k + P],
                                  onehot[:, i, bass.ds(e * CAP, CAP)], start=i == 0, stop=i == NT - 1)
                last.then_inc(S("xs_filled"), 1)

            def scatter(e, us):
                for u in us:
                    i, n = u // 2, u % 2
                    pe.wait_ge(S("sc_added"), e * 8 + (u - 7))
                    mm(bank[6 + u % 2][:, :], gt[:, P * i:P * i + P], ysb[:, 512 * n:512 * n + 512], start=True, stop=True)\
                        .then_inc(S("sc_filled"), 1)

            def expert(e, first=False, final=False):
                def gate_up(c):
                    ab = bank[c % 2]
                    pe.wait_ge(S("h_made"), e * NFC + (c + 1))
                    for which in range(2):
                        s = 3 * (c % 2) + which
                        pe.wait_ge(S(f"ew_in{s}"), e * 32 + 16 * (c // 2 + 1))
                        w = mslot[s].rearrange("p (k n) -> p k n", n=FC)
                        for k in range(KD):
                            for half in range(2):
                                last = mm(ab[64 * half:64 * half + 64, 256 * which:256 * which + 256], xsT[:, k, :],
                                          w[:, k, 256 * half:256 * half + 256], start=k == 0, stop=k == KD - 1)
                    last.then_inc(S("ab_filled"), 1)

                def turn_hidden(c):
                    pe.wait_ge(S("h_made"), e * NFC + (c + 3))
                    if not (first and c == 0):
                        pe.wait_ge(S("hidT_made"), e * NFC + c)
                    for t in range(2):
                        last = turn(bank[2][:, 256 * (c % 2) + P * t:256 * (c % 2) + P * t + P],
                                    hid[c % 2][:, P * t:P * t + P], ident)
                    last.then_inc(S("hid_turned"), 1)

                def down(c):
                    s = 3 * (c % 2) + 2
                    pe.wait_ge(S(f"ew_in{s}"), e * 32 + 16 * (c // 2 + 1))
                    pe.wait_ge(S("hidT_made"), e * NFC + (c + 1))
                    w = mslot[s].rearrange("p (k n) -> p k n", n=D)
                    for t in range(2):
                        for n in range(2):
                            for half in range(2):
                                last = mm(bank[4 + n][64 * half:64 * half + 64, :],
                                          hidT[c % 2][:, P * t + 64 * half:P * t + 64 * half + 64],
                                          w[:, 2 * half + t, 512 * n:512 * n + 512],
                                          start=(c == 0 and t == 0), stop=(c == NFC - 1 and t == 1))
                    last.then_inc(S("y_part"), 1)

                pe.wait_ge(S("xs_made"), e + 1)
                gate_up(0)
                gate_up(1)
                turn_hidden(0)
                if not first:
                    pe.wait_ge(S("gt_made"), e)
                    pe.wait_ge(S("y_copied"), e * 2)
                    scatter(e, range(4))
                down(0)
                turn_hidden(1)
                if not first:
                    scatter(e, range(4, 8))
                gate_up(2)
                down(1)
                turn_hidden(2)
                gate_up(3)
                down(2)
                turn_hidden(3)
                pe.wait_ge(S("pg_made"), e * 2 + 2)
                pe.wait_ge(S("sc_added"), e * 8 + 1)
                for i in range(NT):
                    last = turn(bank[6][:, P * i:P * i + P], pg[:, i, :], ident)
                last.then_inc(S("gt_filled"), 1)
                if not final:
                    gather(e + 1)
                down(3)

            gather(0)
            pe.wait_ge(S("onehot_made"), 2 * NT)
            expert(0, first=True)
            with pe.Fori(1, NE - 1) as e:
                expert(e)
            expert(NE - 1, final=True)
            pe.wait_ge(S("gt_made"), NE)
            pe.wait_ge(S("y_copied"), NE * 2)
            scatter(NE, range(8))
            second_pe(pe, mm, turn)

        def two_pi_fold(dve, own, src, bcol, n):
            own(dve.tensor_scalar(fa, src, col(bcol), col("freq"), ALU.add, ALU.mult))
            own.wait()
            own(dve.tensor_scalar(fk, fa, 1.0 / (2 * np.pi), MAGIC, ALU.mult, ALU.add))
            own.wait()
            own(dve.tensor_scalar(fk, fk, MAGIC, None, ALU.subtract))
            own.wait()
            own(dve.scalar_tensor_tensor(out=fa, in0=fk, scalar=-TWO_PI_HI, in1=fa, op0=ALU.mult, op1=ALU.add))
            own.wait()
            own(dve.scalar_tensor_tensor(out=fa, in0=fk, scalar=-TWO_PI_LO, in1=fa, op0=ALU.mult, op1=ALU.add))
            own.wait()
            dve.tensor_scalar(fa, fa, PI, -PI, ALU.min, ALU.max).then_inc(S("angle_made"), 1)

        @block.vector
        def _(dve):
            own = Own(dve, "dve_own")
            stt = dve.scalar_tensor_tensor
            tt = dve.tensor_tensor
            ts = dve.tensor_scalar
            for k in range(KD):
                if k % 4 == 0:
                    dve.wait_ge(S(f"xT_in{k // 4}"), 16)
                if k >= 2:
                    dve.wait_ge(S("sq1_summed"), k - 1)
                tt(out=hyt[:, k % 2, :], in0=hT[:, k, :], in1=hT[:, k, :], op=ALU.mult).then_inc(S("sq1_made"), 1)
            dve.wait_ge(S("sq1_summed"), KD)
            ts(hyt[:, 0, :], bank[0][:, :], 1.0 / D, EPS, ALU.mult, ALU.add).then_inc(S("var1_made"), 1)
            dve.wait_ge(S("sd1_made"), nth("sd1_made", 1))
            own(dve.reciprocal(hyt[:, 1, :], hyt[:, 0, :]))
            own.wait()
            for k in range(KD):
                if k == 0:
                    dve.wait_ge(S("cols_in"), 32)
                stt(out=hT[:, k, :], in0=hT[:, k, :], scalar=col("norm1", k), in1=hyt[:, 1, :], op0=ALU.mult, op1=ALU.mult)\
                    .then_inc(S("hT_ready"), 1)
            dve.wait_ge(S("net1_filled"), nth("net1_filled", 1))
            two_pi_fold(dve, own, bank[1][:, :], "fb1", 1)
            for u in range(6):
                dve.wait_ge(S("proj_copied"), u + 1)
                ps = bank[2 + u % 4]
                own(stt(out=hyu[:, u, 1:L], in0=ps[:, 0:L - 1], scalar=col("hw0", u), in1=hyu[:, u, 1:L],
                        op0=ALU.mult, op1=ALU.add))
                own.wait()
                stt(out=hyu[:, u, 0:L - 1], in0=ps[:, 1:L], scalar=col("hw2", u), in1=hyu[:, u, 0:L - 1],
                    op0=ALU.mult, op1=ALU.add).then_inc(S("conv_done"), 1)
            dve.wait_ge(S("net2_filled"), nth("net2_filled", 1))
            dve.wait_ge(S("fh_made"), nth("fh_made", 1))
            two_pi_fold(dve, own, bank[1][:, :], "fb2", 2)
            dve.wait_ge(S("conv_done"), 6)
            for m in range(2):
                tt(out=hz[:, m, :], in0=hyu[:, 4 + m, :], in1=hyu[:, 2 + m, :], op=ALU.mult).then_inc(S("z_made"), 1)
            dve.wait_ge(S("decay_made"), nth("decay_made", NT))
            for i in range(NT):
                dve.wait_ge(S("filt_filled"), nth("filt_filled", i + 1))
                own(tt(out=filt[:, i, 0:256], in0=bank[6 + i % 2][:, 0:256], in1=decay[:, i, :], op=ALU.mult))
                tt(out=filt[:, i, 256:512], in0=bank[6 + i % 2][:, 256:512], in1=decay[:, i, :], op=ALU.mult)\
                    .then_inc(S("filt_made"), 1)
            dve.wait_ge(S("filt_made"), nth("filt_made", NT))
            own(dve.memset(filt[0:1, 0, 256:512], 0.0))
            own.wait()
            tt(out=zqp[:, :, 0:256], in0=filt[:, :, 0:256], in1=filt[:, :, 256:512], op=ALU.add).then_inc(S("pq_made"), 1)
            tt(out=zqp[:, :, 512:768], in0=filt[:, :, 0:256], in1=filt[:, :, 256:512], op=ALU.subtract)\
                .then_inc(S("pq_made"), 1)
            for f in range(NT):
                b = (6, 0)[f % 2]
                dve.wait_ge(S("rs_made"), nth("rs_made", 2 * f + 2))
                zr, zs = bank[b][:, 256:512], bank[b + 1][:, 0:256]
                for o, x, y in ((0, zr, 0), (1, zs, 256), (2, zr, 256), (3, zs, 0)):
                    own(tt(out=pr[o], in0=x, in1=rs[:, y:y + 256], op=ALU.mult))
                own.wait()
                n = own(tt(out=ywf[:, f, 0:256], in0=pr[0], in1=pr[1], op=ALU.subtract))
                if f == 0:
                    own.wait()
                    own(dve.tensor_copy(ywf[0:1, 0, 0:256], pr[0][0:1, :]))
                    own(tt(out=ywf[:, f, 256:512], in0=pr[2], in1=pr[3], op=ALU.add))
                    own.wait()
                    dve.tensor_copy(ywf[0:1, 0, 256:512], pr[1][0:1, :]).then_inc(S("ywf_made"), 1)
                else:
                    tt(out=ywf[:, f, 256:512], in0=pr[2], in1=pr[3], op=ALU.add).then_inc(S("ywf_made"), 1)
                dve.wait_ge(S("ywf_made"), f + 1)
            dve.wait_ge(S("four_filled"), nth("four_filled", NT))
            dve.memset(sinm[:, :, 0:1], 0.0).then_inc(S("sin_turned"), 1)
            dve.wait_ge(S("sin_turned"), 1)
            alt = sinm[0:1, 0, :].rearrange("p (n a) -> p n a", a=2)
            dve.memset(alt[:, :, 0], 1.0).then_inc(S("sin_turned"), 1)
            dve.memset(alt[:, :, 1], -1.0).then_inc(S("sin_turned"), 1)
            for m in range(2):
                dve.wait_ge(S("yhy_filled"), nth("yhy_filled", m + 1))
                own(stt(out=hz[:, m, :], in0=hz[:, m, :], scalar=col("skip", m), in1=bank[4 + m][:, :],
                        op0=ALU.mult, op1=ALU.add))
                own.wait()
                own(tt(out=hyu[:, m, :], in0=hz[:, m, :], in1=hyu[:, m, :], op=ALU.mult))
                own.wait()
                tt(out=hyt[:, m, :], in0=hyu[:, m, :], in1=hyu[:, m, :], op=ALU.mult).then_inc(S("hsq_made"), 1)

            sneg = stat[:, 132:164]
            lsum = stat[:, 164:196]
            linv = stat[:, 196:228]

            def attend(n):
                j, m = divmod(n, 4)
                dve.wait_ge(S("s_filled"), n + 1)
                if n >= 3:
                    dve.wait_ge(S("pt_filled"), n - 2)
                tt(out=sc[n % 3], in0=sbank[n % 3][:, :], in1=bias[:, KIND[j], 512 * m:512 * m + 512], op=ALU.add)\
                    .then_inc(S("s_made"), 1)
                dve.wait_ge(S("s_made"), n + 1)
                dve.tensor_reduce(out=sneg[:, 2 * n:2 * n + 2], in_=sc[n % 3].rearrange("p (h k) -> p h k", h=2),
                                  axis=AX.X, op=ALU.max, negate=True).then_inc(S("neg_made"), 1)

            def weigh(j):
                dve.wait_ge(S("p_made"), 8 * (j + 1))
                own(dve.reciprocal(linv[:, 8 * j:8 * j + 8], lsum[:, 8 * j:8 * j + 8]))
                own.wait()
                dve.wait_ge(S("pv_filled"), 4 * (j + 1))
                tt(out=ona[:, j, :].rearrange("p (h d) -> p h d", d=HD),
                   in0=bank[2 + j % 2][:, :].rearrange("p (h d) -> p h d", d=HD),
                   in1=linv[:, 8 * j:8 * j + 8].unsqueeze(2).to_broadcast([P, NH, HD]), op=ALU.mult)\
                    .then_inc(S("o_made"), 1)

            dve.wait_ge(S("bias_made"), 3 * NH)
            dve.wait_ge(S("four_filled"), nth("four_filled", NT))
            def norm_channels(q):
                dve.wait_ge(S("hsd_made"), nth("hsd_made", q + 1))
                own(dve.reciprocal(hyt[:, q, :], filt[:, 2 + q, :]))
                own.wait()
                for m in range(2):
                    src = hyu[:, m, :] if q == 0 else pooled[:, m, :]
                    at = m if q == 0 else 6 + m
                    stt(out=mixT[:, at, :], in0=src, scalar=col("mixg", at), in1=hyt[:, q, :],
                        op0=ALU.mult, op1=ALU.mult).then_inc(S("mix_made"), 1)

            for n in range(16):
                attend(n)
                if n % 4 == 1 and n > 4:
                    weigh(n // 4 - 1)
                if n in (6, 12):
                    q = n // 12
                    dve.wait_ge(S("hsum_filled"), nth("hsum_filled", q + 1))
                    ts(filt[:, 2 + q, :], bank[5][:, :], 1.0 / 256, EPS, ALU.mult, ALU.add).then_inc(S("hvar_made"), 1)
                if n in (9, 15):
                    norm_channels(n // 15)
            weigh(3)
            nss = stat[:, 228:232]
            nrs = stat[:, 232:236]
            dve.wait_ge(S("nsq_made"), nth("nsq_made", NT))
            own(ts(nss, nss, 1.0 / NAW, EPS, ALU.mult, ALU.add))
            own.wait()
            dve.engine_nop().then_inc(S("nvar_made"), 1)
            dve.wait_ge(S("nsd_made"), nth("nsd_made", 1))
            own(dve.reciprocal(nrs, nss))
            own.wait()
            for j in range(NT):
                ts(ona[:, j, :], ona[:, j, :], nrs[:, j:j + 1], None, ALU.mult).then_inc(S("on_made"), 1)
            dve.wait_ge(S("x_in"), 16)
            for c in range(N_OUT1 // 2):
                for i in range(NT):
                    u = 4 * c + i
                    dve.wait_ge(S("out1_filled"), u + 1)
                    xs = x_res[:, i, 512 * c:512 * c + 512]
                    tt(out=xs, in0=xs, in1=bank[i][:, :], op=ALU.add).then_inc(S("out1_added"), 1)
            v2 = stat[:, 236:240]
            r2 = stat[:, 240:244]
            dve.wait_ge(S("n2sq_made"), nth("n2sq_made", NT))
            ts(v2, v2, 1.0 / D, EPS, ALU.mult, ALU.add).then_inc(S("n2var_made"), 1)
            dve.wait_ge(S("n2sd_made"), nth("n2sd_made", 1))
            own(dve.reciprocal(r2, v2))
            own.wait()
            for k in range(1, KD, 2):
                dve.wait_ge(S("h2_turned"), nth("h2_turned", k + 1))
                ts(hT[:, k, :], bank[5][:, :], col("norm2", k), None, ALU.mult).then_inc(S("h2t_v"), 1)
            dve.wait_ge(S("g2_in"), 16)
            for i in range(NT):
                stt(out=h2[:, i, :], in0=x_res[:, i, :], scalar=r2[:, i:i + 1], in1=grow, op0=ALU.mult, op1=ALU.mult)\
                    .then_inc(S("h2_made"), 1)
            rmx = stat[:, 244:248]
            dve.wait_ge(S("lg_filled"), nth("lg_filled", 1))
            l3 = bank[6][:, 0:NT * NE].rearrange("p (i e) -> p i e", e=NE)
            own(tt(out=lg, in0=l3, in1=r2.unsqueeze(2).to_broadcast([P, NT, NE]), op=ALU.mult))
            own.wait()
            own(dve.tensor_reduce(out=rmx, in_=lg, axis=AX.X, op=ALU.max))
            own.wait()
            tt(out=lg, in0=lg, in1=rmx.unsqueeze(2).to_broadcast([P, NT, NE]), op=ALU.subtract).then_inc(S("lg_made"), 1)
            dve.wait_ge(S("lg_exp"), nth("lg_exp", 1))
            own(dve.tensor_reduce(out=rmx, in_=lg, axis=AX.X, op=ALU.add))
            own.wait()
            own(dve.reciprocal(rmx, rmx))
            own.wait()
            tt(out=aff, in0=lg, in1=rmx.unsqueeze(2).to_broadcast([P, NT, NE]), op=ALU.mult).then_inc(S("aff_made"), 1)
            dve.wait_ge(S("aff_turned"), nth("aff_turned", 1))
            w16 = work[0:NE, :]
            top = stat[0:NE, 248:256]
            own(dve.tensor_copy(w16, bank[7][0:NE, :]))
            own.wait()
            for _ in range(CAP // 8):
                own(dve.max(out=top, in_=w16))
                own.wait()
                own(dve.match_replace(out=w16, in_to_replace=top, in_values=w16, imm_value=-1.0))
                own.wait()
            own(ts(sel[0:NE, :], w16, 0.0, None, ALU.is_lt))
            own.wait()
            own(dve.tensor_tensor_scan(out=rank[0:NE, :], data0=sel[0:NE, :], data1=sel[0:NE, :], initial=0.0,
                                       op0=ALU.add, op1=ALU.bypass))
            own.wait()
            own(tt(out=rank[0:NE, :], in0=rank[0:NE, :], in1=sel[0:NE, :], op=ALU.mult))
            own.wait()
            ts(rank[0:NE, :], rank[0:NE, :], -1.0, None, ALU.add).then_inc(S("rank_made"), 1)
            dve.wait_ge(S("rank_turned"), nth("rank_turned", 1))
            own(dve.tensor_copy(rankc, l3))
            own.wait()
            dve.wait_ge(S("wr_in"), 32)
            for es in (slice(0, 2), slice(2, NE)):
                for i in range(NT):
                    n = es.stop - es.start
                    tt(out=onehot[:, i, :].rearrange("p (e s) -> p e s", s=CAP)[:, es],
                       in0=iota.unsqueeze(1).to_broadcast([P, n, CAP]),
                       in1=rankc[:, i, es].unsqueeze(2).to_broadcast([P, n, CAP]), op=ALU.is_equal)\
                        .then_inc(S("onehot_made"), 1)
            dve.sem_inc(S("h_made"), 2)
            dve.sem_inc(S("sc_added"), 2)

            def hidden(e, c):
                dve.wait_ge(S("silu_made"), e * NFC + (c + 1))
                dve.wait_ge(S("hid_turned"), e * NFC + (c + 1))
                tt(out=hid[c % 2], in0=silu[c % 2], in1=bank[c % 2][:, 256:512], op=ALU.mult).then_inc(S("h_made"), 1)

            def add_scattered(e, us):
                for u in us:
                    i, n = u // 2, u % 2
                    dve.wait_ge(S("sc_filled"), e * 8 + (u - 7))
                    xs = x_res[:, i, 512 * n:512 * n + 512]
                    tt(out=xs, in0=xs, in1=bank[6 + u % 2][:, :], op=ALU.add).then_inc(S("sc_added"), 1)

            def expert(e, first=False):
                hidden(e, 0)
                hidden(e, 1)
                if not first:
                    add_scattered(e, range(8))
                hidden(e, 2)
                hidden(e, 3)
                dve.wait_ge(S("y_part"), e * NFC + NFC)
                dve.tensor_copy(ysb[:, 512:1024], bank[5][:, :]).then_inc(S("y_copied"), 1)

            expert(0, first=True)
            with dve.Fori(1, NE) as e:
                expert(e)
            add_scattered(NE, range(8))
            second_dve(dve, own)

        @block.scalar
        def _(act):
            own = Own(act, "act_own")
            fn = act.activation
            act.wait_ge(S("var1_made"), nth("var1_made", 1))
            fn(hyt[:, 0, :], hyt[:, 0, :], ACT.Sqrt).then_inc(S("sd1_made"), 1)
            act.wait_ge(S("fnet_in"), 16 * 5)
            act.wait_ge(S("cols_in"), 32)
            for i in (3, 2, 1, 0):
                fn(decay[:, i, :], decay[:, 0, :], ACT.Exp, scale=col("negt", i)).then_inc(S("decay_made"), 1)
            act.wait_ge(S("angle_made"), 1)
            fn(fh, fa, ACT.Sin).then_inc(S("fh_made"), 1)

            def proj_out(u):
                act.wait_ge(S("proj_filled"), u + 1)
                if u < 16:
                    ps = bank[2 + u % 4][:, :]
                grid = ps.rearrange("p (r c) -> p r c", c=GW) if u < 16 else None
                if u < 6:
                    last = fn(hyu[:, u, :], ps, ACT.Identity, bias=col("hb", u), scale=col("hw1", u))
                elif u < 10:
                    m = u - 6
                    if m == 0:
                        act.wait_ge(S("qz_zero"), 1)
                    for hh in range(2):
                        q = slice(64 * hh, 64 * hh + 64)
                        last = fn(qz[q, 2 * m + hh, :].rearrange("p (c r) -> p r c", r=ROWS), grid[q], ACT.Copy,
                                  scale=HD ** -0.5)
                        if hh == 0:
                            own(last)
                elif u < 14:
                    last = fn(kT[:, u - 10, :].rearrange("p (c r) -> p r c", r=ROWS), grid, ACT.Copy)
                elif u < 16:
                    act.wait_ge(S("filt_made"), nth("filt_made", NT))
                    last = fn(pu[:, u - 14, 16:16 + L], ps, ACT.Copy)
                else:
                    last = fn(va[:, u - 16, :], bank[2 + u - 16][:, :], ACT.Copy)
                last.then_inc(S("proj_copied"), 1)

            for u in range(6):
                proj_out(u)
            act.wait_ge(S("angle_made"), 2)
            act.wait_ge(S("net2_filled"), nth("net2_filled", 1))
            fn(fh, fa, ACT.Sin).then_inc(S("fh_made"), 1)
            for u in range(6, 10):
                proj_out(u)
            for i in range(NT):
                act.wait_ge(S("z_turned"), nth("z_turned", i + 1))
                fn(zqp[:, i, 256:512], bank[i % 2][:, 0:256], ACT.Copy).then_inc(S("z_copied"), 1)
            for u in range(10, 20):
                proj_out(u)
            for f in range(NT):
                b = (6, 0)[f % 2]
                act.wait_ge(S("four_filled"), nth("four_filled", f + 1))
                act.wait_ge(S("ywf_made"), f)
                fn(rs[:, 0:256], bank[b][:, 0:256], ACT.Copy, scale=col("wk", f)).then_inc(S("rs_made"), 1)
                fn(rs[:, 256:512], bank[b + 1][:, 256:512], ACT.Copy, scale=col("wk", f)).then_inc(S("rs_made"), 1)
            act.wait_ge(S("pmix_filled"), nth("pmix_filled", 2))
            for m in range(2):
                fn(pooled[:, m, :], bank[2 + m][:, :], ACT.Copy, scale=col("pscale", m)).then_inc(S("pmix_copied"), 1)
            act.wait_ge(S("yhy_filled"), nth("yhy_filled", 2))
            act.wait_ge(S("pmix_copied"), nth("pmix_copied", 2))
            for m in range(2):
                fn(ywf[:, m, :], pooled[:, m, :], ACT.Square).then_inc(S("psq_made"), 1)
            lsum = stat[:, 164:196]
            sneg = stat[:, 132:164]

            def exps(n):
                act.wait_ge(S("neg_made"), n + 1)
                for hh in range(2):
                    at = 2 * n + hh
                    s = sc[n % 3][:, NKEY * hh:NKEY * hh + NKEY]
                    fn(s, s, ACT.Exp, bias=sneg[:, at:at + 1], accum_out=lsum[:, at:at + 1]).then_inc(S("p_made"), 1)

            exps(0)
            exps(1)
            for n in range(16):
                if n < 14:
                    exps(n + 2)
                act.wait_ge(S("pt_filled"), n + 1)
                if n >= 3:
                    act.wait_ge(S("pv_filled"), n - 2)
                fn(pt[n % 3], bank[n % 2][:, :], ACT.Copy).then_inc(S("pt_copied"), 1)
                if n in (7, 13):
                    q = n // 13
                    act.wait_ge(S("hvar_made"), nth("hvar_made", q + 1))
                    fn(filt[:, 2 + q, :], filt[:, 2 + q, :], ACT.Sqrt).then_inc(S("hsd_made"), 1)
            nss = stat[:, 228:232]
            for j in range(NT):
                act.wait_ge(S("o_made"), j + 1)
                if j:
                    act.wait_ge(S("nsq_made"), nth("nsq_made", j))
                fn(filt[:, 0, :], ona[:, j, :], ACT.Square, accum_out=nss[:, j:j + 1]).then_inc(S("nsq_made"), 1)
            act.wait_ge(S("nvar_made"), nth("nvar_made", 1))
            fn(nss, nss, ACT.Sqrt).then_inc(S("nsd_made"), 1)
            for m in range(4):
                act.wait_ge(S("ot_filled"), nth("ot_filled", m + 1))
                fn(mixT[:, 2 + m, :].rearrange("p (r c) -> p c r", c=GW),
                   bank[6 + m % 2][:, :].rearrange("p (c r) -> p c r", r=ROWS), ACT.Copy, scale=col("mixg", 2 + m))\
                    .then_inc(S("ot_copied"), 1)
            v2 = stat[:, 236:240]
            for i in range(NT):
                act.wait_ge(S("out1_added"), 5 + i)
                if i:
                    act.wait_ge(S("n2sq_made"), nth("n2sq_made", i))
                fn(sqd, x_res[:, i, :], ACT.Square, accum_out=v2[:, i:i + 1]).then_inc(S("n2sq_made"), 1)
            act.wait_ge(S("n2var_made"), nth("n2var_made", 1))
            fn(v2, v2, ACT.Sqrt).then_inc(S("n2sd_made"), 1)
            for k in range(0, KD, 2):
                act.wait_ge(S("h2_turned"), nth("h2_turned", k + 1))
                fn(hT[:, k, :], bank[4][:, :], ACT.Copy, scale=col("norm2", k)).then_inc(S("h2t_a"), 1)
            act.wait_ge(S("lg_made"), nth("lg_made", 1))
            fn(lg, lg, ACT.Exp).then_inc(S("lg_exp"), 1)

            def tokens(e):
                act.wait_ge(S("xs_filled"), e + 1)
                fn(xsT.rearrange("p k s -> p (k s)"), bank[3][:, :], ACT.Copy).then_inc(S("xs_made"), 1)

            def expert(e, final=False):
                def silu_of(c):
                    act.wait_ge(S("ab_filled"), e * NFC + (c + 1))
                    act.wait_ge(S("h_made"), e * NFC + (c + 1))
                    fn(silu[c % 2], bank[c % 2][:, 0:256], ACT.Silu).then_inc(S("silu_made"), 1)

                def turned(c):
                    act.wait_ge(S("hid_turned"), e * NFC + (c + 3))
                    fn(hidT[c % 2], bank[2][:, 256 * (c % 2):256 * (c % 2) + 256], ACT.Copy).then_inc(S("hidT_made"), 1)

                silu_of(0)
                silu_of(1)
                turned(0)
                turned(1)
                silu_of(2)
                turned(2)
                silu_of(3)
                turned(3)
                act.wait_ge(S("gt_filled"), e + 1)
                fn(gt, bank[6][:, :], ACT.Copy).then_inc(S("gt_made"), 1)
                if not final:
                    tokens(e + 1)
                act.wait_ge(S("y_part"), e * NFC + NFC)
                fn(ysb[:, 0:512], bank[4][:, :], ACT.Copy).then_inc(S("y_copied"), 1)

            tokens(0)
            with act.Fori(0, NE - 1) as e:
                expert(e)
            expert(NE - 1, final=True)
            second_act(act, own)


def tables():
    f = np.float32
    k = np.arange(L)
    ang = 2 * np.pi * ((k[:, None] * k[None, :]) % (2 * L)) / (2 * L)
    cosm, sinm = np.cos(ang).astype(f), np.sin(ang).astype(f)
    sinm[:, 0] = (-1.0) ** k
    consts = np.concatenate([np.eye(P), np.ones((P, P)), np.triu(np.ones((P, P))), np.triu(np.ones((P, P)), 1)], 1)
    inv = np.zeros((P, 2, L), f)
    for g, w in enumerate((2, 4, 8, 16)):
        cnt = np.clip(k + w // 2, 0, L) - np.clip(k - w // 2, 0, L)
        inv[64 * (g % 2):64 * (g % 2) + 64, g // 2] = (1.0 / cnt).astype(f)
    mask = np.zeros((P, 3, KC), f)
    for a, j in ((0, 0), (1, 1), (2, 3)):
        c = QC * j + np.arange(QC)
        start = np.clip(c - KWIN // 2, 0, GW - KWIN)
        key = KSTART[j] + np.arange(KC)
        ok = (key[None] >= start[:, None]) & (key[None] < start[:, None] + KWIN)
        mask[:, a] = np.repeat(np.where(ok, 0.0, -1e30), ROWS, axis=0)
    t = np.linspace(0.0, 1.0, L, dtype=f)[:, None]
    a = (2.0 * np.pi * np.arange(L, dtype=f)[:, None] / L).astype(f)
    fr = np.linspace(1e-4, 15, 16, dtype=f)[None]
    pos = np.zeros((P, L), f)
    pos[:33] = np.concatenate([t, np.cos(fr * a), -np.sin(fr * a)], -1).T
    deltas = np.abs(np.linspace(np.log(1e-2) / 0.3, np.log(1e-2) / 1.5, HY, dtype=f))
    wk = np.full(L, 2.0 / (2 * L), f)
    wk[0] = 1.0 / (2 * L)
    b = np.arange(P)
    blk = np.zeros((P, 7, P), f)
    for lv in range(7):
        w = 2 << lv
        blk[:, lv] = (b[:, None] // w == b[None] // w) & (b[:, None] % w < w // 2) & (b[None] % w >= w // 2)
    return dict(blk=blk, cosm=cosm, sinm=sinm, consts=consts.astype(f), invc=inv.reshape(P, 2 * L), mask=mask, pos=pos,
                deltas=deltas, wk=wk, negt=-t[:, 0], iota=np.arange(CAP, dtype=f))


def lay_out(a):
    f = np.float32
    c = tables()
    a = {k: np.asarray(v) for k, v in a.items()}

    def chunks(w, n):
        kk, nn = w.shape
        r = w.reshape(kk // P, P, nn // n, n).transpose(2, 1, 0, 3).reshape(nn // n, P, -1)
        return r

    w = a["w_in"][0]
    hy, q, k, v, pu = np.split(w, [768, 1280, 1792, 2304], axis=1)
    parts = [chunks(np.concatenate([hy, q, k, pu, v], 1), 256), chunks(a["w_out"][0], 256)]
    w2 = a["w_in_2"][0]
    at = np.cumsum([0, 512, 512, 512, 512, 4, 4, 256, 256, 512, 512, 4, 4, 1024, 1024])
    (gq, gk, gv, gz, gb, ga, mq, mk, mv, mo, mi, mf, sa, sb) = [w2[:, at[i]:at[i + 1]] for i in range(14)]
    parts.append(chunks(np.concatenate([gq, gk, gv, gz, mv, mo, mq, mk], 1), 256))
    parts += [chunks(sa, 256), chunks(sb, 256), chunks(a["w_branch_a_2"][0], 512), chunks(a["w_branch_b_2"][0], 512)]
    parts.append(chunks(a["w_out_2"][0], 256))
    up = np.stack([chunks(a["w1_2"][0], 256), chunks(a["w3_2"][0], 256)], 1)
    parts.append(up.reshape(-1, P, WCH))
    down = np.pad(a["w2_2"][0], ((0, 2 * P), (0, 0)))
    for n in range(2):
        d = down[:, 512 * n:512 * n + 512].reshape(6, 4, P, 512).transpose(0, 2, 1, 3).reshape(6, P, WCH)
        parts.append(d)
    parts.append(chunks(a["w_ple_2"][0], 1024))
    parts.append(chunks(a["w_ple_gate_2"][0], 256))
    wpack = np.concatenate(parts)
    assert wpack.shape == (N_CHUNKS, P, WCH), wpack.shape

    cols = np.zeros((P, N_COLS), f)

    def put(name, v):
        v = np.asarray(v).reshape(-1)
        if v.size < P:
            v = np.pad(v, (0, P - v.size))
        n = v.size // P
        cols[:, COLS[name]:COLS[name] + n] = v.reshape(n, P).T

    put("norm1", a["norm1_g"])
    for i in range(3):
        put(f"hw{i}", a["hy_short_w"][0, i])
    put("hb", a["hy_short_b"])
    put("skip", a["hy_skip"])
    put("pscale", a["pool_scale"])
    put("mixg", a["mix_norm_g"])
    put("gmix2", a["g_mix_2"])
    for i in range(4):
        put(f"cw{i}", a["conv_w_2"][0, i])
    put("gffn", a["g_ffn_2"])
    put("norm2", a["norm2_g"])
    put("gple", a["g_ple_2"])
    put("fb1", a["hy_f_b1"])
    put("fb2", a["hy_f_b2"])
    put("freq", a["hy_f_freq"])
    put("wk", c["wk"])
    put("negt", c["negt"])
    put("alt2", 2.0 * (-1.0) ** np.arange(P))
    rows = np.concatenate([a["gdn_norm_2"][0], a["ml_norm_2"][0].reshape(-1), a["a_log_2"][0], a["dt_bias_2"][0],
                           a["ml_i_bias_2"][0], a["ml_f_bias_2"][0]])
    pw = np.zeros((2, P, P), f)
    for g in range(4):
        s = slice(64 * (g % 2), 64 * (g % 2) + 64)
        pw[g // 2, s, s] = a["pool_w"][0, g]
    pad2 = lambda v, r, q: np.pad(v, ((0, r - v.shape[0]), (0, q - v.shape[1])))
    pad = np.pad(a["na_rpb"][0], ((0, 0), (0, 0), (16, 17)))
    d = dict(
        x=a["x"][0], xT=a["x"][0].T, wpack=wpack, cols=cols, rows=rows, pwbd=pw,
        w_gate=a["w_gate"][0], w_up=a["w_up"][0], w_down=a["w_down"][0], w_router=a["w_router"][0],
        w_gates=np.concatenate([gb, ga, mi, mf], 1), pT=a["p_2"][0, 0].T,
        g2=a["norm2_g"][0], gfin=a["g_final_2"],
        fw1=pad2(a["hy_f_w1"][0], P, P), fw2=pad2(a["hy_f_w2"][0], P, P), fwo=pad2(a["hy_f_wout"][0], P, 512),
        rpbw=np.stack([pad[:, ROWS - 1 - r:2 * ROWS - 1 - r].reshape(NH * ROWS, 64) for r in range(ROWS)]),
        gfirst=a["final_g"],
    )
    for n in ("cosm", "sinm", "consts", "invc", "mask", "pos", "deltas", "iota", "blk"):
        d[n] = c[n]
    return {k: np.ascontiguousarray(v) for k, v in d.items()}


def kernel(**inputs):
    import concourse.bacc as bacc
    from concourse.bass_utils import run_bass_kernel_spmd

    nc = bacc.Bacc("TRN2", target_bir_lowering=False, num_devices=1)
    arrays, args = {}, {}
    for name, a in lay_out(inputs).items():
        arrays[f"in_{name}_dram"] = a
        args[name] = nc.dram_tensor(f"in_{name}_dram", a.shape, mybir.dt.from_np(a.dtype), kind="ExternalInput").ap()
    out = nc.dram_tensor("out_0_dram", (1, L, D), F32, kind="ExternalOutput").ap()
    program(nc, args, out)
    r = run_bass_kernel_spmd(nc, [arrays], core_ids=[0])
    return r.results[0]["out_0_dram"]
```
